# Optimizing a Trainium2 kernel written in Bass

```python
import functools
import jax
import jax.numpy as jnp
from jax import lax
import numpy as np

D_MODEL = 1024
BATCH = 1
SEQ = 512
DEPTH = 1

GRID_W = 64
CTX_LEN = 256
N_BRANCH = 4
BR_W = D_MODEL // 2
RWKV_HS = 64
RWKV_H = BR_W // RWKV_HS
RWKV_W_LORA = 64
RWKV_A_LORA = 64
RWKV_G_LORA = 128
RWKV_GN_EPS = 64e-5
L2_EPS = 1e-12
CONV_K = 31
LRU_BLOCKS = 8
LRU_BS = BR_W // LRU_BLOCKS
LRU_CONV = 4
LRU_C = 8.0
RET_H = 4
RET_DK = 64
RET_DV = BR_W // RET_H
RET_CHUNK = 128
ROPE_BASE = 10000.0
N_EXPERTS = 32
N_GROUPS = 4
EXPERTS_PER_GROUP = N_EXPERTS // N_GROUPS
TOP_K = 2
D_EXPERT = D_MODEL // 2
MOE_BLOCK = 128
RMS_EPS = 1e-6
LN_EPS = 1e-5
F32 = jnp.float32

RWKV_COLS = (('r', BR_W), ('k', BR_W), ('v', BR_W), ('wlo0', RWKV_W_LORA), ('wlo1', RWKV_W_LORA),
             ('alo0', RWKV_A_LORA), ('alo1', RWKV_A_LORA), ('glo', RWKV_G_LORA))
REST_COLS = (('conv_val', BR_W), ('conv_gate', BR_W), ('lru_x', BR_W), ('lru_gate', BR_W),
             ('ret_q', RET_H * RET_DK), ('ret_k', RET_H * RET_DK), ('ret_v', BR_W), ('ret_g', BR_W),
             ('merge', N_BRANCH * D_MODEL))
RWKV_WIDTH = 3 * BR_W + 2 * RWKV_W_LORA + 2 * RWKV_A_LORA + RWKV_G_LORA
IN_WIDTH = RWKV_WIDTH + 4 * BR_W + 2 * RET_H * RET_DK + 2 * BR_W + N_BRANCH * D_MODEL

kernel_name = 'hybrid_flow_backbone_block'

def _rmsnorm(x, g):
    xf = x.astype(F32)
    y = xf * lax.rsqrt(jnp.mean(xf * xf, axis=-1, keepdims=True) + RMS_EPS)
    return (y * g.astype(F32)).astype(x.dtype)

def _layernorm(x, g, b, eps):
    xf = x.astype(F32)
    xc = xf - jnp.mean(xf, axis=-1, keepdims=True)
    return xc * lax.rsqrt(jnp.mean(xc * xc, axis=-1, keepdims=True) + eps) * g.astype(F32) + b.astype(F32)

def _head_norm(y, g, b, eps):
    yf = y.astype(F32)
    yc = yf - jnp.mean(yf, axis=-1, keepdims=True)
    yn = yc * lax.rsqrt(jnp.mean(yc * yc, axis=-1, keepdims=True) + eps)
    return yn.reshape(*y.shape[:2], -1) * g.astype(F32) + b.astype(F32)

def _heads(z, n_heads, head_dim):
    return z.reshape(*z.shape[:2], n_heads, head_dim)

def _split(p, layout):
    out, off = {}, 0
    for name, width in layout:
        out[name] = p[..., off:off + width]
        off += width
    return out

def _shift_prev(z):
    return jnp.pad(z, ((0, 0), (1, 0), (0, 0)))[:, :-1]

def _shift_next(z):
    return jnp.pad(z, ((0, 0), (0, 1), (0, 0)))[:, 1:]

def _depthwise_conv(z, w, b, pad_lo, pad_hi):
    ch = z.shape[-1]
    y = lax.conv_general_dilated(z, w.astype(z.dtype)[:, None, :], (1,), [(pad_lo, pad_hi)],
                                 dimension_numbers=('NWC', 'WIO', 'NWC'), feature_group_count=ch)
    return y + b.astype(y.dtype)

def _modulate(h, shift, scale):
    return h * (1 + scale) + shift

def _project(h, lp):
    p = h @ lp['w_in']
    za = p[..., :RWKV_WIDTH]
    za = za + lp['rwkv_mu_prev'] * (_shift_prev(za) - za) + lp['rwkv_mu_next'] * (_shift_next(za) - za)
    return _split(za, RWKV_COLS), _split(p[..., RWKV_WIDTH:], REST_COLS)

def _two_way(scan_f, scan_b, ctx_f, ctx_b, lat_f, lat_b, s_zero, need_ctx):
    flip = lambda tup: tuple(jnp.flip(t, 1) for t in tup)
    yc_f, sc_f = scan_f(ctx_f, s_zero)
    yc_b, sc_b = scan_b(flip(ctx_b), s_zero)
    yl_f, _ = scan_f(lat_f, sc_f)
    yl_b, _ = scan_b(flip(lat_b), sc_b)
    y_lat = yl_f + jnp.flip(yl_b, 1)
    y_ctx = yc_f + jnp.flip(yc_b, 1) if need_ctx else None
    return y_ctx, y_lat

def _rwkv_scan_inputs(ca, lp):
    r = _heads(ca['r'].astype(F32), RWKV_H, RWKV_HS)
    k = ca['k'].astype(F32)
    v = _heads(ca['v'].astype(F32), RWKV_H, RWKV_HS)
    kk = _heads(k * lp['rwkv_k_k'], RWKV_H, RWKV_HS)
    kk = kk * lax.rsqrt(jnp.sum(kk * kk, axis=-1, keepdims=True) + L2_EPS)
    dirs = []
    for d in range(2):
        w_raw = lp['rwkv_w0'][d] + jnp.tanh(ca['wlo%d' % d].astype(F32)) @ lp['rwkv_w2'][d]
        decay = jnp.exp(-jnp.exp(-jax.nn.softplus(-w_raw) - 0.5))
        a = jax.nn.sigmoid(lp['rwkv_a0'][d] + ca['alo%d' % d].astype(F32) @ lp['rwkv_a2'][d])
        k_d = k * (1.0 + (a - 1.0) * lp['rwkv_k_a'])
        dirs.append((r, _heads(decay, RWKV_H, RWKV_HS), _heads(k_d, RWKV_H, RWKV_HS), v, kk,
                     _heads(a, RWKV_H, RWKV_HS)))
    return dirs

def _rwkv7_scan(inputs, s0):
    def step(S, xs):
        r_t, w_t, k_t, v_t, kk_t, a_t = xs
        sa = jnp.einsum('bhvk,bhk->bhv', S, kk_t)
        S = (S * w_t[:, :, None, :] - sa[..., None] * (kk_t * a_t)[:, :, None, :]
             + v_t[..., None] * k_t[:, :, None, :])
        return S, jnp.einsum('bhvk,bhk->bhv', S, r_t)
    s_fin, y = lax.scan(step, s0, tuple(jnp.swapaxes(t, 0, 1) for t in inputs))
    return jnp.swapaxes(y, 0, 1), s_fin

def _rwkv_out(y, ca, lp):
    r = _heads(ca['r'].astype(F32), RWKV_H, RWKV_HS)
    k = _heads(ca['k'].astype(F32), RWKV_H, RWKV_HS)
    v = _heads(ca['v'].astype(F32), RWKV_H, RWKV_HS)
    g = jax.nn.sigmoid(ca['glo'].astype(F32)) @ lp['rwkv_g2']
    bonus = jnp.sum(r * k * lp['rwkv_r_k'].reshape(RWKV_H, RWKV_HS), axis=-1, keepdims=True) * v
    yn = _head_norm(y, lp['rwkv_gn_g'], lp['rwkv_gn_b'], RWKV_GN_EPS) + bonus.reshape(*bonus.shape[:2], BR_W)
    return (yn * g) @ lp['rwkv_proj']

def _conformer_conv(cr, lp):
    u = cr['conv_val'] * jax.nn.sigmoid(cr['conv_gate'])
    u = _depthwise_conv(u, lp['conv_w'], lp['conv_b'], CONV_K // 2, CONV_K // 2)
    u = jax.nn.silu(_layernorm(u, lp['conv_ln_g'], lp['conv_ln_b'], LN_EPS))
    return u @ lp['conv_proj']

def _lru_scan_inputs(cr, lp):
    dirs = []
    for d in range(2):
        pad = (LRU_CONV - 1, 0) if d == 0 else (0, LRU_CONV - 1)
        xc = _depthwise_conv(cr['lru_x'], lp['lru_conv_w'][d], lp['lru_conv_b'][d], *pad).astype(F32)
        xb = _heads(xc, LRU_BLOCKS, LRU_BS)
        gate_r = jax.nn.sigmoid(jnp.einsum('btgi,gij->btgj', xb, lp['lru_wr'][d].astype(F32)).reshape(xc.shape)
                                + lp['lru_br'][d])
        gate_i = jax.nn.sigmoid(jnp.einsum('btgi,gij->btgj', xb, lp['lru_wi'][d].astype(F32)).reshape(xc.shape)
                                + lp['lru_bi'][d])
        log_a = -LRU_C * gate_r * jax.nn.softplus(-lp['lru_lambda'][d].astype(F32))
        dirs.append((jnp.exp(log_a), jnp.sqrt(-jnp.expm1(2.0 * log_a)) * (gate_i * xc)))
    return dirs

def _linear_scan(inputs, h0):
    a, b = inputs
    def combine(lhs, rhs):
        return lhs[0] * rhs[0], rhs[0] * lhs[1] + rhs[1]
    a_cum, h = lax.associative_scan(combine, (a, b), axis=1)
    h = h + a_cum * h0[:, None, :]
    return h, h[:, -1]

def _lru_out(h, cr, lp):
    return (h * jax.nn.gelu(cr['lru_gate'].astype(F32))) @ lp['lru_proj']

def _rotary_2d(z, rows, cols):
    n_freq = RET_DK // 4
    inv = ROPE_BASE ** (-jnp.arange(n_freq, dtype=F32) / n_freq)
    ang = jnp.concatenate([rows[:, None] * inv, cols[:, None] * inv], axis=-1)[None, :, None, :]
    cos, sin = jnp.cos(ang), jnp.sin(ang)
    z1, z2 = z[..., :RET_DK // 2], z[..., RET_DK // 2:]
    return jnp.concatenate([z1 * cos - z2 * sin, z1 * sin + z2 * cos], axis=-1)

def _ret_scan_inputs(cr, rows, cols):
    q = _heads(cr['ret_q'].astype(F32), RET_H, RET_DK)
    k = _heads(cr['ret_k'].astype(F32), RET_H, RET_DK) * (RET_DK ** -0.5)
    v = _heads(cr['ret_v'].astype(F32), RET_H, RET_DV)
    if rows is not None:
        q, k = _rotary_2d(q, rows, cols), _rotary_2d(k, rows, cols)
    return (q, k, v)

def _retention_chunkwise(inputs, s0, include_diag):
    q, k, v = inputs
    bsz, n_tok = q.shape[:2]
    n_chunk = n_tok // RET_CHUNK
    log_g = jnp.log1p(-jnp.exp2(-5.0 - jnp.arange(RET_H, dtype=F32)))
    idx = jnp.arange(RET_CHUNK, dtype=F32)
    diff = idx[:, None] - idx[None, :]
    keep = diff >= 0 if include_diag else diff > 0
    dmat = jnp.where(keep[None], jnp.exp(log_g[:, None, None] * jnp.maximum(diff, 0.0)[None]), 0.0)
    xi = jnp.exp(log_g[None, :] * (idx[:, None] + 1.0))
    zeta = jnp.exp(log_g[None, :] * (RET_CHUNK - 1.0 - idx)[:, None])
    g_chunk = jnp.exp(log_g * RET_CHUNK)
    chunks = lambda t: jnp.moveaxis(t.reshape(bsz, n_chunk, RET_CHUNK, *t.shape[2:]), 1, 0)

    def step(S, xs):
        qc, kc, vc = xs
        att = jnp.einsum('bihd,bjhd->bhij', qc, kc) * dmat
        o = (jnp.einsum('bhij,bjhv->bihv', att, vc)
             + jnp.einsum('bihd,bhdv->bihv', qc, S) * xi[None, :, :, None])
        S = S * g_chunk[None, :, None, None] + jnp.einsum('bjhd,bjhv->bhdv', kc * zeta[None, :, :, None], vc)
        return S, o
    s_fin, o = lax.scan(step, s0, (chunks(q), chunks(k), chunks(v)))
    return jnp.moveaxis(o, 0, 1).reshape(bsz, n_tok, RET_H, RET_DV), s_fin

def _ret_out(o, cr, lp):
    yn = _head_norm(o, lp['ret_gn_g'], lp['ret_gn_b'], LN_EPS)
    return (jax.nn.silu(cr['ret_g'].astype(F32)) * yn) @ lp['ret_proj']

def _merge(cr, branches, lp):
    gates = jax.nn.sigmoid(cr['merge'].astype(F32) + lp['b_merge'])
    gates = gates.reshape(*gates.shape[:2], N_BRANCH, D_MODEL)
    mixed = sum(gates[:, :, i] * br for i, br in enumerate(branches))
    return mixed @ lp['w_out']

def _mixer(hc, hl, lp, rows, cols, need_ctx):
    bsz = hl.shape[0]
    ca_c, cr_c = _project(hc, lp)
    ca_l, cr_l = _project(hl, lp)
    rc, rl = _rwkv_scan_inputs(ca_c, lp), _rwkv_scan_inputs(ca_l, lp)
    ya_c, ya_l = _two_way(_rwkv7_scan, _rwkv7_scan, rc[0], rc[1], rl[0], rl[1],
                          jnp.zeros((bsz, RWKV_H, RWKV_HS, RWKV_HS), F32), need_ctx)
    lc, ll = _lru_scan_inputs(cr_c, lp), _lru_scan_inputs(cr_l, lp)
    yl_c, yl_l = _two_way(_linear_scan, _linear_scan, lc[0], lc[1], ll[0], ll[1],
                          jnp.zeros((bsz, BR_W), F32), need_ctx)
    ret_f = functools.partial(_retention_chunkwise, include_diag=True)
    ret_b = functools.partial(_retention_chunkwise, include_diag=False)
    qc = _ret_scan_inputs(cr_c, None, None)
    ql = _ret_scan_inputs(cr_l, rows, cols)
    yr_c, yr_l = _two_way(ret_f, ret_b, qc, qc, ql, ql,
                          jnp.zeros((bsz, RET_H, RET_DK, RET_DV), F32), need_ctx)
    out_l = _merge(cr_l, [_rwkv_out(ya_l, ca_l, lp), _conformer_conv(cr_l, lp),
                          _lru_out(yl_l, cr_l, lp), _ret_out(yr_l, cr_l, lp)], lp)
    out_c = None
    if need_ctx:
        out_c = _merge(cr_c, [_rwkv_out(ya_c, ca_c, lp), _conformer_conv(cr_c, lp),
                              _lru_out(yl_c, cr_c, lp), _ret_out(yr_c, cr_c, lp)], lp)
    return out_c, out_l

def _grouped_experts(tokens, e_idx, wts, w1, w3, w2):
    n_tok = tokens.shape[0]
    n_asg = n_tok * TOP_K
    flat_e = e_idx.reshape(-1)
    flat_t = jnp.repeat(jnp.arange(n_tok, dtype=jnp.int32), TOP_K)
    order = jnp.argsort(flat_e)
    se, st, sw = flat_e[order], flat_t[order], wts.reshape(-1)[order]
    counts = jnp.bincount(flat_e, length=N_EXPERTS)
    starts = jnp.cumsum(counts) - counts
    padded = (counts + MOE_BLOCK - 1) // MOE_BLOCK * MOE_BLOCK
    pad_end = jnp.cumsum(padded)
    pad_start = pad_end - padded
    dest = pad_start[se] + jnp.arange(n_asg, dtype=jnp.int32) - starts[se]
    n_blocks = -(-n_asg // MOE_BLOCK) + N_EXPERTS
    slot_tok = jnp.full((n_blocks * MOE_BLOCK,), n_tok, jnp.int32).at[dest].set(st)
    block_e = jnp.minimum(jnp.searchsorted(pad_end, jnp.arange(n_blocks) * MOE_BLOCK, side='right'),
                          N_EXPERTS - 1)
    x_pad = jnp.concatenate([tokens, jnp.zeros((1, tokens.shape[1]), tokens.dtype)], axis=0)
    xb = x_pad[slot_tok].reshape(n_blocks, MOE_BLOCK, -1)

    def expert_block(args):
        xblk, e = args
        return (jax.nn.silu(xblk @ w1[e]) * (xblk @ w3[e])) @ w2[e]
    yb = lax.map(expert_block, (xb, block_e)).reshape(n_blocks * MOE_BLOCK, -1)
    return jax.ops.segment_sum(yb[dest] * sw[:, None], st, num_segments=n_tok)

def _moe(tokens, w_router, b_router, w1, w3, w2):
    aff = jax.nn.sigmoid(tokens.astype(F32) @ w_router.astype(F32))
    sel = (aff + b_router.astype(F32)).reshape(-1, N_GROUPS, EXPERTS_PER_GROUP)
    grp_score = jnp.sum(lax.top_k(sel, TOP_K)[0], axis=-1)
    grp = jnp.argmax(grp_score, axis=-1)
    grp_mask = jnp.arange(N_GROUPS)[None, :] == grp[:, None]
    masked = jnp.where(grp_mask[:, :, None], sel, -jnp.inf).reshape(-1, N_EXPERTS)
    _, e_idx = lax.top_k(masked, TOP_K)
    wts = jnp.take_along_axis(aff, e_idx, axis=1)
    wts = wts / jnp.sum(wts, axis=-1, keepdims=True)
    return _grouped_experts(tokens, e_idx, wts, w1, w3, w2)

def setup_inputs(seed: int = 0) -> dict:
    key = jax.random.key(seed)
    keys = jax.random.split(key, 80)
    count = [0]

    def nk():
        count[0] += 1
        return keys[count[0] - 1]

    def nrm(shape, scale):
        return scale * jax.random.normal(nk(), shape, F32)

    def uni(shape, lo, hi):
        return jax.random.uniform(nk(), shape, F32, lo, hi)

    L, D = DEPTH, D_MODEL
    s_lam = uni((L, 2, BR_W), 0.9, 0.999) ** (1.0 / LRU_C)
    return {
        'x': nrm((BATCH, SEQ, D), 1.0),
        'c': nrm((BATCH, D), 1.0),
        'ctx': nrm((BATCH, CTX_LEN, D), 1.0),
        'c_ctx': nrm((D,), 1.0),
        'w_ada': nrm((L, D, 6 * D), 0.5 * D ** -0.5),
        'b_ada': nrm((L, 6 * D), 0.01),
        'norm1_g': 1.0 + nrm((L, D), 0.05),
        'norm2_g': 1.0 + nrm((L, D), 0.05),
        'w_in': nrm((L, D, IN_WIDTH), D ** -0.5),
        'b_merge': nrm((L, N_BRANCH * D), 0.01),
        'rwkv_mu_prev': uni((L, RWKV_WIDTH), 0.0, 0.5),
        'rwkv_mu_next': uni((L, RWKV_WIDTH), 0.0, 0.5),
        'rwkv_w0': uni((L, 2, BR_W), -6.5, -1.5),
        'rwkv_w2': nrm((L, 2, RWKV_W_LORA, BR_W), 0.1 * RWKV_W_LORA ** -0.5),
        'rwkv_a0': nrm((L, 2, BR_W), 0.1),
        'rwkv_a2': nrm((L, 2, RWKV_A_LORA, BR_W), 0.1 * RWKV_A_LORA ** -0.5),
        'rwkv_g2': nrm((L, RWKV_G_LORA, BR_W), RWKV_G_LORA ** -0.5),
        'rwkv_k_k': 0.85 + nrm((L, BR_W), 0.05),
        'rwkv_k_a': 1.0 + nrm((L, BR_W), 0.05),
        'rwkv_r_k': nrm((L, BR_W), 0.1),
        'rwkv_gn_g': 1.0 + nrm((L, BR_W), 0.05),
        'rwkv_gn_b': nrm((L, BR_W), 0.01),
        'rwkv_proj': nrm((L, BR_W, D), BR_W ** -0.5),
        'conv_w': nrm((L, CONV_K, BR_W), CONV_K ** -0.5),
        'conv_b': nrm((L, BR_W), 0.01),
        'conv_ln_g': 1.0 + nrm((L, BR_W), 0.05),
        'conv_ln_b': nrm((L, BR_W), 0.01),
        'conv_proj': nrm((L, BR_W, D), BR_W ** -0.5),
        'lru_conv_w': nrm((L, 2, LRU_CONV, BR_W), LRU_CONV ** -0.5),
        'lru_conv_b': nrm((L, 2, BR_W), 0.01),
        'lru_wr': nrm((L, 2, LRU_BLOCKS, LRU_BS, LRU_BS), LRU_BS ** -0.5),
        'lru_br': nrm((L, 2, BR_W), 0.01),
        'lru_wi': nrm((L, 2, LRU_BLOCKS, LRU_BS, LRU_BS), LRU_BS ** -0.5),
        'lru_bi': nrm((L, 2, BR_W), 0.01),
        'lru_lambda': jnp.log(s_lam) - jnp.log1p(-s_lam),
        'lru_proj': nrm((L, BR_W, D), BR_W ** -0.5),
        'ret_gn_g': 1.0 + nrm((L, BR_W), 0.05),
        'ret_gn_b': nrm((L, BR_W), 0.01),
        'ret_proj': nrm((L, BR_W, D), BR_W ** -0.5),
        'w_out': nrm((L, D, D), D ** -0.5),
        'w_router': nrm((D, N_EXPERTS), D ** -0.5),
        'b_router': nrm((N_EXPERTS,), 0.01),
        'e_w1': nrm((L, N_EXPERTS, D, D_EXPERT), D ** -0.5),
        'e_w3': nrm((L, N_EXPERTS, D, D_EXPERT), D ** -0.5),
        'e_w2': nrm((L, N_EXPERTS, D_EXPERT, D), D_EXPERT ** -0.5),
        'final_g': 1.0 + nrm((D,), 0.05),
    }

def reference(x, c, ctx, c_ctx, w_ada, b_ada, norm1_g, norm2_g, w_in, b_merge,
              rwkv_mu_prev, rwkv_mu_next, rwkv_w0, rwkv_w2, rwkv_a0, rwkv_a2, rwkv_g2,
              rwkv_k_k, rwkv_k_a, rwkv_r_k, rwkv_gn_g, rwkv_gn_b, rwkv_proj,
              conv_w, conv_b, conv_ln_g, conv_ln_b, conv_proj,
              lru_conv_w, lru_conv_b, lru_wr, lru_br, lru_wi, lru_bi, lru_lambda, lru_proj,
              ret_gn_g, ret_gn_b, ret_proj, w_out, w_router, b_router, e_w1, e_w3, e_w2, final_g):
    n_tok = x.shape[1]
    n_rows = n_tok // GRID_W
    rows = jnp.repeat(jnp.arange(n_rows, dtype=F32), GRID_W)
    cols = jnp.tile(jnp.arange(GRID_W, dtype=F32), n_rows)
    per_layer = {
        'w_in': w_in, 'b_merge': b_merge,
        'rwkv_mu_prev': rwkv_mu_prev, 'rwkv_mu_next': rwkv_mu_next, 'rwkv_w0': rwkv_w0,
        'rwkv_w2': rwkv_w2, 'rwkv_a0': rwkv_a0, 'rwkv_a2': rwkv_a2, 'rwkv_g2': rwkv_g2,
        'rwkv_k_k': rwkv_k_k, 'rwkv_k_a': rwkv_k_a, 'rwkv_r_k': rwkv_r_k,
        'rwkv_gn_g': rwkv_gn_g, 'rwkv_gn_b': rwkv_gn_b, 'rwkv_proj': rwkv_proj,
        'conv_w': conv_w, 'conv_b': conv_b, 'conv_ln_g': conv_ln_g, 'conv_ln_b': conv_ln_b,
        'conv_proj': conv_proj,
        'lru_conv_w': lru_conv_w, 'lru_conv_b': lru_conv_b, 'lru_wr': lru_wr, 'lru_br': lru_br,
        'lru_wi': lru_wi, 'lru_bi': lru_bi, 'lru_lambda': lru_lambda, 'lru_proj': lru_proj,
        'ret_gn_g': ret_gn_g, 'ret_gn_b': ret_gn_b, 'ret_proj': ret_proj, 'w_out': w_out,
    }
    h_ctx = ctx
    for layer in range(DEPTH):
        lp = {name: arr[layer] for name, arr in per_layer.items()}
        need_ctx = layer < DEPTH - 1
        mod_l = jax.nn.silu(c) @ w_ada[layer] + b_ada[layer]
        mod_c = jax.nn.silu(c_ctx) @ w_ada[layer] + b_ada[layer]
        sh1, sc1, g1, sh2, sc2, g2 = jnp.split(mod_l[:, None, :], 6, axis=-1)
        csh1, csc1, cg1, csh2, csc2, cg2 = jnp.split(mod_c, 6, axis=-1)
        hl = _modulate(_rmsnorm(x, norm1_g[layer]), sh1, sc1)
        hc = _modulate(_rmsnorm(h_ctx, norm1_g[layer]), csh1, csc1)
        out_c, out_l = _mixer(hc, hl, lp, rows, cols, need_ctx)
        x = x + (g1 * out_l).astype(x.dtype)
        hl2 = _modulate(_rmsnorm(x, norm2_g[layer]), sh2, sc2)
        if need_ctx:
            h_ctx = h_ctx + (cg1 * out_c).astype(h_ctx.dtype)
            hc2 = _modulate(_rmsnorm(h_ctx, norm2_g[layer]), csh2, csc2)
            n_c = hc2.shape[0] * hc2.shape[1]
            y = _moe(jnp.concatenate([hc2.reshape(-1, D_MODEL), hl2.reshape(-1, D_MODEL)], axis=0),
                     w_router, b_router, e_w1[layer], e_w3[layer], e_w2[layer])
            h_ctx = h_ctx + (cg2 * y[:n_c].reshape(hc2.shape)).astype(h_ctx.dtype)
            y_lat = y[n_c:].reshape(hl2.shape)
        else:
            y_lat = _moe(hl2.reshape(-1, D_MODEL), w_router, b_router,
                         e_w1[layer], e_w3[layer], e_w2[layer]).reshape(hl2.shape)
        x = x + (g2 * y_lat).astype(x.dtype)
    return _rmsnorm(x, final_g)


_drawn_inputs = setup_inputs


def setup_inputs(seed=0):
    import zlib

    import numpy as np

    out = dict(_drawn_inputs(seed))
    spreads = {}
    factors = {'b_merge': 8.0,
     'rwkv_w2': 8.0,
     'rwkv_a0': 5.256,
     'rwkv_a2': 6.423,
     'rwkv_k_a': 3.091,
     'rwkv_gn_g': 10.953,
     'rwkv_gn_b': 38.749,
     'conv_b': 8.0,
     'conv_ln_g': 3.969,
     'conv_ln_b': 32.749,
     'lru_conv_b': 2.814,
     'lru_br': 40.51,
     'lru_bi': 28.768,
     'ret_gn_g': 5.199,
     'ret_gn_b': 26.957}
    for name, (base, spread) in spreads.items():
        noise = np.random.default_rng([zlib.crc32(name.encode()), seed]).standard_normal(out[name].shape)
        drawn = base * np.exp(spread * noise) if base else spread * noise
        out[name] = jnp.asarray(drawn.astype(out[name].dtype))
    for name, factor in factors.items():
        out[name] = (out[name] * factor).astype(out[name].dtype)
    return out
```

```python
from contextlib import ExitStack

import numpy as np

import concourse.bass as bass
from concourse import mybir

F32 = mybir.dt.float32
I32 = mybir.dt.int32
U32 = mybir.dt.uint32
ALU = mybir.AluOpType
ACT = mybir.ActivationFunctionType
AX = mybir.AxisListType.X

P = 128
D = 1024
KT = D // P
CTX, LAT = 256, 512
TOK = CTX + LAT
NCH = TOK // P
CCH, LCH = CTX // P, LAT // P
BW = 512
BT = BW // P
HS = 64
GH = 4
HALF = GH * HS
HT = HALF // P
NE, NG, TOPK = 32, 4, 2
EPG = NE // NG
DE = 512
NBLK = LAT * TOPK // P + NE
CONV_K = 31
LOGW = -float(np.exp(-0.5))
GW = 256
RSLOT = 4
SLOTW = KT * GW

C_R, C_K, C_V, C_LORA = 0, 512, 1024, 1536
C_CVAL, C_CGATE, C_LX, C_LG = 1920, 2432, 2944, 3456
C_Q, C_RV, C_RG, C_MERGE = 3968, 4480, 4992, 5504


class Chain:

    def __init__(self, eng, sem):
        self.eng, self.sem, self.base, self.k = eng, sem, 0, 0

    def __call__(self, ins):
        self.k += 1
        ins.then_inc(self.sem, 1)
        self.eng.wait_ge(self.sem, self.base + self.k)

    def step(self, ins):
        self.k += 1
        ins.then_inc(self.sem, 1)

    def wait(self):
        self.eng.wait_ge(self.sem, self.base + self.k)

    def start(self, base):
        self.base, self.k = base, 0


class Arena:

    def __init__(self, sb, at, end):
        self.sb, self.at, self.end = sb, at, end

    def take(self, *shape):
        n = int(np.prod(shape))
        a = self.sb[:, self.at:self.at + n]
        self.at += n
        assert self.at <= self.end, (self.at, self.end)
        if len(shape) == 2:
            a = a.rearrange("p (a b) -> p a b", a=shape[0])
        if len(shape) == 3:
            a = a.rearrange("p (a b c) -> p a b c", a=shape[0], b=shape[1])
        return a


def shape_constants():
    i = np.arange(P)
    c = {}
    c["ident"] = np.eye(P)
    c["ones"] = np.ones((P, P))
    c["bones"] = (i[:, None] // HS == i[None] // HS)
    for b in range(7):
        n = 1 << b
        c["lev%d" % b] = -1.0 * ((i[:, None] // (2 * n) == i[None] // (2 * n)) & (i[:, None] // n != i[None] // n))
    c["keep0"] = np.concatenate([i[:, None] < i[None], i[:, None] <= i[None]], 1)
    c["keep1"] = np.concatenate([i[:, None] > i[None], i[:, None] >= i[None]], 1)
    c["reset"] = np.tile((np.arange(TOK) % P != 0), (P, 1))
    c["head2"] = (i[:, None] // HS == np.arange(2)[None])
    c["iota32"] = np.tile(np.arange(NE), (P, 1))
    c["iotab"] = np.tile(np.arange(NBLK), (P, 1))
    c["tokid"] = (np.arange(LCH)[None] * P + i[:, None])
    names = list(c)
    first = np.concatenate([np.asarray(c[n], np.float64) for n in names], 1).astype(np.float32)
    at, off = {}, 0
    for n in names:
        at[n] = (off, c[n].shape[1])
        off += c[n].shape[1]
    r = {}
    half, nf = HS // 2, HS // 4
    inv = 10000.0 ** (-np.arange(nf) / nf)
    t = np.arange(LAT)
    ang = np.concatenate([(t // 64)[:, None] * inv, (t % 64)[:, None] * inv], 1).T
    ang = ang.astype(np.float32).astype(np.float64)
    r["cos"] = np.tile(np.cos(ang), (4, 1))
    r["sin"] = np.tile(np.sin(ang), (4, 1))
    rot = np.zeros((P, P))
    for o in range(P):
        h, d = o // HS, o % HS
        if d < half:
            rot[h * HS + d + half, o] = -1
        else:
            rot[h * HS + d - half, o] = 1
    r["rot"] = rot
    for h in range(4):
        g = 1 - 2.0 ** (-5 - h)
        x = np.arange(896)[None]
        y = np.arange(640)[None]
        r["near%d" % h] = g ** np.abs(x - 384 - i[:, None])
        r["far%d" % h] = g ** (y + 128.0 - i[:, None]) + g ** (640.0 - y + i[:, None])
    rat, off = {}, 0
    for n in r:
        rat[n] = (off, r[n].shape[1])
        off += r[n].shape[1]
    second = np.concatenate([r[n] for n in r], 1).astype(np.float32)
    return first, at, second, rat


CONST, CAT, RCONST, RAT = shape_constants()

ROWS = [("c", 8), ("c_ctx", 8), ("norm1_g", 8), ("rwkv_mu_prev", 15), ("rwkv_mu_next", 15), ("rwkv_w0", 8),
        ("rwkv_a0", 8), ("rwkv_k_k", 4), ("rwkv_k_a", 4), ("rwkv_r_k", 4), ("conv_b", 4), ("conv_ln_g", 4),
        ("conv_ln_b", 4), ("lru_conv_b", 8), ("lru_br", 8), ("lru_bi", 8), ("lru_lambda", 8),
        ("b_merge", 32), ("lru_conv_w", 32), ("ret_gn_g", 4), ("ret_gn_b", 4), ("conv_w", 124)]


def place_rows():
    at, n = {}, 0
    for name, k in ROWS:
        if n % P + k > P:
            n = (n // P + 1) * P
        at[name] = n
        n += k
    return at, (n + P - 1) // P


ROWAT, NROWT = place_rows()


def weight_groups():
    g = [("ada%d" % n, [("w_ada", n * GW, GW, 0)], 1) for n in range(6 * D // GW)]
    g.append(("lora0", [("w_in", C_LORA, GW, 0)], 2))
    g.append(("lora1", [("w_in", C_LORA + GW, P, 0)], 1))
    for h in range(2):
        for name, col in (("r", C_R), ("k", C_K), ("v", C_V)):
            g.append((name + str(h), [("w_in", col + h * HALF, HALF, 0)], HT))
    for name, col in (("cval", C_CVAL), ("cgate", C_CGATE), ("lx", C_LX), ("lg", C_LG),
                      ("qk", C_Q), ("rv", C_RV), ("rg", C_RG)):
        for h in range(2):
            g.append((name + str(h), [("w_in", col + h * GW, GW, 0)], NCH if name == "rv" else 2))
    for m in range(KT):
        for h in range(2):
            g.append(("merge%d" % (2 * m + h),
                      [("w_in", C_MERGE + (2 * h + b) * D + m * P, P, b * P) for b in range(2)], 2))
    for n in range(D // GW):
        g.append(("out%d" % n, [("w_out", n * GW, GW, 0)], LCH))
    return g


GROUPS = weight_groups()
GIDX = {g[0]: n for n, g in enumerate(GROUPS)}
TILE0 = {}
_n = 0
for _g in GROUPS:
    TILE0[_g[0]] = _n
    _n += _g[2]
NTILES = _n

NORM = {"norm1": 0, "kk": 1, "gn": 5, "conv": 6, "ret": 7, "norm2": 11, "final": 12}
SQUARED = {"norm1": 0, "conv": NCH, "ret": NCH + BT, "norm2": NCH + 2 * BT, "final": NCH + 2 * BT + LCH}
CLEARED = {"rows": 0, "zeros": 1, "raw": 2, "lx": 4, "u": 5, "wb": 6}
TURNED = {"rows": 0, "x": 1, "v": 1 + KT, "z": 7 + KT, "h2": 7 + KT + BT}


class Kernel:

    def __init__(self, nc, ctx, ins, out):
        self.nc, self.ctx, self.ins, self.out = nc, ctx, ins, out
        words = 53100
        self.sb = ctx.enter_context(nc.sbuf_tensor("arena", [P, words], F32))
        self.bank = [ctx.enter_context(nc.psum_tensor("bank%d" % b, [P, 512], F32))[:, :] for b in range(8)]
        self.sems = {}
        a = Arena(self.sb, 0, words)
        self.const = a.take(CONST.shape[1])
        self.cols = a.take(NROWT, P)
        self.modc = a.take(16, 2)
        self.modA = a.take(8, 2)
        self.silu_c = a.take(KT, 2)
        self.small = a.take(256)
        self.ring_at = a.at
        self.ring = a.take(RSLOT, SLOTW)
        self.hT = a.take(KT, TOK)
        self.after_rwkv = a.at
        self.Ar = a.take(BT, LAT)
        self.free = a.at
        self.words = words
        self.zeros = Arena(self.sb, words - 300, words).take(GW)
        dram = lambda n, s, t: nc.dram_tensor(n, s, t, kind="Internal").ap()
        self.mod_dram = dram("mod_rows", (1, 6 * D), F32)
        self.h2_dram = dram("h2_rows", (LAT, D), F32)
        self.list_dram = dram("slot_tokens", (NBLK * P, 1), I32)
        self.y_dram = dram("expert_rows", (NBLK * P, D), F32)

    def sem(self, name):
        if name not in self.sems:
            self.sems[name] = self.ctx.enter_context(self.nc.semaphore(name))
        return self.sems[name]

    def c(self, name):
        o, n = CAT[name]
        return self.const[:, o:o + n]

    def col(self, name, j, n=1):
        r = ROWAT[name] + j
        return self.cols[:, r // P, r % P:r % P + n]

    def region(self, at=None):
        return Arena(self.sb, self.free if at is None else at, self.words)

    def slot(self, name, w=GW):
        return self.ring[:, GIDX[name] % RSLOT, :].rearrange("p (k n) -> p k n", k=KT)[:, :, 0:w]

    def await_weights(self, eng, name):
        n = GIDX[name]
        total = sum(16 * len(GROUPS[g][1]) for g in range(n % RSLOT, n + 1, RSLOT))
        eng.wait_ge(self.sem("weights%d" % (n % RSLOT)), total)


def bc(ap, shape):
    return ap.to_broadcast(shape)


def weights_sync(k, sp, first, last):
    for n in range(first, last):
        name, loads, _ = GROUPS[n]
        if n >= RSLOT:
            old = GROUPS[n - RSLOT]
            sp.wait_ge(k.sem("tile_done"), TILE0[old[0]] + old[2])
        for src, col, w, at in loads:
            view = k.ins[src][0].rearrange("(k p) n -> p k n", p=P)[:, :, col:col + w]
            dst = k.ring[:, n % RSLOT, :].rearrange("p (k n) -> p k n", k=KT)[:, :, at:at + w]
            sp.dma_start(dst, view).then_inc(k.sem("weights%d" % (n % RSLOT)), 16)


class Stage1:
    def __init__(self, k):
        self.k = k
        a = k.region()
        self.X = a.take(NCH, D)
        self.mod = a.take(6 * D)
        self.bada = a.take(6 * D)
        self.rows = a.take(NROWT, P)
        self.sq = a.take(D)
        self.ss = k.small[:, 0:NCH]
        self.rs = k.small[:, 8:8 + NCH]

    def sync(self, sp):
        k = self.k
        sp.wait_ge(k.sem("cleared"), 1)
        sp.dma_start(k.const, k.ins["const_tables"]).then_inc(k.sem("const_in"), 16)
        n = 0
        for name, cnt in ROWS:
            r, src = ROWAT[name], k.ins[name]
            while len(src.shape) > 1:
                names = "abcdef"[:len(src.shape)]
                src = src.rearrange("%s -> (%s)" % (" ".join(names), " ".join(names)))
            t = r // P
            sp.dma_start(self.rows[r % P:r % P + cnt, t, :], src.rearrange("(j p) -> j p", p=P)).then_inc(k.sem("rows_in"), 16)
            n += 1
        sp.dma_start(self.bada[0:1, :], k.ins["b_ada"]).then_inc(k.sem("rows_in"), 16)
        weights_sync(k, sp, 0, RSLOT)
        sp.dma_start(self.X[:, 0:CCH, :], k.ins["ctx"][0].rearrange("(t p) d -> p t d", p=P)).then_inc(k.sem("x_in"), 16)
        sp.dma_start(self.X[:, CCH:NCH, :], k.ins["x"][0].rearrange("(t p) d -> p t d", p=P)).then_inc(k.sem("x_in"), 16)
        weights_sync(k, sp, RSLOT, GIDX["lora0"])
        sp.wait_ge(k.sem("tile_free"), TILE0["lora0"])
        sp.dma_start(k.mod_dram, self.mod[0:1, :]).then_inc(k.sem("mod_out"), 16)
        sp.wait_ge(k.sem("mod_out"), 16)
        weights_sync(k, sp, GIDX["lora0"], GIDX["v1"])
        sp.wait_ge(k.sem("cleared"), 2)
        sp.dma_start(k.y_dram.rearrange("(p b) (q n) -> p (b q) n", p=P, n=GW),
                     bc(k.zeros.unsqueeze(1), [P, NBLK * D // GW, GW])).then_inc(k.sem("rows_zeroed"), 16)
        sp.dma_start(k.list_dram.rearrange("(p b) a -> p (b a)", p=P),
                     k.zeros[:, 0:NBLK].bitcast(I32)).then_inc(k.sem("rows_zeroed"), 16)
        weights_sync(k, sp, GIDX["v1"], WLAST)

    def tensor(self, pe):
        k = self.k
        pe.wait_ge(k.sem("const_in"), 16)
        pe.wait_ge(k.sem("rows_in"), 16 * (len(ROWS) + 1))
        pe.wait_ge(k.sem("cleared"), 1)
        for t in range(NROWT):
            ins = pe.transpose(k.bank[7][:, t * P:(t + 1) * P], self.rows[:, t, :], k.c("ident"))
        ins.then_inc(k.sem("turned"), 1)
        pe.wait_ge(k.sem("silu_ready"), 2)
        for n in range(8):
            self.ada(pe, n)
        pe.wait_ge(k.sem("tile_free"), 8)
        for j in range(16):
            ins = pe.matmul(k.bank[7][:, 2 * j:2 * j + 2], self.mod[0:2, j * P:(j + 1) * P], k.c("ident")[0:2, 0:2],
                            start=True, stop=True)
        ins.then_inc(k.sem("modc_done"), 1)
        pe.wait_ge(k.sem("x_scaled"), NCH)
        for d in range(KT):
            if d >= 2:
                pe.wait_ge(k.sem("h_ready"), 2 * (d - 1))
            lat, ctx = k.bank[4 + d % 2], k.bank[6 + d % 2]
            if d == 1:
                pe.wait_ge(k.sem("modc_ready"), 1)
            for t in range(CCH):
                pe.transpose(ctx[:, t * P:(t + 1) * P], self.X[:, t, d * P:(d + 1) * P], k.c("ident"))
            for t in range(LCH):
                ins = pe.transpose(lat[:, t * P:(t + 1) * P], self.X[:, CCH + t, d * P:(d + 1) * P], k.c("ident"))
            ins.then_inc(k.sem("turned"), 1)
        for n in range(8, 24):
            self.ada(pe, n)

    def ada(self, pe, n):
        k = self.k
        k.await_weights(pe, "ada%d" % n)
        if n >= 2:
            pe.wait_ge(k.sem("tile_free"), n - 1)
        w = k.slot("ada%d" % n)
        bank = k.bank[2 * (n % 2)]
        for kt in range(KT):
            pe.matmul(bank[0:2, 0:GW], k.silu_c[:, kt, :], w[:, kt, :], start=(kt == 0), stop=False)
        pe.matmul(bank[0:2, 0:GW], k.c("ones")[0:1, 0:2], self.bada[0:1, n * GW:(n + 1) * GW],
                  start=False, stop=True).then_inc(k.sem("tile_done"), 1)

    def scalar(self, act):
        k = self.k
        act.wait_ge(k.sem("cols_ready"), 1)
        act.activation(k.silu_c[:, :, 0], k.col("c", 0, 8), ACT.Silu).then_inc(k.sem("silu_ready"), 1)
        act.activation(k.silu_c[:, :, 1], k.col("c_ctx", 0, 8), ACT.Silu).then_inc(k.sem("silu_ready"), 1)
        act.wait_ge(k.sem("x_in"), 32)
        for t in range(NCH):
            if t:
                act.wait_ge(k.sem("squared"), t)
            act.activation(self.sq, self.X[:, t, :], ACT.Square, accum_out=self.ss[:, t:t + 1]).then_inc(k.sem("squared"), 1)
        act.wait_ge(k.sem("variance"), 1)
        act.activation(self.rs, self.ss, ACT.Sqrt).then_inc(k.sem("root"), 1)
        for n in range(24):
            act.wait_ge(k.sem("tile_done"), n + 1)
            act.activation(self.mod[0:2, n * GW:(n + 1) * GW], k.bank[2 * (n % 2)][0:2, 0:GW], ACT.Copy).then_inc(k.sem("tile_free"), 1)

    def vector(self, dve, link):
        k = self.k
        dve.wait_ge(k.sem("turned"), 1)
        dve.tensor_copy(k.cols, k.bank[7][:, 0:NROWT * P].rearrange("p (a b) -> p a b", a=NROWT)).then_inc(k.sem("cols_ready"), 1)
        dve.wait_ge(k.sem("squared"), NCH)
        dve.tensor_scalar(self.ss, self.ss, 1.0 / D, 1e-6, ALU.mult, ALU.add).then_inc(k.sem("variance"), 1)
        dve.wait_ge(k.sem("root"), 1)
        link(dve.reciprocal(self.rs, self.rs))
        for t in range(NCH):
            dve.tensor_scalar(self.X[:, t, :], self.X[:, t, :], self.rs[:, t:t + 1], None, ALU.mult).then_inc(k.sem("x_scaled"), 1)
        dve.wait_ge(k.sem("cols_ready"), 1)
        dve.wait_ge(k.sem("modc_done"), 1)
        dve.tensor_copy(k.modc, k.bank[7][:, 0:32].rearrange("p (a b) -> p a b", a=16)).then_inc(k.sem("modc_ready"), 1)
        dve.wait_ge(k.sem("modc_ready"), 1)
        link(dve.tensor_scalar(k.modA, k.modc[:, 8:16, :], 1.0, None, ALU.add))
        link(dve.tensor_tensor(k.modA, k.modA, bc(k.col("norm1_g", 0, 8).unsqueeze(2), [P, 8, 2]), ALU.mult))
        for d in range(KT):
            dve.wait_ge(k.sem("turned"), TURNED["x"] + d + 1)
            dve.tensor_scalar(k.hT[:, d, 0:CTX], k.bank[6 + d % 2][:, 0:CTX], k.modA[:, d, 1:2], k.modc[:, d, 1:2],
                              ALU.mult, ALU.add).then_inc(k.sem("h_ready"), 1)
            dve.tensor_scalar(k.hT[:, d, CTX:TOK], k.bank[4 + d % 2], k.modA[:, d, 0:1], k.modc[:, d, 0:1],
                              ALU.mult, ALU.add).then_inc(k.sem("h_ready"), 1)

    def gpsimd(self, pool):
        k = self.k
        pool.memset(self.rows, 0.0).then_inc(k.sem("cleared"), 1)
        pool.memset(k.zeros, 0.0).then_inc(k.sem("cleared"), 1)


def project(k, pe, name, j, ctx, w=P):
    T = TILE0[name] + j
    if j == 0:
        k.await_weights(pe, name)
    pe.wait_ge(k.sem("tile_free"), T - 1)
    wt = k.slot(name)
    lat, cb = k.bank[2 * (T % 2)], k.bank[2 * (T % 2) + 1]
    for kt in range(KT):
        lhs = wt[:, kt, j * P:(j + 1) * P]
        if ctx:
            pe.matmul(cb[:, 0:CTX], lhs, k.hT[:, kt, 0:CTX], start=(kt == 0), stop=(kt == KT - 1))
        last = pe.matmul(lat[:, 0:LAT], lhs, k.hT[:, kt, CTX:TOK], start=(kt == 0), stop=(kt == KT - 1))
    last.then_inc(k.sem("tile_done"), 1)


def tile_banks(k, name, j):
    T = TILE0[name] + j
    return T, k.bank[2 * (T % 2)], k.bank[2 * (T % 2) + 1]


T_LORA = TILE0["lora0"]
RAWW = 1 + CTX + 1 + LAT + 1
RAW_C, RAW_L = 1, 2 + CTX


def span(at, n):
    return slice(at, at + n) if isinstance(at, int) else bass.ds(at, n)


class Stage2:
    def __init__(self, k):
        self.k = k
        a = k.region()
        self.R = a.take(HT, LAT)
        self.KK = a.take(HT, TOK)
        self.B = [a.take(HT, TOK) for d in range(2)]
        self.KD = [a.take(HT, TOK) for d in range(2)]
        self.C = [a.take(HT, NCH * (P + 1)) for d in range(2)]
        self.V = a.take(NCH, BW)
        self.bonus = a.take(LCH, 8)
        self.wlo, self.alo, self.glo = a.take(TOK), a.take(TOK), a.take(LAT)
        self.w2, self.a2, self.g2 = a.take(BW), a.take(BW), a.take(BW)
        self.mu0 = a.take(15)
        self.kac = a.take(4)
        self.Y = k.Ar.rearrange("p a b -> p (a b)").rearrange("p (a b) -> p a b", a=LCH)
        at = a.at
        self.st = []
        for d in range(2):
            s = {}
            if d == 0:
                at = a.at
            s["S0"] = a.take(HT, HS)
            s["ee"], s["fm"], s["ef"] = a.take(HT, 1), a.take(HT, 1), a.take(HT, 1)
            s["E"], s["F"] = a.take(HT, P + 1), a.take(HT, P + 1)
            s["AR"] = a.take(HT, 2, P)
            s["beta"], s["kappa"] = a.take(HT, P), a.take(HT, P)
            s["Vc"] = a.take(HALF)
            s["tok"] = a.take(2, HALF)
            s["LR"], s["MK"] = a.take(GH, 2, P), a.take(GH, 2, P)
            s["X"], s["XT"], s["T1"] = a.take(GH, P), a.take(GH, P), a.take(GH, P)
            s["rhs"], s["U"] = a.take(HALF), a.take(HALF)
            self.st.append(s)
        b = Arena(k.sb, at, a.at)
        self.K, self.VT, self.SQ = b.take(HT, TOK), b.take(HT, TOK), b.take(HT, TOK)
        self.lw, self.at = b.take(2, TOK), b.take(2, TOK)
        self.cs = b.take(2, TOK)
        self.raw = b.take(2, RAWW)
        b = Arena(k.sb, at, a.at)
        self.Z, self.Z2 = b.take(LCH, BW), b.take(LCH, BW)
        self.gng, self.gnb = b.take(BW), b.take(BW)
        self.mean, self.rstd = b.take(LCH, 8), b.take(LCH, 8)

    def loops_done(self, eng, g):
        for d in range(2):
            eng.wait_ge(self.k.sem("state_new%d" % d), (NCH + 1) * g)

    def chunk_loops(self, eng, body):
        body(0, False, 1, False)
        body(1, False, 2, True)
        with eng.Fori(CCH, NCH - 1) as i:
            body(i, True, i + 1, True)
        body(NCH - 1, True, None, True)

    def await_state(self, eng, d, g, i):
        eng.wait_ge(self.k.sem("state_new%d" % d), (NCH + 1) * g + 1 + i)

    def gpsimd(self, pool):
        k = self.k
        pool.wait_ge(k.sem("mod_out"), 16)
        pool.dma_start(self.w2, k.ins["rwkv_w2"][0].rearrange("d l n -> (d l) n")).then_inc(k.sem("lora_w_in"), 16)
        pool.dma_start(self.a2, k.ins["rwkv_a2"][0].rearrange("d l n -> (d l) n")).then_inc(k.sem("lora_w_in"), 16)
        pool.dma_start(self.g2, k.ins["rwkv_g2"][0]).then_inc(k.sem("lora_w_in"), 16)
        for g in range(2):
            if g:
                self.loops_done(pool, g)
            for s in range(2):
                pool.memset(self.raw[:, s, 0:1], 0.0)
                pool.memset(self.raw[:, s, RAW_L - 1:RAW_L], 0.0)
                ins = pool.memset(self.raw[:, s, RAWW - 1:RAWW], 0.0)
            ins.then_inc(k.sem("cleared"), 1)
            pool.wait_ge(k.sem("unit_used"), 4 * (g + 1))
            for lat in (False, True):
                with pool.Fori(CCH * lat, CCH + LCH * lat) as i:
                    for d in range(2):
                        self.await_state(pool, d, g, i)
                        ch = self.chunk(d, i, lat)
                        pool.tensor_copy(self.st[d]["Vc"].unsqueeze(1),
                                         self.V[:, bass.ds(ch, 1), g * HALF:(g + 1) * HALF]).then_inc(k.sem("v_chunk%d" % d), 1)
        self.loops_done(pool, 2)
        pool.dma_start(self.gng, k.ins["rwkv_gn_g"].to_broadcast([P, BW])).then_inc(k.sem("gn_in"), 16)
        pool.dma_start(self.gnb, k.ins["rwkv_gn_b"].to_broadcast([P, BW])).then_inc(k.sem("gn_in"), 16)

    def chunk(self, d, i, lat):
        return i if d == 0 else i * -1 + (NCH + CCH - 1 if lat else CCH - 1)

    def tensor(self, pe):
        k = self.k
        for g in range(2):
            if g:
                self.loops_done(pe, g)
            else:
                pe.wait_ge(k.sem("h_ready"), 2 * KT)
                project(k, pe, "lora0", 0, True)
                project(k, pe, "lora0", 1, True)
                project(k, pe, "lora1", 0, False)
            for j in range(HT):
                project(k, pe, "r%d" % g, j, False)
            for n in "kv":
                for j in range(HT):
                    project(k, pe, n + str(g), j, True)
            for j in range(HT):
                pe.wait_ge(k.sem("kk_squared"), HT * g + j + 1)
                pe.matmul(k.bank[4 + 2 * j][:, 0:CTX], k.c("bones"), self.SQ[:, j, 0:CTX], start=True, stop=True)
                pe.matmul(k.bank[5 + 2 * j], k.c("bones"), self.SQ[:, j, CTX:TOK], start=True,
                          stop=True).then_inc(k.sem("kk_summed"), 1)
            pe.wait_ge(k.sem("tile_free"), TILE0["v%d" % g] + HT)
            pe.wait_ge(k.sem("mixed"), TILE0["v%d" % g] + HT - T_LORA)
            for t in range(NCH):
                for j in range(HT):
                    ins = pe.transpose(k.bank[t // 2][:, (t % 2) * HALF + j * P:(t % 2) * HALF + (j + 1) * P],
                                       self.VT[:, j, t * P:(t + 1) * P], k.c("ident"))
                if t % 2:
                    ins.then_inc(k.sem("turned"), 1)
            pe.wait_ge(k.sem("rk_ready"), HT * (g + 1))
            for c in range(LCH):
                for j in range(HT):
                    o = (c * HT + j) * 2
                    ins = pe.matmul(k.bank[3][:, o:o + 2], self.SQ[:, j, CTX + c * P:CTX + (c + 1) * P], k.c("head2"),
                                    start=True, stop=True)
            ins.then_inc(k.sem("bonus_done"), 1)
            pe.wait_ge(k.sem("lora_w_in"), 48)
            pe.wait_ge(k.sem("lora_ready"), 1)
            for q in range(8):
                d, j, isa = q // 4, q // 2 % 2, q % 2
                if q < 2:
                    pe.wait_ge(k.sem("variance"), NORM["kk"] + HT * g + q + 1)
                else:
                    pe.wait_ge(k.sem("unit_half"), 8 * g + q - 1)
                w, src = (self.a2, self.alo) if isa else (self.w2, self.wlo)
                rows = slice(HS * d, HS * d + HS)
                ch = (HT * g + j) * P
                pe.matmul(k.bank[4 + 2 * (q % 2)][:, 0:CTX], w[rows, ch:ch + P], src[rows, 0:CTX], start=True, stop=True)
                pe.matmul(k.bank[5 + 2 * (q % 2)], w[rows, ch:ch + P], src[rows, CTX:TOK], start=True,
                          stop=True).then_inc(k.sem("unit_mm"), 1)
            pe.wait_ge(k.sem("v_copied"), 3 * (g + 1))
            pe.wait_ge(k.sem("bonus_copied"), g + 1)
            pe.wait_ge(k.sem("unit_half"), 8 * (g + 1))
            self.chunk_loops(pe, lambda i, lat, nxt, nlat: self.chunk_tensor(pe, g, i, lat))
        pe.wait_ge(k.sem("lora_ready"), 2)
        self.loops_done(pe, 2)
        for c in range(LCH):
            pe.matmul(k.bank[4 + c], self.glo[:, c * P:(c + 1) * P], self.g2, start=True, stop=True).then_inc(k.sem("gates_done"), 1)
        for j in range(BT):
            pe.wait_ge(k.sem("z_ready"), LCH)
            for c in range(LCH):
                ins = pe.transpose(k.bank[4 + j][:, c * P:(c + 1) * P], self.Z[:, c, j * P:(j + 1) * P], k.c("ident"))
            ins.then_inc(k.sem("turned"), 1)

    def score_count(self, g, i, lat):
        return 4 * (NCH * g + i)

    def chunk_tensor(self, pe, g, i, lat):
        k = self.k
        it = NCH * g + i
        n = 2 if lat else 1
        sc = self.score_count(g, i, lat)
        banks = [k.bank[4 * d:4 * d + 4] for d in range(2)]
        hs = lambda h: (slice(HS * (h % 2), HS * (h % 2) + HS), h // 2)
        for d in range(2):
            s = self.st[d]
            pe.wait_ge(k.sem("chunk_ops"), 2 * it + d + 1)
            if lat:
                pe.wait_ge(k.sem("rho_made"), 2 * (LCH * g + i - CCH) + d + 1)
            self.await_state(pe, d, g, i)
            pe.wait_ge(k.sem("y_added%d" % d), LCH * g + 1 + (i - CCH if lat else 0))
            for lhs, b0 in ((s["beta"], 0), (s["kappa"], 2)):
                for par in range(2):
                    for j in range(HT):
                        rows = slice(HS * par, HS * par + HS)
                        o = j * n * P
                        ins = pe.matmul(banks[d][b0 + par][:, o:o + n * P].rearrange("p (a b) -> p a b", a=n),
                                        lhs[rows, j, :], s["AR"][rows, j, 0:n, :], start=True, stop=True)
                    ins.then_inc(k.sem("scores%d" % d), 1)
        for d in range(2):
            s = self.st[d]
            pe.wait_ge(k.sem("scores_kept%d" % d), sc + 1)
            for a, x in enumerate((s["beta"], s["kappa"])):
                for j in range(HT):
                    ins = pe.transpose(banks[d][0][:, a * HALF + j * P:a * HALF + (j + 1) * P], x[:, j, :], k.c("ident"))
            ins.then_inc(k.sem("tok_done"), 1)
        for d in range(2):
            s = self.st[d]
            pe.wait_ge(k.sem("tok_copied"), 2 * it + d + 1)
            pe.wait_ge(k.sem("scores_kept%d" % d), sc + 4)
            pe.wait_ge(k.sem("v_chunk%d" % d), it + 1)
            for h in range(GH):
                rows, j = hs(h)
                o = banks[d][h % 2][:, j * HS:(j + 1) * HS]
                pe.matmul(o, s["AR"][rows, j, 0, :], s["S0"][rows, j, :], start=True, stop=False)
                ins = pe.matmul(o, s["MK"][:, h, 0, :], s["Vc"][:, h * HS:(h + 1) * HS], start=False, stop=True)
            ins.then_inc(k.sem("rhs_done"), 1)
        ident4 = bc(k.c("ident").unsqueeze(1), [P, GH, P])
        for d in range(2):
            for b in (2, 3):
                pe.matmul(banks[d][b].rearrange("p (a b) -> p a b", a=GH), k.c("ident"), ident4, start=True,
                          stop=False, skip_group_check=True)
        for l in range(7):
            for d in range(2):
                s = self.st[d]
                if l:
                    pe.wait_ge(k.sem("x_copied%d" % d), 7 * it + l)
                else:
                    pe.wait_ge(k.sem("rhs_copied"), 2 * it + d + 1)
                for h in range(GH):
                    ins = pe.matmul(banks[d][1][:, h * P:(h + 1) * P], s["LR"][:, h, 0, :],
                                    s["X"][:, h, :] if l else k.c("ident"), start=True, stop=True)
                ins.then_inc(k.sem("lx_done%d" % d), 1)
            for d in range(2):
                s = self.st[d]
                pe.wait_ge(k.sem("lx_kept%d" % d), 7 * it + l + 1)
                for h in range(GH):
                    xt = s["XT"][:, h, :] if l else k.c("ident")
                    if l < 6:
                        pe.matmul(banks[d][2][:, h * P:(h + 1) * P], xt, s["T1"][:, h, :], start=False, stop=False,
                                  skip_group_check=True)
                    ins = pe.matmul(banks[d][3][:, h * P:(h + 1) * P], s["T1"][:, h, :], xt, start=False,
                                    stop=(l == 6), skip_group_check=True)
                ins.then_inc(k.sem("x_done%d" % d), 1)
        for d in range(2):
            s = self.st[d]
            pe.wait_ge(k.sem("x_copied%d" % d), 7 * it + 7)
            for h in range(GH):
                ins = pe.matmul(banks[d][0][:, h * HS:(h + 1) * HS], s["XT"][:, h, :], s["rhs"][:, h * HS:(h + 1) * HS],
                                start=True, stop=True)
            ins.then_inc(k.sem("u_done"), 1)
        for d in range(2):
            s = self.st[d]
            pe.wait_ge(k.sem("u_copied"), 2 * it + d + 1)
            if lat:
                for h in range(GH):
                    rows, j = hs(h)
                    o, hv = banks[d][1 + h % 2][:, j * HS:(j + 1) * HS], slice(h * HS, (h + 1) * HS)
                    pe.matmul(o, s["AR"][rows, j, 1, :], s["S0"][rows, j, :], start=True, stop=False)
                    pe.matmul(o, s["LR"][:, h, 1, :], s["U"][:, hv], start=False, stop=False)
                    ins = pe.matmul(o, s["MK"][:, h, 1, :], s["Vc"][:, hv], start=False, stop=True)
                ins.then_inc(k.sem("y_done"), 1)
            for h in range(GH):
                rows, j = hs(h)
                o, hv = banks[d][0][rows, j * HS:(j + 1) * HS], slice(h * HS, (h + 1) * HS)
                pe.matmul(o, s["tok"][:, 0, hv], s["U"][:, hv], start=True, stop=False)
                ins = pe.matmul(o, s["tok"][:, 1, hv], s["Vc"][:, hv], start=False, stop=True)
            ins.then_inc(k.sem("state_grown"), 1)

    def scalar(self, act):
        k = self.k
        act.wait_ge(k.sem("mod_out"), 16)
        for g in range(2):
            if g:
                self.loops_done(act, g)
            act.wait_ge(k.sem("cleared"), CLEARED["raw"] + g + 1)
            tiles = ([("lora0", 0, 1), ("lora0", 1, 1), ("lora1", 0, 0)] if g == 0 else [])
            tiles += [("r%d" % g, j, 0) for j in range(HT)] + [(n + str(g), j, 1) for n in "kv" for j in range(HT)]
            for name, j, ctx in tiles:
                T, lat, cb = tile_banks(k, name, j)
                n = T - T_LORA
                act.wait_ge(k.sem("tile_done"), T + 1)
                if n >= 2:
                    act.wait_ge(k.sem("mixed"), n - 1)
                raw = self.raw[:, n % 2, :]
                if ctx:
                    act.activation(raw[:, RAW_C:RAW_C + CTX], cb[:, 0:CTX], ACT.Copy)
                act.activation(raw[:, RAW_L:RAW_L + LAT], lat, ACT.Copy).then_inc(k.sem("tile_free"), 1)
            if g == 0:
                act.wait_ge(k.sem("mixed"), 3)
                act.activation(self.wlo, self.wlo, ACT.Tanh).then_inc(k.sem("lora_ready"), 1)
                act.activation(self.glo, self.glo, ACT.Sigmoid).then_inc(k.sem("lora_ready"), 1)
            for j in range(HT):
                act.wait_ge(k.sem("variance"), NORM["kk"] + HT * g + j + 1)
                act.activation(self.cs[:, j, :], self.cs[:, j, :], ACT.Sqrt).then_inc(k.sem("root"), 1)
            for t in range(3):
                act.wait_ge(k.sem("turned"), TURNED["v"] + 3 * g + t + 1)
                act.activation(self.V[:, 2 * t:2 * t + 2, g * HALF:(g + 1) * HALF],
                               k.bank[t].rearrange("p (a b) -> p a b", a=2), ACT.Copy).then_inc(k.sem("v_copied"), 1)
            for q in range(8):
                d, j, isa = q // 4, q // 2 % 2, q % 2
                act.wait_ge(k.sem("unit_mm"), 8 * g + q + 1)
                if q >= 4:
                    act.wait_ge(k.sem("unit_used"), 4 * g + q // 2 - 1)
                dst = (self.at if isa else self.lw)[:, q // 2 % 2, :]
                bias = k.col("rwkv_a0" if isa else "rwkv_w0", 4 * d + HT * g + j)
                act.activation(dst[:, 0:CTX], k.bank[4 + 2 * (q % 2)][:, 0:CTX], ACT.Sigmoid, bias=bias)
                act.activation(dst[:, CTX:TOK], k.bank[5 + 2 * (q % 2)], ACT.Sigmoid, bias=bias).then_inc(k.sem("unit_half"), 1)
            act.wait_ge(k.sem("unit_used"), 4 * (g + 1))
            for d in range(2):
                self.exps(act, d, g, 0, False)
            self.chunk_loops(act, lambda i, lat, nxt, nlat: self.chunk_scalar(act, g, i, lat, nxt, nlat))
        act.wait_ge(k.sem("variance"), NORM["gn"] + 1)
        rstd = self.rstd.rearrange("p a b -> p (a b)")
        act.activation(rstd, rstd, ACT.Sqrt).then_inc(k.sem("root"), 1)
        for j in range(BT):
            act.wait_ge(k.sem("turned"), TURNED["z"] + j + 1)
            act.activation(k.Ar[:, j, :], k.bank[4 + j], ACT.Copy).then_inc(k.sem("rwkv_out"), 1)

    def exps(self, act, d, g, i, lat):
        s = self.st[d]
        src = self.C[d][:, :, span((P + 1) * self.chunk(d, i, lat), P + 1)]
        act.activation(s["E"], src, ACT.Exp).then_inc(self.k.sem("exps"), 1)
        act.activation(s["F"], src, ACT.Exp, scale=-1.0).then_inc(self.k.sem("exps"), 1)

    def chunk_scalar(self, act, g, i, lat, nxt, nlat):
        k = self.k
        it = NCH * g + i
        for d in range(2):
            s = self.st[d]
            act.wait_ge(k.sem("tok_done"), 2 * it + d + 1)
            act.activation(s["tok"].rearrange("p a b -> p (a b)"), k.bank[4 * d], ACT.Copy).then_inc(k.sem("tok_copied"), 1)
        for d in range(2):
            s = self.st[d]
            act.wait_ge(k.sem("rhs_done"), 2 * it + d + 1)
            for par in range(2):
                ins = act.activation(s["rhs"].rearrange("p (j q v) -> p j q v", q=2, v=HS)[:, :, par, :],
                                     k.bank[4 * d + par][:, 0:HT * HS].rearrange("p (j v) -> p j v", v=HS), ACT.Copy)
            ins.then_inc(k.sem("rhs_copied"), 1)
        for l in range(7):
            for d in range(2):
                s = self.st[d]
                act.wait_ge(k.sem("x_done%d" % d), 7 * it + l + 1)
                if l < 6:
                    act.activation(s["X"], k.bank[4 * d + 2].rearrange("p (a b) -> p a b", a=GH), ACT.Copy)
                act.activation(s["XT"], k.bank[4 * d + 3].rearrange("p (a b) -> p a b", a=GH), ACT.Copy).then_inc(k.sem("x_copied%d" % d), 1)
            if l == 0 and nxt is not None:
                for d in range(2):
                    act.wait_ge(k.sem("chunk_ops"), 2 * it + d + 1)
                    if lat:
                        act.wait_ge(k.sem("rho_made"), 2 * (LCH * g + i - CCH) + d + 1)
                    self.exps(act, d, g, nxt, nlat)
            if l == 1:
                for d in range(2):
                    s = self.st[d]
                    self.await_state(act, d, g, i)
                    end = (P + 1) * self.chunk(d, i, lat) + (P if d == 0 else 0)
                    mid = (P + 1) * (self.chunk(d, i, lat) if nxt is None else self.chunk(d, nxt, nlat)) + P * d
                    act.activation(s["ee"], self.C[d][:, :, span(end, 1)], ACT.Exp).then_inc(k.sem("ends"), 1)
                    act.activation(s["fm"], self.C[d][:, :, span(mid, 1)], ACT.Exp, scale=-1.0).then_inc(k.sem("ends"), 1)
        for d in range(2):
            s = self.st[d]
            act.wait_ge(k.sem("u_done"), 2 * it + d + 1)
            act.activation(s["U"], k.bank[4 * d][:, 0:HALF], ACT.Copy, scale=-1.0).then_inc(k.sem("u_copied"), 1)

    def mix(self, dve, link, name, j, mu, dst_ctx, dst_lat):
        k = self.k
        T = TILE0[name] + j
        n = T - T_LORA
        raw = self.raw[:, n % 2, :]
        dve.wait_ge(k.sem("tile_free"), T + 1)
        parts = ([(dst_ctx, RAW_C, CTX)] if dst_ctx is not None else []) + [(dst_lat, RAW_L, LAT)]
        for dst, o, w in parts:
            link.step(dve.tensor_scalar(dst, raw[:, o:o + w], self.mu0[:, mu:mu + 1], None, ALU.mult))
        link.wait()
        for dst, o, w in parts:
            link.step(dve.scalar_tensor_tensor(dst, raw[:, o - 1:o - 1 + w], k.col("rwkv_mu_prev", mu), dst, ALU.mult, ALU.add))
        link.wait()
        for dst, o, w in parts:
            ins = dve.scalar_tensor_tensor(dst, raw[:, o + 1:o + 1 + w], k.col("rwkv_mu_next", mu), dst, ALU.mult, ALU.add)
            if o == RAW_C:
                link.step(ins)
        ins.then_inc(k.sem("mixed"), 1)
        link.wait()
        dve.wait_ge(k.sem("mixed"), n + 1)

    def vector(self, dve, link):
        k = self.k
        dve.wait_ge(k.sem("mod_out"), 16)
        link(dve.tensor_tensor(self.mu0, k.col("rwkv_mu_prev", 0, 15), k.col("rwkv_mu_next", 0, 15), ALU.add))
        link(dve.tensor_scalar(self.mu0, self.mu0, -1.0, 1.0, ALU.mult, ALU.add))
        link(dve.tensor_scalar(self.kac, k.col("rwkv_k_a", 0, 4), -1.0, 1.0, ALU.mult, ALU.add))
        for d in range(2):
            dve.memset(self.Y[:, d * HT:(d + 1) * HT, :], 0.0).then_inc(k.sem("y_added%d" % d), 1)
        for g in range(2):
            if g == 0:
                self.mix(dve, link, "lora0", 0, 12, self.wlo[:, 0:CTX], self.wlo[:, CTX:TOK])
                self.mix(dve, link, "lora0", 1, 13, self.alo[:, 0:CTX], self.alo[:, CTX:TOK])
                self.mix(dve, link, "lora1", 0, 14, None, self.glo)
            for j in range(HT):
                self.mix(dve, link, "r%d" % g, j, HT * g + j, None, self.R[:, j, :])
            for j in range(HT):
                self.mix(dve, link, "k%d" % g, j, 4 + HT * g + j, self.K[:, j, 0:CTX], self.K[:, j, CTX:TOK])
            for j in range(HT):
                self.mix(dve, link, "v%d" % g, j, 8 + HT * g + j, self.VT[:, j, 0:CTX], self.VT[:, j, CTX:TOK])
            for j in range(HT):
                link(dve.tensor_scalar(self.KK[:, j, :], self.K[:, j, :], k.col("rwkv_k_k", HT * g + j), None, ALU.mult))
                dve.tensor_tensor(self.SQ[:, j, :], self.KK[:, j, :], self.KK[:, j, :], ALU.mult).then_inc(k.sem("kk_squared"), 1)
            for j in range(HT):
                dve.wait_ge(k.sem("kk_summed"), HT * g + j + 1)
                link.step(dve.tensor_scalar(self.cs[:, j, 0:CTX], k.bank[4 + 2 * j][:, 0:CTX], 1e-12, None, ALU.add))
                dve.tensor_scalar(self.cs[:, j, CTX:TOK], k.bank[5 + 2 * j], 1e-12, None, ALU.add).then_inc(k.sem("variance"), 1)
                dve.scalar_tensor_tensor(self.SQ[:, j, CTX:TOK], self.R[:, j, :], k.col("rwkv_r_k", HT * g + j),
                                         self.K[:, j, CTX:TOK], ALU.mult, ALU.mult).then_inc(k.sem("rk_ready"), 1)
            for j in range(HT):
                dve.wait_ge(k.sem("root"), NORM["kk"] + HT * g + j + 1)
                link(dve.reciprocal(self.cs[:, j, :], self.cs[:, j, :]))
                link(dve.tensor_tensor(self.KK[:, j, :], self.KK[:, j, :], self.cs[:, j, :], ALU.mult))
            dve.wait_ge(k.sem("bonus_done"), g + 1)
            dve.tensor_copy(self.bonus[:, :, GH * g:GH * g + GH],
                            k.bank[3][:, 0:LCH * GH].rearrange("p (a b) -> p a b", a=LCH)).then_inc(k.sem("bonus_copied"), 1)
            for u in range(4):
                d, j = u // 2, u % 2
                lw, a, cs = self.lw[:, u % 2, :], self.at[:, u % 2, :], self.cs[:, u % 2, :]
                dve.wait_ge(k.sem("unit_half"), 8 * g + 2 * u + 1)
                link(dve.tensor_scalar(lw, lw, LOGW, None, ALU.mult))
                back = slice(None, None, -1 if d else 1)
                link(dve.tensor_tensor_scan(cs[:, back], k.c("reset"), lw[:, back], 0.0, ALU.mult, ALU.add))
                cs3 = cs.rearrange("p (c t) -> p c t", t=P)
                mid = cs3[:, :, HS - 1 + d:HS + d]
                C = self.C[d][:, j, :].rearrange("p (c t) -> p c t", t=P + 1)
                dve.tensor_tensor(C[:, :, 1 - d:1 - d + P], cs3, bc(mid, [P, NCH, P]), ALU.subtract)
                dve.tensor_scalar(C[:, :, P * d:P * d + 1], mid, -1.0, None, ALU.mult)
                dve.wait_ge(k.sem("unit_half"), 8 * g + 2 * u + 2)
                dve.tensor_tensor(self.B[d][:, j, :], self.KK[:, j, :], a, ALU.mult)
                link(dve.tensor_scalar(self.KD[d][:, j, :], a, k.col("rwkv_k_a", HT * g + j), self.kac[:, HT * g + j:HT * g + j + 1],
                                       ALU.mult, ALU.add))
                dve.tensor_tensor(self.KD[d][:, j, :], self.KD[d][:, j, :], self.K[:, j, :], ALU.mult).then_inc(k.sem("unit_used"), 1)
            dve.wait_ge(k.sem("unit_used"), 4 * (g + 1))
            for d in range(2):
                dve.memset(self.st[d]["S0"], 0.0).then_inc(k.sem("state_new%d" % d), 1)
            for d in range(2):
                self.operands(dve, d, g, 0, False)
            self.chunk_loops(dve, lambda i, lat, nxt, nlat: self.chunk_vector(dve, g, i, lat, nxt, nlat))
        self.finish(dve, link)

    def operands(self, dve, d, g, i, lat):
        k, s = self.k, self.st[d]
        E, F = s["E"], s["F"]
        dve.wait_ge(k.sem("exps"), 4 * (NCH * g + i) + 2 * d + 2)
        cols = span(P * self.chunk(d, i, lat), P)
        dve.tensor_tensor(s["AR"][:, :, 0, :], self.KK[:, :, cols], E[:, :, d:d + P], ALU.mult)
        dve.tensor_tensor(s["beta"], self.B[d][:, :, cols], F[:, :, 1 - d:1 - d + P], ALU.mult)
        dve.tensor_tensor(s["kappa"], self.KD[d][:, :, cols], F[:, :, 1 - d:1 - d + P], ALU.mult).then_inc(k.sem("chunk_ops"), 1)

    def chunk_vector(self, dve, g, i, lat, nxt, nlat):
        k = self.k
        it = NCH * g + i
        sc = self.score_count(g, i, lat)
        n = 2 if lat else 1
        for d in range(2):
            s = self.st[d]
            keep = k.c("keep%d" % d)
            for q in range(4):
                dve.wait_ge(k.sem("scores%d" % d), sc + q + 1)
                dst = s["LR"] if q < 2 else s["MK"]
                dst = dst.rearrange("p (j q) a t -> p j q (a t)", q=2)[:, :, q % 2, 0:n * P]
                dve.tensor_tensor(dst, k.bank[4 * d + q][:, 0:HT * n * P].rearrange("p (j x) -> p j x", j=HT),
                                  bc(keep[:, 0:n * P].unsqueeze(1), [P, HT, n * P]), ALU.mult).then_inc(k.sem("scores_kept%d" % d), 1)
        for l in range(7):
            for d in range(2):
                s = self.st[d]
                dve.wait_ge(k.sem("lx_done%d" % d), 7 * it + l + 1)
                dve.tensor_tensor(s["T1"], k.bank[4 * d + 1].rearrange("p (a b) -> p a b", a=GH),
                                  bc(k.c("lev%d" % l).unsqueeze(1), [P, GH, P]), ALU.mult).then_inc(k.sem("lx_kept%d" % d), 1)
            if l == 1 and nxt is not None:
                dve.wait_ge(k.sem("tok_done"), 2 * it + 2)
                dve.wait_ge(k.sem("rhs_done"), 2 * it + 2)
                for d in range(2):
                    self.operands(dve, d, g, nxt, nlat)
        for d in range(2):
            s = self.st[d]
            if lat:
                dve.wait_ge(k.sem("y_done"), 2 * (LCH * g + i - CCH) + d + 1)
                dve.wait_ge(k.sem("y_added%d" % (1 - d)), LCH * g + 1 + i - CCH)
                dve.wait_ge(k.sem("y_added%d" % d), LCH * g + 1 + i - CCH)
                y = self.Y[:, span(self.chunk(d, i, lat) - CCH, 1), g * HALF:(g + 1) * HALF]
                y = y.rearrange("p a (j q v) -> p (a j) q v", q=2, v=HS)
                for par in range(2):
                    ins = dve.tensor_tensor(y[:, :, par, :], y[:, :, par, :],
                                            k.bank[4 * d + 1 + par][:, 0:HT * HS].rearrange("p (j v) -> p j v", v=HS), ALU.add)
                ins.then_inc(k.sem("y_added%d" % d), 1)
            if nlat and nxt is not None:
                dve.tensor_tensor(s["AR"][:, :, 1, :], self.R[:, :, span(P * (self.chunk(d, nxt, True) - CCH), P)],
                                  s["E"][:, :, 1 - d:1 - d + P], ALU.mult).then_inc(k.sem("rho_made"), 1)
            dve.wait_ge(k.sem("ends"), 4 * it + 2 * d + 2)
            dve.tensor_tensor(s["ef"], s["ee"], s["fm"], ALU.mult).then_inc(k.sem("state_sum"), 1)
            dve.wait_ge(k.sem("state_grown"), 2 * it + d + 1)
            dve.tensor_tensor(s["S0"], s["S0"], k.bank[4 * d][:, 0:HT * HS].rearrange("p (a b) -> p a b", a=HT),
                              ALU.add).then_inc(k.sem("state_sum"), 1)
            dve.wait_ge(k.sem("state_sum"), 4 * it + 2 * d + 2)
            dve.tensor_tensor(s["S0"], s["S0"], bc(s["ef"], [P, HT, HS]), ALU.mult).then_inc(k.sem("state_new%d" % d), 1)

    def finish(self, dve, link):
        k = self.k
        y4 = self.Y.rearrange("p c (h v) -> p (c h) v", v=HS)
        z4 = self.Z.rearrange("p c (h v) -> p (c h) v", v=HS)
        q4 = self.Z2.rearrange("p c (h v) -> p (c h) v", v=HS)
        v4 = self.V[:, CCH:NCH, :].rearrange("p c (h v) -> p (c h) v", v=HS)
        NH = LCH * 8
        flat = lambda x: x.rearrange("p a b -> p (a b)")
        wide = lambda x: bc(flat(x).unsqueeze(2), [P, NH, HS])
        for d in range(2):
            dve.wait_ge(k.sem("y_added%d" % d), 2 * LCH + 1)
        self.loops_done(dve, 2)
        link(dve.tensor_reduce(flat(self.mean), y4, AX, ALU.add))
        link(dve.tensor_scalar(flat(self.mean), flat(self.mean), 1.0 / HS, None, ALU.mult))
        link(dve.tensor_tensor(z4, y4, wide(self.mean), ALU.subtract))
        link(dve.tensor_tensor(q4, z4, z4, ALU.mult))
        link(dve.tensor_reduce(flat(self.rstd), q4, AX, ALU.add))
        dve.tensor_scalar(flat(self.rstd), flat(self.rstd), 1.0 / HS, 64e-5, ALU.mult, ALU.add).then_inc(k.sem("variance"), 1)
        dve.wait_ge(k.sem("root"), NORM["gn"] + 1)
        link(dve.reciprocal(flat(self.rstd), flat(self.rstd)))
        link(dve.tensor_tensor(z4, z4, wide(self.rstd), ALU.mult))
        dve.wait_ge(k.sem("gn_in"), 32)
        link(dve.tensor_tensor(self.Z, self.Z, bc(self.gng.unsqueeze(1), [P, LCH, BW]), ALU.mult))
        link(dve.tensor_tensor(q4, v4, wide(self.bonus), ALU.mult))
        link(dve.tensor_tensor(self.Z, self.Z, bc(self.gnb.unsqueeze(1), [P, LCH, BW]), ALU.add))
        link(dve.tensor_tensor(self.Z, self.Z, self.Z2, ALU.add))
        for c in range(LCH):
            dve.wait_ge(k.sem("gates_done"), c + 1)
            dve.tensor_tensor(self.Z[:, c, :], self.Z[:, c, :], k.bank[4 + c], ALU.mult).then_inc(k.sem("z_ready"), 1)


UW = LAT + CONV_K - 1
LP = 3
LXW = LP + CTX + LP + LAT + LP
XW = CTX + LP + LAT
XL = CTX + LP
NT_CONV = BT * CONV_K


class Stage3:
    def __init__(self, k):
        self.k = k
        a = k.region()
        k.Ac, k.Al, k.At = a.take(BT, LAT), a.take(BT, LAT), a.take(BT, LAT)
        k.free3 = a.at
        conv_at = a.at
        self.U, self.acc, self.sq = a.take(BT, UW), a.take(BT, LAT), a.take(BT, LAT)
        self.crs = a.take(LAT)
        lru_at = a.at
        self.LX = a.take(BT, LXW)
        self.xc, self.gr, self.gi, self.a = [a.take(2, XW) for n in range(4)]
        self.tmp = a.take(XW)
        self.WB = a.take(16, P)
        self.lam = a.take(6, 8)
        lru_end = a.at
        self.rt = a.take(LAT)
        self.q, self.kk, self.V = a.take(2, LAT), a.take(2, TOK), a.take(NCH, BW)
        self.att = a.take(2, LAT)
        self.tab = Arena(k.sb, lru_at, lru_end).take(RCONST.shape[1])
        b = Arena(k.sb, conv_at, lru_at)
        self.O, self.Osq, self.ors = b.take(2, LAT), b.take(2, LAT), b.take(2, LAT)

    def table(self, name):
        o, n = RAT[name]
        return self.tab[:, o:o + n]

    def gpsimd(self, pool):
        k = self.k
        pool.wait_ge(k.sem("rwkv_out"), BT)
        for j in range(BT):
            for lo, hi in ((0, LP), (LP + CTX, 2 * LP + CTX), (LXW - LP, LXW)):
                ins = pool.memset(self.LX[:, j, lo:hi], 0.0)
        ins.then_inc(k.sem("cleared"), 1)
        for j in range(BT):
            pool.memset(self.U[:, j, 0:CONV_K // 2], 0.0)
            ins = pool.memset(self.U[:, j, UW - CONV_K // 2:UW], 0.0)
        ins.then_inc(k.sem("cleared"), 1)
        pool.memset(self.WB, 0.0).then_inc(k.sem("cleared"), 1)
        pool.wait_ge(k.sem("cleared"), CLEARED["wb"] + 1)
        for w, name in enumerate(("lru_wr", "lru_wi")):
            for half in range(2):
                src = k.ins[name][0].rearrange("d (j q) a b -> q a (d j) b", q=2)[half]
                dst = self.WB[HS * half:HS * half + HS, 8 * w:8 * w + 8, HS * half:HS * half + HS]
                pool.dma_start(dst, src).then_inc(k.sem("wb_in"), 16)
        pool.wait_ge(k.sem("lru_out"), BT)
        pool.dma_start(self.tab, k.ins["ret_tables"]).then_inc(k.sem("tab_in"), 16)

    TAIL = ([("qk%d" % (n // 2), n % 2) for n in range(4)] + [("rv%d" % (n // NCH), n % NCH) for n in range(2 * NCH)]
            + [("rg%d" % (n // 2), n % 2) for n in range(4)])

    def tensor(self, pe):
        k = self.k
        for name in ("cval", "cgate"):
            for n in range(4):
                project(k, pe, "%s%d" % (name, n // 2), n % 2, False)
        for n in range(4):
            project(k, pe, "lx%d" % (n // 2), n % 2, True)
        for n in range(4):
            project(k, pe, "lg%d" % (n // 2), n % 2, False)
        pe.wait_ge(k.sem("rwkv_out"), BT)
        pe.wait_ge(k.sem("wb_in"), 64)
        for n, (name, j) in enumerate(self.TAIL):
            if n % 2 == 0 and n < 16:
                self.gates(pe, n // 2)
            if name[:2] == "rv":
                self.values(pe, name, j)
            else:
                project(k, pe, name, j, name == "qk1")
        pe.wait_ge(k.sem("gate_read"), 16)
        pe.wait_ge(k.sem("conv_done"), BT)
        for j in range(BT):
            ins = pe.matmul(k.bank[4], k.c("ones"), self.acc[:, j, :], start=(j == 0), stop=(j == BT - 1))
        ins.then_inc(k.sem("mean_summed"), 1)
        for j in range(BT):
            pe.wait_ge(k.sem("squared"), SQUARED["conv"] + j + 1)
            ins = pe.matmul(k.bank[5], k.c("ones"), self.sq[:, j, :], start=(j == 0), stop=(j == BT - 1))
        ins.then_inc(k.sem("var_summed"), 1)
        pe.wait_ge(k.sem("tab_in"), 16)
        pe.wait_ge(k.sem("tile_free"), TILE0["merge0"])
        for n, x in enumerate((self.q[:, 0, :], self.q[:, 1, :], self.kk[:, 0, CTX:TOK], self.kk[:, 1, CTX:TOK])):
            pe.matmul(k.bank[n], self.table("rot"), x, start=True, stop=True).then_inc(k.sem("rotated"), 1)
        for h in range(4):
            rows = slice(HS * (h % 2), HS * (h % 2) + HS)
            for jt in range(NCH):
                n = h * NCH + jt
                if n == 0:
                    pe.wait_ge(k.sem("rope_done"), 4)
                    pe.wait_ge(k.sem("centred"), BT)
                    pe.wait_ge(k.sem("variance"), NORM["conv"] + 1)
                if n >= 2:
                    pe.wait_ge(k.sem("att_kept"), n - 1)
                pe.matmul(k.bank[4 + n % 2], self.kk[rows, h // 2, jt * P:(jt + 1) * P], self.q[rows, h // 2, :],
                          start=True, stop=True).then_inc(k.sem("att_done"), 1)
                if n >= 1:
                    self.att_v(pe, n - 1)
            if h >= 1:
                self.ret_norm(pe, h - 1)
        self.att_v(pe, 4 * NCH - 1)
        self.ret_norm(pe, 3)

    def att_v(self, pe, n):
        k = self.k
        h, jt = n // NCH, n % NCH
        pe.wait_ge(k.sem("att_kept"), n + 1)
        if jt == 0 and h >= 2:
            pe.wait_ge(k.sem("o_copied"), h - 1)
        ins = pe.matmul(k.bank[6 + h % 2], self.V[:, jt, h * P:(h + 1) * P], self.att[:, n % 2, :],
                        start=(jt == 0), stop=(jt == NCH - 1))
        ins.then_inc(k.sem("att_used"), 1)

    def ret_norm(self, pe, h):
        k = self.k
        pe.wait_ge(k.sem("o_copied"), h + 1)
        if h:
            pe.wait_ge(k.sem("variance"), NORM["ret"] + h)
        pe.matmul(k.bank[0], k.c("ones"), self.O[:, h % 2, :], start=True, stop=True).then_inc(k.sem("mean_summed"), 1)
        pe.wait_ge(k.sem("squared"), SQUARED["ret"] + h + 1)
        pe.matmul(k.bank[1], k.c("ones"), self.Osq[:, h % 2, :], start=True, stop=True).then_inc(k.sem("var_summed"), 1)

    def values(self, pe, name, t):
        k = self.k
        T, lat, _ = tile_banks(k, name, t)
        if t == 0:
            k.await_weights(pe, name)
        pe.wait_ge(k.sem("tile_free"), T - 1)
        for kt in range(KT):
            ins = pe.matmul(lat[:, 0:GW], k.hT[:, kt, t * P:(t + 1) * P], k.slot(name)[:, kt, :], start=(kt == 0),
                            stop=(kt == KT - 1))
        ins.then_inc(k.sem("tile_done"), 1)

    def gates(self, pe, u):
        k = self.k
        j, d = u // 2, u % 2
        pe.wait_ge(k.sem("xc_ready"), u + 1)
        for w in range(2):
            if u:
                pe.wait_ge(k.sem("gate_read"), 2 * u - 1 + w)
            lhs = self.WB[:, 8 * w + 4 * d + j, :]
            pe.matmul(k.bank[5 + 2 * w][:, 0:CTX], lhs, self.xc[:, d, 0:CTX], start=True, stop=True)
            pe.matmul(k.bank[4 + 2 * w], lhs, self.xc[:, d, XL:XW], start=True, stop=True).then_inc(k.sem("gate_mm"), 1)

    def scalar(self, act):
        k = self.k
        act.wait_ge(k.sem("cleared"), CLEARED["u"] + 1)
        act.wait_ge(k.sem("cleared"), CLEARED["lx"] + 1)
        for n in range(4):
            T, lat, _ = tile_banks(k, "cval%d" % (n // 2), n % 2)
            act.wait_ge(k.sem("tile_done"), T + 1)
            act.activation(self.U[:, n, CONV_K // 2:CONV_K // 2 + LAT], lat, ACT.Copy).then_inc(k.sem("tile_free"), 1)
        for n in range(4):
            T, lat, _ = tile_banks(k, "cgate%d" % (n // 2), n % 2)
            act.wait_ge(k.sem("tile_done"), T + 1)
            act.activation(k.Ac[:, n, :], lat, ACT.Sigmoid).then_inc(k.sem("tile_free"), 1)
        for n in range(4):
            T, lat, cb = tile_banks(k, "lx%d" % (n // 2), n % 2)
            act.wait_ge(k.sem("tile_done"), T + 1)
            act.activation(self.LX[:, n, LP:LP + CTX], cb[:, 0:CTX], ACT.Copy)
            act.activation(self.LX[:, n, 2 * LP + CTX:2 * LP + CTX + LAT], lat, ACT.Copy).then_inc(k.sem("tile_free"), 1)
        for n in range(4):
            T, lat, _ = tile_banks(k, "lg%d" % (n // 2), n % 2)
            act.wait_ge(k.sem("tile_done"), T + 1)
            act.activation(k.Al[:, n, :], lat, ACT.Gelu_apprx_tanh).then_inc(k.sem("tile_free"), 1)
        act.activation(self.lam[:, 0, :], k.col("lru_lambda", 0, 8), ACT.Abs).then_inc(k.sem("lam_abs"), 1)
        act.wait_ge(k.sem("lam_abs"), 1)
        act.activation(self.lam[:, 1, :], self.lam[:, 0, :], ACT.Exp, scale=-1.0).then_inc(k.sem("lam_exp"), 1)
        for n, (name, j) in enumerate(self.TAIL):
            T, lat, cb = tile_banks(k, name, j)
            if n % 2 == 0 and n < 16:
                self.gate_scalar(act, n // 2)
            act.wait_ge(k.sem("tile_done"), T + 1)
            if name[:2] == "rv":
                ins = act.activation(self.V[:, j, int(name[2]) * GW:int(name[2]) * GW + GW], lat[:, 0:GW], ACT.Copy)
            elif name[:2] == "rg":
                ins = act.activation(k.At[:, 2 * int(name[2]) + j, :], lat, ACT.Silu)
            elif name == "qk0":
                ins = act.activation(self.q[:, j, :], lat, ACT.Copy)
            else:
                act.activation(self.kk[:, j, 0:CTX], cb[:, 0:CTX], ACT.Copy, scale=0.125)
                ins = act.activation(self.kk[:, j, CTX:TOK], lat, ACT.Copy, scale=0.125)
            ins.then_inc(k.sem("tile_free"), 1)
        for j in range(BT):
            act.wait_ge(k.sem("centred"), j + 1)
            act.activation(self.sq[:, j, :], self.acc[:, j, :], ACT.Square).then_inc(k.sem("squared"), 1)
        act.wait_ge(k.sem("variance"), NORM["conv"] + 1)
        act.activation(self.crs, self.crs, ACT.Sqrt).then_inc(k.sem("root"), 1)
        for j in range(BT):
            act.wait_ge(k.sem("conv_normed"), j + 1)
            act.activation(k.Ac[:, j, :], self.acc[:, j, :], ACT.Silu, bias=k.col("conv_ln_b", j),
                           scale=k.col("conv_ln_g", j)).then_inc(k.sem("conv_out"), 1)
        act.wait_ge(k.sem("conv_out"), BT)
        for h in range(4):
            act.wait_ge(k.sem("att_used"), NCH * (h + 1))
            if h >= 2:
                act.wait_ge(k.sem("ret_out"), h - 1)
            act.activation(self.O[:, h % 2, :], k.bank[6 + h % 2], ACT.Copy).then_inc(k.sem("o_copied"), 1)
            act.wait_ge(k.sem("centred"), BT + h + 1)
            act.activation(self.Osq[:, h % 2, :], self.O[:, h % 2, :], ACT.Square).then_inc(k.sem("squared"), 1)
            act.wait_ge(k.sem("variance"), NORM["ret"] + h + 1)
            act.activation(self.ors[:, h % 2, :], self.ors[:, h % 2, :], ACT.Sqrt).then_inc(k.sem("root"), 1)

    def gate_scalar(self, act, u):
        k = self.k
        j, d = u // 2, u % 2
        gr, gi, a = self.gr[:, d, :], self.gi[:, d, :], self.a[:, d, :]
        for w, (g, name) in enumerate(((gr, "lru_br"), (gi, "lru_bi"))):
            act.wait_ge(k.sem("gate_mm"), 2 * u + w + 1)
            if u >= 2:
                act.wait_ge(k.sem("lru_out"), j)
            bias = k.col(name, 4 * d + j)
            act.activation(g[:, 0:CTX], k.bank[5 + 2 * w][:, 0:CTX], ACT.Sigmoid, bias=bias)
            act.activation(g[:, XL:XW], k.bank[4 + 2 * w], ACT.Sigmoid, bias=bias).then_inc(k.sem("gate_read"), 1)
        act.wait_ge(k.sem("gate_read"), 2 * u + 2)
        act.wait_ge(k.sem("lam_ready"), 1)
        c = self.lam[:, 4, 4 * d + j:4 * d + j + 1]
        nc_ = self.lam[:, 5, 4 * d + j:4 * d + j + 1]
        act.activation(a[:, 0:CTX], gr[:, 0:CTX], ACT.Exp, scale=c)
        act.activation(a[:, XL:XW], gr[:, XL:XW], ACT.Exp, scale=c).then_inc(k.sem("lru_a"), 1)
        act.activation(gr[:, 0:CTX], gr[:, 0:CTX], ACT.Tanh, scale=nc_)
        act.activation(gr[:, XL:XW], gr[:, XL:XW], ACT.Tanh, scale=nc_).then_inc(k.sem("lru_a"), 1)
        act.wait_ge(k.sem("lru_power"), u + 1)
        act.activation(gr[:, 0:CTX], gr[:, 0:CTX], ACT.Sqrt)
        act.activation(gr[:, XL:XW], gr[:, XL:XW], ACT.Sqrt).then_inc(k.sem("lru_norm"), 1)

    def vector(self, dve, link):
        k = self.k
        lam = self.lam
        dve.wait_ge(k.sem("rwkv_out"), BT)
        dve.wait_ge(k.sem("lam_exp"), 1)
        link(dve.tensor_scalar(lam[:, 2, :], lam[:, 1, :], 2.0, None, ALU.add))
        link(dve.reciprocal(lam[:, 2, :], lam[:, 2, :]))
        link(dve.tensor_tensor(lam[:, 1, :], lam[:, 1, :], lam[:, 2, :], ALU.mult))
        link(dve.tensor_tensor(lam[:, 2, :], lam[:, 1, :], lam[:, 1, :], ALU.mult))
        link(dve.tensor_scalar(lam[:, 3, :], lam[:, 2, :], 1.0 / 19, 1.0 / 17, ALU.mult, ALU.add))
        for n in range(15, 0, -2):
            link(dve.tensor_tensor(lam[:, 3, :], lam[:, 3, :], lam[:, 2, :], ALU.mult))
            link(dve.tensor_scalar(lam[:, 3, :], lam[:, 3, :], 1.0 / n, None, ALU.add))
        link(dve.tensor_tensor(lam[:, 3, :], lam[:, 3, :], lam[:, 1, :], ALU.mult))
        link(dve.tensor_scalar(lam[:, 0, :], k.col("lru_lambda", 0, 8), -1.0, 0.0, ALU.mult, ALU.max))
        link(dve.scalar_tensor_tensor(lam[:, 3, :], lam[:, 3, :], 2.0, lam[:, 0, :], ALU.mult, ALU.add))
        link(dve.tensor_scalar(lam[:, 4, :], lam[:, 3, :], -8.0, None, ALU.mult))
        dve.tensor_scalar(lam[:, 5, :], lam[:, 3, :], 8.0, None, ALU.mult).then_inc(k.sem("lam_ready"), 1)
        for j in range(BT):
            dve.wait_ge(k.sem("tile_free"), TILE0["cgate0"] + j + 1)
            u = self.U[:, j, CONV_K // 2:CONV_K // 2 + LAT]
            link(dve.tensor_tensor(u, u, k.Ac[:, j, :], ALU.mult))
        dve.wait_ge(k.sem("cleared"), CLEARED["lx"] + 1)
        dve.wait_ge(k.sem("cleared"), CLEARED["u"] + 1)
        for u in range(8):
            if u % 2 == 0:
                self.lru_conv(dve, link, u)
                self.lru_conv(dve, link, u + 1)
            self.conv_taps(dve, link, u * NT_CONV // 8, (u + 1) * NT_CONV // 8)
            self.lru_unit(dve, link, u)
        dve.wait_ge(k.sem("mean_summed"), 1)
        for j in range(BT):
            dve.scalar_tensor_tensor(self.acc[:, j, :], k.bank[4], -1.0 / BW, self.acc[:, j, :], ALU.mult,
                                     ALU.add).then_inc(k.sem("centred"), 1)
        dve.wait_ge(k.sem("var_summed"), 1)
        dve.tensor_scalar(self.crs, k.bank[5], 1.0 / BW, 1e-5, ALU.mult, ALU.add).then_inc(k.sem("variance"), 1)
        dve.wait_ge(k.sem("root"), NORM["conv"] + 1)
        link(dve.reciprocal(self.crs, self.crs))
        for j in range(BT):
            dve.wait_ge(k.sem("squared"), SQUARED["conv"] + j + 1)
            dve.tensor_tensor(self.acc[:, j, :], self.acc[:, j, :], self.crs, ALU.mult).then_inc(k.sem("conv_normed"), 1)
        dve.wait_ge(k.sem("tab_in"), 16)
        for n, x in enumerate((self.q[:, 0, :], self.q[:, 1, :], self.kk[:, 0, CTX:TOK], self.kk[:, 1, CTX:TOK])):
            dve.wait_ge(k.sem("rotated"), n + 1)
            link.step(dve.tensor_tensor(self.rt, k.bank[n], self.table("sin"), ALU.mult))
            link(dve.tensor_tensor(x, x, self.table("cos"), ALU.mult))
            dve.tensor_tensor(x, x, self.rt, ALU.add).then_inc(k.sem("rope_done"), 1)
            dve.wait_ge(k.sem("rope_done"), n + 1)
        for h in range(4):
            for jt in range(NCH):
                n = h * NCH + jt
                dve.wait_ge(k.sem("att_done"), n + 1)
                if n >= 2:
                    dve.wait_ge(k.sem("att_used"), n - 1)
                if jt < CCH:
                    decay = self.table("far%d" % h)[:, P - P * jt:P - P * jt + LAT]
                else:
                    decay = self.table("near%d" % h)[:, 3 * P - P * (jt - CCH):3 * P - P * (jt - CCH) + LAT]
                dve.tensor_tensor(self.att[:, n % 2, :], k.bank[4 + n % 2], decay, ALU.mult).then_inc(k.sem("att_kept"), 1)
            if h:
                self.ret_vector(dve, link, h - 1)
        self.ret_vector(dve, link, 3)

    def ret_vector(self, dve, link, h):
        k = self.k
        O, rs = self.O[:, h % 2, :], self.ors[:, h % 2, :]
        dve.wait_ge(k.sem("mean_summed"), 1 + h + 1)
        dve.wait_ge(k.sem("o_copied"), h + 1)
        dve.scalar_tensor_tensor(O, k.bank[0], -1.0 / P, O, ALU.mult, ALU.add).then_inc(k.sem("centred"), 1)
        dve.wait_ge(k.sem("var_summed"), 1 + h + 1)
        dve.tensor_scalar(rs, k.bank[1], 1.0 / P, 1e-5, ALU.mult, ALU.add).then_inc(k.sem("variance"), 1)
        dve.wait_ge(k.sem("root"), NORM["ret"] + h + 1)
        link(dve.reciprocal(rs, rs))
        link(dve.tensor_tensor(O, O, rs, ALU.mult))
        link(dve.tensor_scalar(O, O, k.col("ret_gn_g", h), k.col("ret_gn_b", h), ALU.mult, ALU.add))
        dve.tensor_tensor(k.At[:, h, :], k.At[:, h, :], O, ALU.mult).then_inc(k.sem("ret_out"), 1)

    def conv_taps(self, dve, link, lo, hi):
        k = self.k
        for n in range(lo, hi):
            j, t = n // CONV_K, n % CONV_K
            x, w = self.U[:, j, t:t + LAT], k.col("conv_w", t * BT + j)
            if t == 0:
                link(dve.tensor_scalar(self.acc[:, j, :], x, w, k.col("conv_b", j), ALU.mult, ALU.add))
            elif t < CONV_K - 1:
                link(dve.scalar_tensor_tensor(self.acc[:, j, :], x, w, self.acc[:, j, :], ALU.mult, ALU.add))
            else:
                dve.scalar_tensor_tensor(self.acc[:, j, :], x, w, self.acc[:, j, :], ALU.mult,
                                         ALU.add).then_inc(k.sem("conv_done"), 1)

    def lru_conv(self, dve, link, u):
        k = self.k
        j, d = u // 2, u % 2
        xc = self.xc[:, d, :]
        dve.wait_ge(k.sem("tile_free"), TILE0["lx0"] + j + 1)
        if j:
            dve.wait_ge(k.sem("gate_mm"), 2 * u - 2)
            dve.wait_ge(k.sem("lru_out"), j)
        for t in range(4):
            x = self.LX[:, j, LP * d + t:LP * d + t + XW]
            w = k.col("lru_conv_w", (4 * d + t) * BT + j)
            if t == 0:
                link(dve.tensor_scalar(xc, x, w, k.col("lru_conv_b", 4 * d + j), ALU.mult, ALU.add))
            elif t < 3:
                link(dve.scalar_tensor_tensor(xc, x, w, xc, ALU.mult, ALU.add))
            else:
                dve.scalar_tensor_tensor(xc, x, w, xc, ALU.mult, ALU.add).then_inc(k.sem("xc_ready"), 1)

    def lru_unit(self, dve, link, u):
        k = self.k
        j, d = u // 2, u % 2
        xc, gr, gi, a = self.xc[:, d, :], self.gr[:, d, :], self.gi[:, d, :], self.a[:, d, :]
        parts = (slice(0, CTX), slice(XL, XW))
        dve.wait_ge(k.sem("lru_a"), 2 * u + 2)
        for s in parts:
            link.step(dve.tensor_tensor(self.tmp[:, s], a[:, s], a[:, s], ALU.mult))
        link.wait()
        for s in parts:
            ins = dve.scalar_tensor_tensor(gr[:, s], self.tmp[:, s], 1.0, gr[:, s], ALU.add, ALU.mult)
        ins.then_inc(k.sem("lru_power"), 1)
        dve.wait_ge(k.sem("xc_ready"), u + 1)
        dve.wait_ge(k.sem("gate_read"), 2 * u + 2)
        for s in parts:
            link.step(dve.tensor_tensor(gi[:, s], gi[:, s], xc[:, s], ALU.mult))
        link.wait()
        dve.wait_ge(k.sem("lru_norm"), u + 1)
        for s in parts:
            link.step(dve.tensor_tensor(gi[:, s], gi[:, s], gr[:, s], ALU.mult))
        link.wait()
        dve.wait_ge(k.sem("gate_mm"), 2 * u + 2)
        if d == 0:
            c, l, last = slice(0, CTX), slice(XL, XW), slice(CTX - 1, CTX)
        else:
            c, l, last = slice(CTX - 1, None, -1), slice(XW - 1, XL - 1, -1), slice(0, 1)
        link(dve.tensor_tensor_scan(xc[:, c], a[:, c], gi[:, c], 0.0, ALU.mult, ALU.add))
        link(dve.tensor_tensor_scan(xc[:, l], a[:, l], gi[:, l], xc[:, last], ALU.mult, ALU.add))
        if d:
            link(dve.tensor_tensor(self.tmp[:, 0:LAT], self.xc[:, 0, XL:XW], self.xc[:, 1, XL:XW], ALU.add))
            dve.wait_ge(k.sem("tile_free"), TILE0["lg0"] + j + 1)
            dve.tensor_tensor(k.Al[:, j, :], k.Al[:, j, :], self.tmp[:, 0:LAT], ALU.mult).then_inc(k.sem("lru_out"), 1)


T_MERGE, T_OUT = TILE0["merge0"], TILE0["out0"]
PROJ = ("rwkv_proj", "conv_proj", "lru_proj", "ret_proj")


class Stage4:
    def __init__(self, k):
        self.k = k
        a = Arena(k.sb, k.words - 10600, k.words)
        self.X1 = k.X1 = a.take(LCH, D)
        self.mod = k.mod = a.take(4, D)
        self.fg = k.fg = a.take(D)
        k.slot_f, k.slot_i, k.wt = a.take(2, LCH), a.take(2, LCH), a.take(2, LCH)
        self.wr = a.take(KT, NE)
        self.br = a.take(NE)
        self.r = [a.take(LCH, NE) for n in range(5)]
        top = k.words - 10600
        b = Arena(k.sb, k.free3, top)
        self.mixed = b.take(KT, LAT)
        self.PRflat = b.take(2 * 4 * BT * P)
        self.gs = b.take(4, LAT)
        self.tmp = b.take(LAT)
        self.n2 = b.take(D)
        self.sqbuf = b.take(D)
        c = Arena(k.sb, k.free3, top)
        self.H2 = c.take(LCH, D)
        self.H2T = c.take(KT, LAT)
        c = Arena(k.sb, k.free, top)
        self.ss = k.small[:, 16:20]
        self.rs = k.small[:, 20:24]
        self.oh = [c.take(LCH, NE) for n in range(2)]
        self.g8 = c.take(LCH * NG, 8)
        self.gscore, self.gid = c.take(LCH, NG), c.take(LCH, NG)
        self.v1, self.v2 = c.take(LCH), c.take(LCH)
        self.be = c.take(NBLK, NE)
        self.gscore2 = c.take(LCH, NG)
        self.cntb = c.take(NBLK)
        self.tok_i = c.take(LCH).bitcast(I32)
        self.row = c.take(4, NE)
        self.place_f, self.place_i = c.take(2, LCH), c.take(2, LCH)
        k.block_e = k.small[:, 32:32 + NBLK]
        k.npair = k.small[:, 80:81]

    def sync(self, sp):
        k = self.k
        sp.wait_ge(k.sem("ret_out"), 4)
        sp.wait_ge(k.sem("tab_in"), 16)
        self.load_merge(sp, 0, 0)
        self.load_merge(sp, 1, 0)
        with sp.Fori(0, 3) as i:
            for u in range(2):
                m = i * 2 + (2 + u)
                sp.wait_ge(k.sem("proj_done"), i * 8 + (4 * u + 4))
                self.load_merge(sp, m, u)
        for n in range(D // GW):
            name, loads, _ = GROUPS[GIDX["out%d" % n]]
            old = GROUPS[GIDX[name] - RSLOT]
            sp.wait_ge(k.sem("tile_done"), TILE0[old[0]] + old[2])
            src, col, w, at = loads[0]
            sp.dma_start(k.slot(name), k.ins[src][0].rearrange("(k p) n -> p k n", p=P)[:, :, col:col + w])\
                .then_inc(k.sem("weights%d" % (GIDX[name] % RSLOT)), 16)
        sp.wait_ge(k.sem("h2_ready"), LCH)
        sp.dma_start(k.h2_dram.rearrange("(t p) d -> p t d", p=P), self.H2).then_inc(k.sem("h2_out"), 16)

    def load_merge(self, sp, m, par):
        k = self.k
        static = isinstance(m, int)
        for h in range(2):
            slot = (GIDX["merge0"] + 2 * (par if not static else m) + h) % RSLOT
            for b in range(2):
                base = C_MERGE + (2 * h + b) * D
                cols = slice(base + m * P, base + m * P + P) if static else bass.ds(m * P + base, P)
                sp.dma_start(k.ring[:, slot, :].rearrange("p (k n) -> p k n", k=KT)[:, :, b * P:(b + 1) * P],
                             k.ins["w_in"][0].rearrange("(k p) n -> p k n", p=P)[:, :, cols])\
                    .then_inc(k.sem("weights%d" % slot), 16)
        cols = slice(m * P, m * P + P) if static else bass.ds(m * P, P)
        par = m if static else par
        for b in range(4):
            sp.dma_start(self.PR4(par, b),
                         k.ins[PROJ[b]][0].rearrange("(k p) n -> p k n", p=P)[:, :, cols])\
                .then_inc(k.sem("proj_in%d" % par), 16)

    def PR4(self, par, b):
        o = (par * 4 + b) * BT * P
        return self.PRflat[:, o:o + BT * P].rearrange("p (k n) -> p k n", k=BT)

    def gpsimd(self, pool):
        k = self.k
        pool.wait_ge(k.sem("ret_out"), 4)
        pool.dma_start(self.X1, k.ins["x"][0].rearrange("(t p) d -> p t d", p=P)).then_inc(k.sem("x1_in"), 16)
        pool.dma_start(self.mod, k.mod_dram[:, 2 * D:6 * D].rearrange("a (r n) -> a r n", r=4).to_broadcast([P, 4, D])).then_inc(k.sem("x1_in"), 16)
        pool.dma_start(self.fg, k.ins["final_g"].rearrange("(a n) -> a n", a=1).to_broadcast([P, D])).then_inc(k.sem("x1_in"), 16)
        pool.dma_start(self.n2, k.ins["norm2_g"].to_broadcast([P, D])).then_inc(k.sem("x1_in"), 16)
        pool.dma_start(self.br, k.ins["b_router"].rearrange("(a n) -> a n", a=1).to_broadcast([P, NE])).then_inc(k.sem("x1_in"), 16)
        pool.dma_start(self.wr, k.ins["w_router"].rearrange("(k p) n -> p k n", p=P)).then_inc(k.sem("x1_in"), 16)
        pool.wait_ge(k.sem("rows_zeroed"), 32)
        for t in range(LCH):
            for q in range(2):
                pool.wait_ge(k.sem("slots_ready"), 2)
                pool.indirect_dma_start(out=k.list_dram,
                                        out_offset=bass.IndirectOffsetOnAxis(ap=self.place_i[:, q, t:t + 1].bitcast(U32), axis=0),
                                        in_=self.tok_i[:, t:t + 1], in_offset=None).then_inc(k.sem("list_out"), 16)

    def tensor(self, pe):
        k = self.k
        A = (k.Ar, k.Ac, k.Al, k.At)
        pe.wait_ge(k.sem("tile_free"), T_MERGE)
        pe.wait_ge(k.sem("variance"), NORM["ret"] + 4)
        pe.wait_ge(k.sem("ret_out"), 4)
        pe.wait_ge(k.sem("conv_out"), BT)
        g0 = GIDX["merge0"]
        with pe.Fori(0, 4) as i:
            for u in range(2):
                for b in range(4):
                    g = g0 + 2 * u + b // 2
                    if b % 2 == 0:
                        before = sum(16 * len(GROUPS[x][1]) for x in range(g % RSLOT, g + 1, RSLOT))
                        pe.wait_ge(k.sem("weights%d" % (g % RSLOT)), i * 32 + before)
                    q = 4 * u + b
                    pe.wait_ge(k.sem("tile_free"), i * 8 + (T_MERGE + q - 3))
                    w = k.ring[:, g % RSLOT, :].rearrange("p (k n) -> p k n", k=KT)
                    for kt in range(KT):
                        ins = pe.matmul(k.bank[q % 4], w[:, kt, (b % 2) * P:(b % 2 + 1) * P], k.hT[:, kt, CTX:TOK],
                                        start=(kt == 0), stop=(kt == KT - 1))
                    ins.then_inc(k.sem("tile_done"), 1)
                    if b == 0:
                        pe.wait_ge(k.sem("proj_in%d" % u), i * 64 + 64)
                    pe.wait_ge(k.sem("mix_step"), i * 8 + (q + 1))
                    for kt in range(BT):
                        ins = pe.matmul(k.bank[4 + q % 4], self.PR4(u, b)[:, kt, :], A[b][:, kt, :], start=(kt == 0),
                                        stop=(kt == BT - 1))
                    ins.then_inc(k.sem("proj_done"), 1)
        pe.wait_ge(k.sem("mix_step"), 4 + 32)
        pe.wait_ge(k.sem("tile_free"), T_OUT)
        for n in range(D // GW):
            name = "out%d" % n
            k.await_weights(pe, name)
            for t in range(LCH):
                q = n * LCH + t
                if q >= 4:
                    pe.wait_ge(k.sem("out_read"), q - 3)
                for kt in range(KT):
                    ins = pe.matmul(k.bank[q % 4][:, 0:GW], self.mixed[:, kt, t * P:(t + 1) * P], k.slot(name)[:, kt, :],
                                    start=(kt == 0), stop=(kt == KT - 1))
                ins.then_inc(k.sem("tile_done"), 1)
        for d in range(KT):
            pe.wait_ge(k.sem("h2_ready"), LCH)
            if d >= 2:
                pe.wait_ge(k.sem("h2t_copied"), d - 1)
            for t in range(LCH):
                ins = pe.transpose(k.bank[4 + d % 2][:, t * P:(t + 1) * P], self.H2[:, t, d * P:(d + 1) * P], k.c("ident"))
            ins.then_inc(k.sem("turned"), 1)
        pe.wait_ge(k.sem("h2t_copied"), KT)
        for t in range(LCH):
            for kt in range(KT):
                ins = pe.matmul(k.bank[6][:, t * NE:(t + 1) * NE], self.H2T[:, kt, t * P:(t + 1) * P], self.wr[:, kt, :],
                                start=(kt == 0), stop=(kt == KT - 1))
        ins.then_inc(k.sem("logits"), 1)
        pe.wait_ge(k.sem("chosen"), 1)
        M = self.r[2]
        for t in range(LCH):
            o = k.bank[7][:, t * NE:(t + 1) * NE]
            for s in range(t):
                pe.matmul(o, k.c("ones"), M[:, s, :], start=(s == 0), stop=False)
            pe.matmul(o, k.c("keep0")[:, 0:P], M[:, t, :], start=(t == 0), stop=True)
        for t in range(LCH):
            ins = pe.matmul(k.bank[7][:, LCH * NE:(LCH + 1) * NE], k.c("ones"), M[:, t, :], start=(t == 0), stop=(t == LCH - 1))
        ins.then_inc(k.sem("ranked"), 1)

    def scalar(self, act):
        k = self.k
        with act.Fori(0, 4) as i:
            for u in range(2):
                for b in range(4):
                    q = 4 * u + b
                    act.wait_ge(k.sem("tile_done"), i * 8 + (T_MERGE + q + 1))
                    act.wait_ge(k.sem("mix_step"), i * 8 + (q + 1))
                    act.activation(self.gs[:, q % 4, :], k.bank[q % 4], ACT.Sigmoid,
                                   bias=self.bmerge(i, u, b)).then_inc(k.sem("tile_free"), 1)
        act.wait_ge(k.sem("x1_ready"), 16)
        for t in range(LCH):
            if t:
                act.wait_ge(k.sem("squared"), SQUARED["norm2"] + t)
            act.activation(self.sqbuf, self.X1[:, t, :], ACT.Square, accum_out=self.ss[:, t:t + 1]).then_inc(k.sem("squared"), 1)
        act.wait_ge(k.sem("variance"), NORM["norm2"] + 1)
        act.activation(self.rs, self.ss, ACT.Sqrt).then_inc(k.sem("root"), 1)
        for d in range(KT):
            act.wait_ge(k.sem("turned"), TURNED["h2"] + d + 1)
            act.activation(self.H2T[:, d, :], k.bank[4 + d % 2], ACT.Copy).then_inc(k.sem("h2t_copied"), 1)
        act.wait_ge(k.sem("logits"), 1)
        act.activation(self.r[0], k.bank[6][:, 0:LCH * NE].rearrange("p (a b) -> p a b", a=LCH), ACT.Sigmoid).then_inc(k.sem("affinity"), 1)

    def bmerge(self, i, u, b):
        r = ROWAT["b_merge"] + b * KT + u
        return self.k.cols[:, r // P, bass.ds(i * 2 + r % P, 1)]

    def vector(self, dve, link):
        k = self.k
        dve.memset(k.small[:, 90:91], 0.0).then_inc(k.sem("mix_step"), 4)
        with dve.Fori(0, 4) as i:
            for u in range(2):
                for b in range(4):
                    q = 4 * u + b
                    dve.wait_ge(k.sem("tile_free"), i * 8 + (T_MERGE + q + 1))
                    dve.wait_ge(k.sem("proj_done"), i * 8 + (q + 1))
                    gs, pr = self.gs[:, q % 4, :], k.bank[4 + q % 4]
                    m = self.mixed[:, bass.ds(i * 2 + u, 1), :].rearrange("p a b -> p (a b)")
                    if b == 0:
                        dve.tensor_tensor(m, gs, pr, ALU.mult).then_inc(k.sem("mix_step"), 1)
                    else:
                        dve.wait_ge(k.sem("mix_step"), i * 8 + (q + 4))
                        dve.tensor_tensor(self.tmp, gs, pr, ALU.mult).then_inc(k.sem("mix_part"), 1)
                        dve.wait_ge(k.sem("mix_part"), i * 6 + (3 * u + b))
                        dve.tensor_tensor(m, m, self.tmp, ALU.add).then_inc(k.sem("mix_step"), 1)
        dve.wait_ge(k.sem("mix_step"), 36)
        dve.wait_ge(k.sem("x1_in"), 96)
        for n in range(D // GW):
            for t in range(LCH):
                q = n * LCH + t
                dve.wait_ge(k.sem("tile_done"), T_OUT + q + 1)
                cols = slice(n * GW, (n + 1) * GW)
                dve.tensor_tensor(self.tmp[:, (q % 2) * GW:(q % 2 + 1) * GW], k.bank[q % 4][:, 0:GW], self.mod[:, 0, cols],
                                  ALU.mult).then_inc(k.sem("out_read"), 1)
                dve.wait_ge(k.sem("out_read"), q + 1)
                dve.tensor_tensor(self.X1[:, t, cols], self.X1[:, t, cols], self.tmp[:, (q % 2) * GW:(q % 2 + 1) * GW],
                                  ALU.add).then_inc(k.sem("x1_ready"), 1)
        link(dve.scalar_tensor_tensor(self.mod[:, 2, :], self.mod[:, 2, :], 1.0, self.n2, ALU.add, ALU.mult))
        dve.wait_ge(k.sem("squared"), SQUARED["norm2"] + LCH)
        dve.tensor_scalar(self.ss, self.ss, 1.0 / D, 1e-6, ALU.mult, ALU.add).then_inc(k.sem("variance"), 1)
        dve.wait_ge(k.sem("root"), NORM["norm2"] + 1)
        link(dve.reciprocal(self.rs, self.rs))
        for t in range(LCH):
            link(dve.scalar_tensor_tensor(self.H2[:, t, :], self.X1[:, t, :], self.rs[:, t:t + 1], self.mod[:, 2, :], ALU.mult, ALU.mult))
            dve.tensor_tensor(self.H2[:, t, :], self.H2[:, t, :], self.mod[:, 1, :], ALU.add).then_inc(k.sem("h2_ready"), 1)
        self.route(dve, link)

    def first_of(self, link, dve, vals, best, ids, dst, scratch, n):
        sh = [P, LCH, n]
        big = 1000.0
        link(dve.tensor_tensor(scratch, vals, bc(best.unsqueeze(2), sh), ALU.is_equal))
        link(dve.tensor_scalar(scratch, scratch, -big, big, ALU.mult, ALU.add))
        link(dve.tensor_tensor(scratch, scratch, bc(ids.unsqueeze(1), sh), ALU.add))
        link(dve.tensor_reduce(self.v2, scratch, AX, ALU.min))
        link(dve.tensor_tensor(dst, bc(ids.unsqueeze(1), sh), bc(self.v2.unsqueeze(2), sh), ALU.is_equal))

    def route(self, dve, link):
        k = self.k
        aff, sel, M, s1, s2 = self.r
        ids = k.c("iota32")
        dve.wait_ge(k.sem("affinity"), 1)
        link(dve.tensor_tensor(sel, aff, bc(self.br.unsqueeze(1), [P, LCH, NE]), ALU.add))
        flat = lambda x: x.rearrange("p a b -> p (a b)")
        for n in range(LCH * NG):
            link.step(dve.max(self.g8[:, n, :], flat(sel)[:, n * EPG:(n + 1) * EPG]))
        link.wait()
        link(dve.tensor_tensor(flat(self.gscore), self.g8[:, :, 0], self.g8[:, :, 1], ALU.add))
        link(dve.tensor_reduce(self.v1, self.gscore, AX, ALU.max))
        self.first_of(link, dve, self.gscore, self.v1, ids[:, 0:NG], self.gid, self.gscore2, NG)
        s14 = s1.rearrange("p a (g e) -> p (a g) e", g=NG)
        link(dve.tensor_copy(s14, bc(flat(self.gid).unsqueeze(2), [P, LCH * NG, EPG])))
        link(dve.tensor_tensor(sel, sel, s1, ALU.mult))
        link(dve.tensor_scalar(s1, s1, 1e30, -1e30, ALU.mult, ALU.add))
        link(dve.tensor_tensor(sel, sel, s1, ALU.add))
        for q in range(2):
            link(dve.tensor_reduce(self.v1, sel, AX, ALU.max))
            self.first_of(link, dve, sel, self.v1, ids, self.oh[q], s1, NE)
            link(dve.tensor_tensor(s1, aff, self.oh[q], ALU.mult))
            link(dve.tensor_reduce(k.wt[:, q, :], s1, AX, ALU.add))
            if q == 0:
                link(dve.scalar_tensor_tensor(sel, self.oh[0], -3e30, sel, ALU.mult, ALU.add))
        dve.tensor_tensor(M, self.oh[0], self.oh[1], ALU.add).then_inc(k.sem("chosen"), 1)
        link(dve.tensor_tensor(self.v1, k.wt[:, 0, :], k.wt[:, 1, :], ALU.add))
        link(dve.reciprocal(self.v1, self.v1))
        link(dve.tensor_tensor(k.wt, k.wt, bc(self.v1.unsqueeze(1), [P, 2, LCH]), ALU.mult))
        dve.wait_ge(k.sem("ranked"), 1)
        cnt, nb, end, start = [self.row[:, n, :] for n in range(4)]
        link(dve.tensor_copy(cnt, k.bank[7][:, LCH * NE:(LCH + 1) * NE]))
        link(dve.tensor_scalar(nb, cnt, 0.5, None, ALU.is_gt))
        for n in range(1, LAT // P):
            link(dve.scalar_tensor_tensor(nb, cnt, n * P + 0.5, nb, ALU.is_gt, ALU.add))
        link(dve.tensor_tensor_scan(end, k.c("ones")[:, 0:NE], nb, 0.0, ALU.mult, ALU.add))
        link(dve.tensor_tensor(start, end, nb, ALU.subtract))
        link(dve.tensor_scalar(start, start, float(P), None, ALU.mult))
        rank = k.bank[7][:, 0:LCH * NE].rearrange("p (a b) -> p a b", a=LCH)
        link(dve.tensor_tensor(s2, rank, bc(start.unsqueeze(1), [P, LCH, NE]), ALU.add))
        for q in range(2):
            link(dve.tensor_tensor(s1, s2, self.oh[q], ALU.mult))
            link(dve.tensor_reduce(k.slot_f[:, q, :], s1, AX, ALU.add))
        blk = sel
        link(dve.tensor_scalar(blk, rank, P - 0.5, None, ALU.is_gt))
        for n in range(2, LAT // P):
            link(dve.scalar_tensor_tensor(blk, rank, n * P - 0.5, blk, ALU.is_gt, ALU.add))
        link(dve.scalar_tensor_tensor(blk, bc(start.unsqueeze(1), [P, LCH, NE]), 1.0 / P, blk, ALU.mult, ALU.add))
        link(dve.tensor_scalar(blk, blk, 1.0 - P * NBLK, None, ALU.mult))
        link(dve.scalar_tensor_tensor(s2, s2, float(NBLK), blk, ALU.mult, ALU.add))
        for q in range(2):
            link(dve.tensor_tensor(s1, s2, self.oh[q], ALU.mult))
            link(dve.tensor_reduce(self.place_f[:, q, :], s1, AX, ALU.add))
        link(dve.tensor_copy(self.place_i.bitcast(I32), self.place_f))
        link(dve.tensor_copy(self.tok_i, k.c("tokid")))
        dve.tensor_copy(k.slot_i.bitcast(I32), k.slot_f).then_inc(k.sem("slots_ready"), 1)
        sh = [P, NBLK, NE]
        link(dve.tensor_tensor(self.be, bc(end.unsqueeze(1), sh), bc(k.c("iotab").unsqueeze(2), sh), ALU.is_le))
        link(dve.tensor_reduce(self.cntb, self.be, AX, ALU.add))
        link(dve.tensor_scalar(self.cntb, self.cntb, float(NE - 1), None, ALU.min))
        link(dve.tensor_copy(k.block_e.bitcast(I32), self.cntb))
        link(dve.tensor_scalar(self.cntb[:, 0:NBLK // 2], k.c("iotab")[:, 0:NBLK:2], end[:, NE - 1:NE], None, ALU.is_lt))
        link(dve.tensor_reduce(self.v1[:, 0:1], self.cntb[:, 0:NBLK // 2], AX, ALU.add))
        dve.tensor_copy(k.npair.bitcast(I32), self.v1[:, 0:1]).then_inc(k.sem("slots_ready"), 1)


EW = 4096


class Stage5:
    def __init__(self, k):
        self.k = k
        a = Arena(k.sb, k.ring_at, k.free)
        self.w = [[a.take(KT, DE), a.take(KT, DE), a.take(DE // P, D)]]
        w2b = a.take(DE // P, D)
        b = Arena(k.sb, k.free3 + 8192, k.words - 10600)
        self.w.append([b.take(KT, DE), b.take(KT, DE), w2b])
        c = Arena(k.sb, k.free3, k.free3 + 8192)
        self.xg, self.xT = c.take(2, D), c.take(2, KT, P)
        self.g, self.gT = c.take(2, DE), c.take(2, DE // P, P)
        self.y = c.take(2, D)
        d = Arena(k.sb, k.free + 4096, k.free3)
        self.sil = d.take(2, DE)
        self.idx = d.take(NBLK).bitcast(I32)
        self.idu = d.take(2).bitcast(I32)
        self.spare_i = d.take(1).bitcast(I32)
        a = Arena(k.sb, k.ring_at, k.free)
        self.yg = a.take(LCH * 2, D)
        self.sq = a.take(D)
        self.ss, self.rs = k.small[:, 96:100], k.small[:, 100:104]

    def steps(self, eng):
        k = self.k
        eng.wait_ge(k.sem("slots_ready"), 2)
        eng.wait_ge(k.sem("primed"), 2)
        return eng.value_load(k.npair[0:1, :].bitcast(I32), min_val=1, max_val=NBLK // 2)

    def sync(self, sp):
        k = self.k
        sp.wait_ge(k.sem("h2_out"), 16)
        n = self.steps(sp)
        with sp.Fori(0, n) as i:
            for u in range(2):
                e = sp.value_load(k.block_e[0:1, bass.ds(i * 2 + u, 1)].bitcast(I32), min_val=0, max_val=NE - 1)
                sp.wait_ge(k.sem("h3_done"), i * 2 + (u + 1))
                for w, name in enumerate(("e_w1", "e_w3")):
                    sp.dma_start(self.w[u][w].unsqueeze(1), k.ins[name][0].rearrange("e (k p) n -> p e k n", p=P)[:, bass.ds(e, 1)])\
                        .then_inc(k.sem("w13_in%d" % u), 16)
                sp.wait_ge(k.sem("ye_done%d" % u), i * 2 + 2)
                sp.dma_start(self.w[u][2].unsqueeze(1), k.ins["e_w2"][0].rearrange("e (k p) n -> p e k n", p=P)[:, bass.ds(e, 1)])\
                    .then_inc(k.sem("w2_in%d" % u), 16)
        for t in range(LCH):
            sp.wait_ge(k.sem("out_ready"), t + 1)
            sp.dma_start(k.out[0, t * P:(t + 1) * P, :], k.X1[:, t, :]).then_inc(k.sem("stored"), 16)
        sp.wait_ge(k.sem("stored"), 16 * LCH)

    def gpsimd(self, pool):
        k = self.k
        pool.wait_ge(k.sem("list_out"), 16 * 2 * LCH)
        pool.wait_ge(k.sem("h2_out"), 16)
        pool.dma_start(self.idx, k.list_dram.rearrange("(p b) a -> p (b a)", p=P)).then_inc(k.sem("idx_in"), 16)
        pool.wait_ge(k.sem("idx_in"), 16)
        pool.wait_ge(k.sem("ranked"), 1)
        n = self.steps(pool)
        with pool.Fori(0, n) as i:
            for u in range(2):
                pool.wait_ge(k.sem("xt_copied"), i * 2 + (u + 1))
                pool.tensor_copy(self.idu[:, u:u + 1], self.idx[:, bass.ds(i * 2 + u, 1)]).then_inc(k.sem("idx_picked"), 1)
                pool.wait_ge(k.sem("idx_picked"), i * 2 + (u + 1))
                pool.tensor_copy(self.spare_i, self.idx[:, bass.ds(i + (u + 1), 1)])
                pool.indirect_dma_start(out=self.xg[:, u, :], out_offset=None, in_=k.h2_dram,
                                        in_offset=bass.IndirectOffsetOnAxis(ap=self.idu[:, u:u + 1].bitcast(U32), axis=0))\
                    .then_inc(k.sem("xg_in%d" % u), 16)
        pool.wait_ge(k.sem("rows_stored"), 2)
        for t in range(LCH):
            for q in range(2):
                pool.indirect_dma_start(out=self.yg[:, 2 * t + q, :], out_offset=None, in_=k.y_dram,
                                        in_offset=bass.IndirectOffsetOnAxis(ap=k.slot_i[:, q, t:t + 1].bitcast(U32), axis=0))\
                    .then_inc(k.sem("yg_in%d" % t), 16)

    def tensor(self, pe):
        k = self.k
        bank, ident = k.bank, k.c("ident")
        n = self.steps(pe)
        with pe.Fori(0, n) as i:
            for u in range(2):
                pe.wait_ge(k.sem("xg_in%d" % u), i * 16 + 16)
                if u:
                    pe.wait_ge(k.sem("ye_act0"), i + 1)
                    pe.wait_ge(k.sem("ye_dve0"), i + 1)
                for kt in range(KT):
                    ins = pe.transpose(bank[2 * u + kt // 4][:, (kt % 4) * P:(kt % 4 + 1) * P],
                                       self.xg[:, u, kt * P:(kt + 1) * P], ident)
                ins.then_inc(k.sem("x_lifted"), 1)
            for u in range(2):
                pe.wait_ge(k.sem("w13_in%d" % u), i * 32 + 32)
                pe.wait_ge(k.sem("xt_copied"), i * 2 + (u + 3))
                if u == 0:
                    pe.wait_ge(k.sem("ye_act1"), i + 1)
                    pe.wait_ge(k.sem("ye_dve1"), i + 1)
                for w, name in enumerate(("h1_done%d", "h3_done%d")):
                    for kt in range(KT):
                        ins = pe.matmul(bank[4 + 2 * u + w], self.xT[:, u, kt, :], self.w[u][w][:, kt, :],
                                        start=(kt == 0), stop=(kt == KT - 1))
                    ins.then_inc(k.sem("h1_done") if w == 0 else k.sem("h3_done"), 1)
            for u in range(2):
                pe.wait_ge(k.sem("g_ready"), i * 2 + (u + 1))
                for kt in range(DE // P):
                    ins = pe.transpose(bank[u][:, kt * P:(kt + 1) * P], self.g[:, u, kt * P:(kt + 1) * P], ident)
                ins.then_inc(k.sem("gt_done"), 1)
                pe.wait_ge(k.sem("gt_copied"), i * 2 + (u + 1))
                pe.wait_ge(k.sem("w2_in%d" % u), i * 16 + 16)
                for half in range(2):
                    for kt in range(DE // P):
                        ins = pe.matmul(bank[2 + 2 * u + half], self.gT[:, u, kt, :],
                                        self.w[u][2][:, kt, half * 512:(half + 1) * 512], start=(kt == 0),
                                        stop=(kt == DE // P - 1))
                    ins.then_inc(k.sem("ye_done%d" % u), 1)

    def scalar(self, act):
        k = self.k
        act.wait_ge(k.sem("rows_zeroed"), 32)
        n = self.steps(act)
        with act.Fori(0, n) as i:
            for u in range(2):
                act.wait_ge(k.sem("h1_done"), i * 2 + (u + 1))
                act.activation(self.sil[:, u, :], k.bank[4 + 2 * u], ACT.Silu).then_inc(k.sem("silu_made"), 1)
            for u in range(2):
                act.wait_ge(k.sem("ye_done%d" % u), i * 2 + 3)
                act.wait_ge(k.sem("y_out%d" % u), i * 16 + 16)
                act.activation(self.y[:, u, 0:512], k.bank[2 + 2 * u], ACT.Copy).then_inc(k.sem("ye_act%d" % u), 1)
                act.wait_ge(k.sem("ye_act%d" % u), i + 2)
                act.wait_ge(k.sem("ye_dve%d" % u), i + 2)
                act.dma_start(k.y_dram[bass.ds((i * 2 + u) * P, P), :], self.y[:, u, :]).then_inc(k.sem("y_out%d" % u), 16)
        for u in range(2):
            act.wait_ge(k.sem("y_out%d" % u), n * 16 + 16)
            act.activation(self.sil[:, u, 0:1], k.c("ones")[:, 0:1], ACT.Copy).then_inc(k.sem("rows_stored"), 1)
        for t in range(LCH):
            act.wait_ge(k.sem("x2_ready"), t + 1)
            if t:
                act.wait_ge(k.sem("squared"), SQUARED["final"] + t)
            act.activation(self.sq, k.X1[:, t, :], ACT.Square, accum_out=self.ss[:, t:t + 1]).then_inc(k.sem("squared"), 1)
        act.wait_ge(k.sem("variance"), NORM["final"] + 1)
        act.activation(self.rs, self.ss, ACT.Sqrt).then_inc(k.sem("root"), 1)

    def vector(self, dve, link):
        k = self.k
        for n, (name, count) in enumerate((("h3_done", 2), ("xt_copied", 2), ("ye_done0", 2), ("ye_done1", 2), ("ye_act0", 1), ("ye_act1", 1),
                                    ("ye_dve0", 1), ("ye_dve1", 1), ("y_out0", 16), ("y_out1", 16))):
            dve.memset(k.small[:, 110 + n:111 + n], 0.0).then_inc(k.sem(name), count)
        dve.wait_ge(k.sem("y_out1"), 16)
        dve.wait_ge(k.sem("slots_ready"), 2)
        dve.memset(k.small[:, 92:93], 0.0).then_inc(k.sem("primed"), 2)
        n = self.steps(dve)
        with dve.Fori(0, n) as i:
            for u in range(2):
                dve.wait_ge(k.sem("x_lifted"), i * 2 + (u + 1))
                for half in range(2):
                    ins = dve.tensor_copy(self.xT[:, u, 4 * half:4 * half + 4, :],
                                          k.bank[2 * u + half].rearrange("p (a b) -> p a b", a=4))
                ins.then_inc(k.sem("xt_copied"), 1)
            for u in range(2):
                dve.wait_ge(k.sem("silu_made"), i * 2 + (u + 1))
                dve.wait_ge(k.sem("h3_done"), i * 2 + (u + 3))
                dve.tensor_tensor(self.g[:, u, :], self.sil[:, u, :], k.bank[5 + 2 * u], ALU.mult).then_inc(k.sem("g_ready"), 1)
            for u in range(2):
                dve.wait_ge(k.sem("gt_done"), i * 2 + (u + 1))
                dve.tensor_copy(self.gT[:, u, :, :], k.bank[u].rearrange("p (a b) -> p a b", a=4)).then_inc(k.sem("gt_copied"), 1)
                dve.wait_ge(k.sem("ye_done%d" % u), i * 2 + 4)
                dve.wait_ge(k.sem("y_out%d" % u), i * 16 + 16)
                dve.tensor_copy(self.y[:, u, 512:1024], k.bank[3 + 2 * u]).then_inc(k.sem("ye_dve%d" % u), 1)
        for t in range(LCH):
            dve.wait_ge(k.sem("yg_in%d" % t), 32)
            y0, y1 = self.yg[:, 2 * t, :], self.yg[:, 2 * t + 1, :]
            link(dve.tensor_scalar(y0, y0, k.wt[:, 0, t:t + 1], None, ALU.mult))
            link(dve.scalar_tensor_tensor(y0, y1, k.wt[:, 1, t:t + 1], y0, ALU.mult, ALU.add))
            link(dve.tensor_tensor(y0, y0, k.mod[:, 3, :], ALU.mult))
            dve.tensor_tensor(k.X1[:, t, :], k.X1[:, t, :], y0, ALU.add).then_inc(k.sem("x2_ready"), 1)
        dve.wait_ge(k.sem("squared"), SQUARED["final"] + LCH)
        dve.tensor_scalar(self.ss, self.ss, 1.0 / D, 1e-6, ALU.mult, ALU.add).then_inc(k.sem("variance"), 1)
        dve.wait_ge(k.sem("root"), NORM["final"] + 1)
        link(dve.reciprocal(self.rs, self.rs))
        for t in range(LCH):
            dve.scalar_tensor_tensor(k.X1[:, t, :], k.X1[:, t, :], self.rs[:, t:t + 1], k.fg, ALU.mult, ALU.mult)\
                .then_inc(k.sem("out_ready"), 1)


WLAST = GIDX["merge0"]


def STAGES(k):
    return [Stage1(k), Stage2(k), Stage3(k), Stage4(k), Stage5(k)]


SEMS = [
    "tile_done",
    "weights0",
    "weights1",
    "weights2",
    "weights3",
    "cleared",
    "const_in",
    "rows_in",
    "x_in",
    "tile_free",
    "mod_out",
    "rows_zeroed",
    "turned",
    "silu_ready",
    "modc_done",
    "x_scaled",
    "h_ready",
    "modc_ready",
    "cols_ready",
    "squared",
    "variance",
    "root",
    "state_new0",
    "state_new1",
    "lora_w_in",
    "unit_used",
    "v_chunk0",
    "v_chunk1",
    "gn_in",
    "kk_squared",
    "kk_summed",
    "mixed",
    "rk_ready",
    "bonus_done",
    "lora_ready",
    "unit_half",
    "unit_mm",
    "v_copied",
    "bonus_copied",
    "gates_done",
    "z_ready",
    "chunk_ops",
    "rho_made",
    "y_added0",
    "y_added1",
    "scores0",
    "scores1",
    "scores_kept0",
    "scores_kept1",
    "tok_done",
    "tok_copied",
    "rhs_done",
    "x_copied0",
    "x_copied1",
    "rhs_copied",
    "lx_done0",
    "lx_done1",
    "lx_kept0",
    "lx_kept1",
    "x_done0",
    "x_done1",
    "u_done",
    "u_copied",
    "y_done",
    "state_grown",
    "rwkv_out",
    "exps",
    "ends",
    "state_sum",
    "wb_in",
    "lru_out",
    "tab_in",
    "gate_read",
    "conv_done",
    "mean_summed",
    "var_summed",
    "rotated",
    "rope_done",
    "centred",
    "att_kept",
    "att_done",
    "o_copied",
    "att_used",
    "xc_ready",
    "gate_mm",
    "lam_abs",
    "lam_exp",
    "conv_normed",
    "conv_out",
    "ret_out",
    "lam_ready",
    "lru_a",
    "lru_power",
    "lru_norm",
    "proj_done",
    "h2_ready",
    "h2_out",
    "proj_in0",
    "proj_in1",
    "x1_in",
    "slots_ready",
    "list_out",
    "mix_step",
    "out_read",
    "h2t_copied",
    "logits",
    "chosen",
    "ranked",
    "x1_ready",
    "affinity",
    "mix_part",
    "primed",
    "h3_done",
    "w13_in0",
    "w13_in1",
    "ye_done0",
    "ye_done1",
    "w2_in0",
    "w2_in1",
    "out_ready",
    "stored",
    "idx_in",
    "xt_copied",
    "idx_picked",
    "xg_in0",
    "xg_in1",
    "rows_stored",
    "yg_in0",
    "yg_in1",
    "ye_act0",
    "ye_dve0",
    "x_lifted",
    "ye_act1",
    "ye_dve1",
    "h1_done",
    "g_ready",
    "gt_done",
    "gt_copied",
    "silu_made",
    "y_out0",
    "y_out1",
    "x2_ready",
    "vector_step",
    "yg_in2",
    "yg_in3",
]

NAMES = ["x", "c", "ctx", "c_ctx", "w_ada", "b_ada", "norm1_g", "norm2_g", "w_in", "b_merge", "rwkv_mu_prev",
         "rwkv_mu_next", "rwkv_w0", "rwkv_w2", "rwkv_a0", "rwkv_a2", "rwkv_g2", "rwkv_k_k", "rwkv_k_a", "rwkv_r_k",
         "rwkv_gn_g", "rwkv_gn_b", "rwkv_proj", "conv_w", "conv_b", "conv_ln_g", "conv_ln_b", "conv_proj",
         "lru_conv_w", "lru_conv_b", "lru_wr", "lru_br", "lru_wi", "lru_bi", "lru_lambda", "lru_proj", "ret_gn_g",
         "ret_gn_b", "ret_proj", "w_out", "w_router", "b_router", "e_w1", "e_w3", "e_w2", "final_g"]


def backbone_block(nc, ins, out):
    with ExitStack() as ctx:
        k = Kernel(nc, ctx, ins, out)
        stages = STAGES(k)
        for s in SEMS:
            k.sem(s)
        block = ctx.enter_context(nc.Block())

        @block.sync
        def _(sp):
            for s in stages:
                if hasattr(s, "sync"):
                    s.sync(sp)

        @block.gpsimd
        def _(pool):
            for s in stages:
                if hasattr(s, "gpsimd"):
                    s.gpsimd(pool)

        @block.tensor
        def _(pe):
            for s in stages:
                if hasattr(s, "tensor"):
                    s.tensor(pe)

        @block.scalar
        def _(act):
            for s in stages:
                if hasattr(s, "scalar"):
                    s.scalar(act)

        @block.vector
        def _(dve):
            link = Chain(dve, k.sem("vector_step"))
            for s in stages:
                if hasattr(s, "vector"):
                    s.vector(dve, link)


def kernel(**inputs):
    import concourse.bacc as bacc
    from concourse.bass_utils import run_bass_kernel_spmd

    nc = bacc.Bacc("TRN2", target_bir_lowering=False, num_devices=1)
    arrays, ins = {}, {}
    for name in NAMES:
        arrays["in_" + name] = np.ascontiguousarray(inputs[name])
    arrays["in_const_tables"] = CONST
    arrays["in_ret_tables"] = RCONST
    for name, a in arrays.items():
        ins[name[3:]] = nc.dram_tensor(name, a.shape, mybir.dt.from_np(a.dtype), kind="ExternalInput").ap()
    out = nc.dram_tensor("out", (1, LAT, D), F32, kind="ExternalOutput").ap()
    backbone_block(nc, ins, out)
    result = run_bass_kernel_spmd(nc, [arrays], core_ids=[0])
    return result.results[0]["out"]
```

```python
from contextlib import ExitStack

import numpy as np

import concourse.bass as bass
from concourse import mybir

F32 = mybir.dt.float32
I32 = mybir.dt.int32
U32 = mybir.dt.uint32
BF16 = mybir.dt.bfloat16
ALU = mybir.AluOpType
ACT = mybir.ActivationFunctionType
AX = mybir.AxisListType.X

P = 128
D = 1024
KT = D // P
CTX, LAT = 256, 512
TOK = CTX + LAT
NCH = TOK // P
CCH, LCH = CTX // P, LAT // P
BW = 512
BT = BW // P
HS = 64
GH = 4
HALF = GH * HS
HT = HALF // P
NE, NG, TOPK = 32, 4, 2
EPG = NE // NG
DE = 512
SL = 64
NBLK = LAT * TOPK // SL + NE
NPAIR = NBLK // 2
CONV_K = 31
LOGW = -float(np.exp(-0.5))
GW = 256
RSLOT = 4
SLOTW = KT * GW

C_R, C_K, C_V, C_LORA = 0, 512, 1024, 1536
C_CVAL, C_CGATE, C_LX, C_LG = 1920, 2432, 2944, 3456
C_Q, C_RV, C_RG, C_MERGE = 3968, 4480, 4992, 5504


class Chain:

    def __init__(self, eng, sem):
        self.eng, self.sem, self.base, self.k = eng, sem, 0, 0

    def __call__(self, ins):
        self.k += 1
        ins.then_inc(self.sem, 1)
        self.eng.wait_ge(self.sem, self.base + self.k)

    def step(self, ins):
        self.k += 1
        ins.then_inc(self.sem, 1)

    def wait(self):
        self.eng.wait_ge(self.sem, self.base + self.k)

    def start(self, base):
        self.base, self.k = base, 0


class Arena:

    def __init__(self, sb, at, end):
        self.sb, self.at, self.end = sb, at, end

    def take(self, *shape):
        n = int(np.prod(shape))
        a = self.sb[:, self.at:self.at + n]
        self.at += n
        assert self.at <= self.end, (self.at, self.end)
        if len(shape) == 2:
            a = a.rearrange("p (a b) -> p a b", a=shape[0])
        if len(shape) == 3:
            a = a.rearrange("p (a b c) -> p a b c", a=shape[0], b=shape[1])
        return a


def shape_constants():
    i = np.arange(P)
    c = {}
    c["ident"] = np.eye(P)
    c["ones"] = np.ones((P, P))
    c["bones"] = (i[:, None] // HS == i[None] // HS)
    for b in range(7):
        n = 1 << b
        c["lev%d" % b] = -1.0 * ((i[:, None] // (2 * n) == i[None] // (2 * n)) & (i[:, None] // n != i[None] // n))
    c["keep0"] = np.concatenate([i[:, None] < i[None], i[:, None] <= i[None]], 1)
    c["keep1"] = np.concatenate([i[:, None] > i[None], i[:, None] >= i[None]], 1)
    c["reset"] = np.tile((np.arange(TOK) % P != 0), (P, 1))
    c["head2"] = (i[:, None] // HS == np.arange(2)[None])
    c["iota32"] = np.tile(np.arange(NE), (P, 1))
    c["iotab"] = np.tile(np.arange(NBLK), (P, 1))
    c["tokid"] = (np.arange(LCH)[None] * P + i[:, None])
    names = list(c)
    first = np.concatenate([np.asarray(c[n], np.float64) for n in names], 1).astype(np.float32)
    at, off = {}, 0
    for n in names:
        at[n] = (off, c[n].shape[1])
        off += c[n].shape[1]
    r = {}
    half, nf = HS // 2, HS // 4
    inv = 10000.0 ** (-np.arange(nf) / nf)
    t = np.arange(LAT)
    ang = np.concatenate([(t // 64)[:, None] * inv, (t % 64)[:, None] * inv], 1).T
    ang = ang.astype(np.float32).astype(np.float64)
    r["cos"] = np.tile(np.cos(ang), (4, 1))
    r["sin"] = np.tile(np.sin(ang), (4, 1))
    rot = np.zeros((P, P))
    for o in range(P):
        h, d = o // HS, o % HS
        if d < half:
            rot[h * HS + d + half, o] = -1
        else:
            rot[h * HS + d - half, o] = 1
    r["rot"] = rot
    for h in range(4):
        g = 1 - 2.0 ** (-5 - h)
        x = np.arange(896)[None]
        y = np.arange(640)[None]
        r["near%d" % h] = g ** np.abs(x - 384 - i[:, None])
        r["far%d" % h] = g ** (y + 128.0 - i[:, None]) + g ** (640.0 - y + i[:, None])
    rat, off = {}, 0
    for n in r:
        rat[n] = (off, r[n].shape[1])
        off += r[n].shape[1]
    second = np.concatenate([r[n] for n in r], 1).astype(np.float32)
    return first, at, second, rat


CONST, CAT, RCONST, RAT = shape_constants()

ROWS = [("c", 8), ("c_ctx", 8), ("norm1_g", 8), ("rwkv_mu_prev", 15), ("rwkv_mu_next", 15), ("rwkv_w0", 8),
        ("rwkv_a0", 8), ("rwkv_k_k", 4), ("rwkv_k_a", 4), ("rwkv_r_k", 4), ("conv_b", 4), ("conv_ln_g", 4),
        ("conv_ln_b", 4), ("lru_conv_b", 8), ("lru_br", 8), ("lru_bi", 8), ("lru_lambda", 8),
        ("b_merge", 32), ("lru_conv_w", 32), ("ret_gn_g", 4), ("ret_gn_b", 4), ("conv_w", 124)]


def place_rows():
    at, n = {}, 0
    for name, k in ROWS:
        if n % P + k > P:
            n = (n // P + 1) * P
        at[name] = n
        n += k
    return at, (n + P - 1) // P


ROWAT, NROWT = place_rows()


def weight_groups():
    ada = [("ada%d" % n, [("w_ada", n * GW, GW, 0)], 1) for n in range(6 * D // GW)]
    g = ada[0:NADA]
    g.append(("lora0", [("w_in", C_LORA, GW, 0)], 2))
    g.append(("lora1", [("w_in", C_LORA + GW, P, 0)], 1))
    for h in range(2):
        for name, col in (("r", C_R), ("k", C_K), ("v", C_V)):
            g.append((name + str(h), [("w_in", col + h * HALF, HALF, 0)], HT))
        g += ada[NADA * (h + 1):NADA * (h + 2)]
    for h in range(2):
        for name, col in (("cval", C_CVAL), ("cgate", C_CGATE)):
            g.append((name + str(h), [("w_in", col + h * GW, GW, 0)], 2))
    for name, col in (("lx", C_LX), ("lg", C_LG),
                      ("qk", C_Q), ("rv", C_RV), ("rg", C_RG)):
        for h in range(2):
            g.append((name + str(h), [("w_in", col + h * GW, GW, 0)], NCH if name == "rv" else 2))
    for m in range(KT):
        for h in range(2):
            g.append(("merge%d" % (2 * m + h),
                      [("w_in", C_MERGE + (2 * h + b) * D + m * P, P, b * P) for b in range(2)], 2))
    for n in range(D // GW):
        g.append(("out%d" % n, [("w_out", n * GW, GW, 0)], LCH))
    return g


NADA = 2 * D // GW
GROUPS = weight_groups()
GIDX = {g[0]: n for n, g in enumerate(GROUPS)}
TILE0 = {}
_n = 0
for _g in GROUPS:
    TILE0[_g[0]] = _n
    _n += _g[2]
NTILES = _n

NORM = {"norm1": 0, "kk": 1, "gn": 5, "conv": 6, "ret": 7, "norm2": 11, "final": 12}
SQUARED = {"norm1": 0, "conv": NCH, "ret": NCH + BT, "norm2": NCH + 2 * BT, "final": NCH + 2 * BT + LCH}
CLEARED = {"rows": 0, "zeros": 1, "lora": 2, "raw": 4, "lx": 6, "u": 7, "wb": 8, "q": 9}
TURNED = {"rows": 0, "x": 1, "v": 1 + KT, "z": 7 + KT, "h2": 7 + KT + BT}


class Kernel:

    def __init__(self, nc, ctx, ins, out):
        self.nc, self.ctx, self.ins, self.out = nc, ctx, ins, out
        words = 53100
        self.sb = ctx.enter_context(nc.sbuf_tensor("arena", [P, words], F32))
        self.bank = [ctx.enter_context(nc.psum_tensor("bank%d" % b, [P, 512], F32))[:, :] for b in range(8)]
        self.sems = {}
        a = Arena(self.sb, 0, words)
        self.const = a.take(CONST.shape[1])
        self.cols = a.take(NROWT, P)
        self.modc = a.take(16, 2)
        self.modA = a.take(8, 2)
        self.silu_c = a.take(KT, 2)
        self.small = a.take(256)
        self.ring_at = a.at
        self.ring = a.take(RSLOT, SLOTW)
        self.hT = a.take(KT, TOK)
        self.after_rwkv = a.at
        self.Ar = a.take(BT, LAT)
        self.free = a.at
        self.words = words
        self.zeros = Arena(self.sb, words - 256, words).take(GW)
        dram = lambda n, s, t: nc.dram_tensor(n, s, t, kind="Internal").ap()
        self.mod_dram = dram("mod_rows", (1, 6 * D), F32)
        self.h2_dram = dram("h2_rows", (LAT, D), F32)
        self.list_dram = dram("slot_tokens", (NPAIR * P, 1), I32)
        self.y_dram = dram("expert_rows", (NPAIR * P, D), F32)

    def sem(self, name):
        if name not in self.sems:
            self.sems[name] = self.ctx.enter_context(self.nc.semaphore(name))
        return self.sems[name]

    def c(self, name):
        o, n = CAT[name]
        return self.const[:, o:o + n]

    def col(self, name, j, n=1):
        r = ROWAT[name] + j
        return self.cols[:, r // P, r % P:r % P + n]

    def region(self, at=None):
        return Arena(self.sb, self.free if at is None else at, self.words)

    def slot(self, name, w=GW):
        return self.ring[:, GIDX[name] % RSLOT, :].rearrange("p (k n) -> p k n", k=KT)[:, :, 0:w]

    def await_weights(self, eng, name):
        n = GIDX[name]
        total = sum(16 * len(GROUPS[g][1]) for g in range(n % RSLOT, n + 1, RSLOT))
        eng.wait_ge(self.sem("weights%d" % (n % RSLOT)), total)


def bc(ap, shape):
    return ap.to_broadcast(shape)


def weights_sync(k, sp, first, last):
    for n in range(first, last):
        name, loads, _ = GROUPS[n]
        if n >= RSLOT:
            old = GROUPS[n - RSLOT]
            sp.wait_ge(k.sem("tile_done"), TILE0[old[0]] + old[2])
        for src, col, w, at in loads:
            view = k.ins[src][0].rearrange("(k p) n -> p k n", p=P)[:, :, col:col + w]
            dst = k.ring[:, n % RSLOT, :].rearrange("p (k n) -> p k n", k=KT)[:, :, at:at + w]
            sp.dma_start(dst, view).then_inc(k.sem("weights%d" % (n % RSLOT)), 16)


class Stage1:
    def __init__(self, k):
        self.k = k
        a = k.region()
        self.X = a.take(NCH, D)
        self.mod = a.take(2 * D)
        self.bada = a.take(2 * D)
        self.rows = a.take(NROWT, P)
        self.sq = a.take(D)
        self.ss = k.small[:, 0:NCH]
        self.rs = k.small[:, 8:8 + NCH]

    def sync(self, sp):
        k = self.k
        sp.wait_ge(k.sem("cleared"), 1)
        sp.dma_start(k.const, k.ins["const_tables"]).then_inc(k.sem("const_in"), 16)
        self.load_rows(sp, 0)
        sp.dma_start(self.bada[0:1, :], k.ins["b_ada"][:, 0:2 * D]).then_inc(k.sem("rows_in"), 16)
        weights_sync(k, sp, 0, RSLOT)
        sp.dma_start(self.X[:, 0:CCH, :], k.ins["ctx"][0].rearrange("(t p) d -> p t d", p=P)).then_inc(k.sem("x_in"), 16)
        sp.dma_start(self.X[:, CCH:NCH, :], k.ins["x"][0].rearrange("(t p) d -> p t d", p=P)).then_inc(k.sem("x_in"), 16)
        weights_sync(k, sp, RSLOT, GIDX["v1"])
        sp.wait_ge(k.sem("cleared"), 2)
        sp.wait_ge(k.sem("exps"), 1)
        sp.dma_start(k.y_dram.rearrange("(p b) (q n) -> p (b q) n", p=P, n=GW),
                     bc(k.zeros.unsqueeze(1), [P, NPAIR * D // GW, GW])).then_inc(k.sem("rows_zeroed"), 16)
        sp.dma_start(k.list_dram.rearrange("(p b) a -> p (b a)", p=P),
                     k.zeros[:, 0:NPAIR].bitcast(I32)).then_inc(k.sem("rows_zeroed"), 16)
        weights_sync(k, sp, GIDX["v1"], WLAST)

    def load_rows(self, eng, half):
        k = self.k
        for name, cnt in ROWS[half::2]:
            r, src = ROWAT[name], k.ins[name]
            while len(src.shape) > 1:
                names = "abcdef"[:len(src.shape)]
                src = src.rearrange("%s -> (%s)" % (" ".join(names), " ".join(names)))
            eng.dma_start(self.rows[r % P:r % P + cnt, r // P, :], src.rearrange("(j p) -> j p", p=P))\
                .then_inc(k.sem("rows_in"), 16)

    def tensor(self, pe):
        k = self.k
        pe.wait_ge(k.sem("const_in"), 16)
        pe.wait_ge(k.sem("rows_in"), 16 * (len(ROWS) + 1))
        pe.wait_ge(k.sem("cleared"), 1)
        for t in range(NROWT):
            ins = pe.transpose(k.bank[7][:, t * P:(t + 1) * P], self.rows[:, t, :], k.c("ident"))
        ins.then_inc(k.sem("turned"), 1)
        pe.wait_ge(k.sem("silu_ready"), 2)
        for n in range(NADA):
            self.ada(pe, n)
        pe.wait_ge(k.sem("tile_free"), 8)
        for j in range(16):
            ins = pe.matmul(k.bank[7][:, 2 * j:2 * j + 2], self.mod[0:2, j * P:(j + 1) * P], k.c("ident")[0:2, 0:2],
                            start=True, stop=True)
        ins.then_inc(k.sem("modc_done"), 1)
        pe.wait_ge(k.sem("x_scaled"), NCH)
        for d in range(KT):
            if d >= 2:
                pe.wait_ge(k.sem("h_ready"), 2 * (d - 1))
            lat, ctx = k.bank[4 + d % 2], k.bank[6 + d % 2]
            if d == 1:
                pe.wait_ge(k.sem("modc_ready"), 1)
            for t in range(CCH):
                pe.transpose(ctx[:, t * P:(t + 1) * P], self.X[:, t, d * P:(d + 1) * P], k.c("ident"))
            for t in range(LCH):
                ins = pe.transpose(lat[:, t * P:(t + 1) * P], self.X[:, CCH + t, d * P:(d + 1) * P], k.c("ident"))
            ins.then_inc(k.sem("turned"), 1)

    def ada(self, pe, n):
        k = self.k
        k.await_weights(pe, "ada%d" % n)
        if n >= 2:
            pe.wait_ge(k.sem("tile_free"), n - 1)
        w = k.slot("ada%d" % n)
        bank = k.bank[2 * (n % 2)]
        for kt in range(KT):
            pe.matmul(bank[0:2, 0:GW], k.silu_c[:, kt, :], w[:, kt, :], start=(kt == 0), stop=False)
        pe.matmul(bank[0:2, 0:GW], k.c("ones")[0:1, 0:2], self.bada[0:1, n * GW:(n + 1) * GW],
                  start=False, stop=True).then_inc(k.sem("tile_done"), 1)

    def scalar(self, act):
        k = self.k
        act.wait_ge(k.sem("cleared"), 1)
        self.load_rows(act, 1)
        act.wait_ge(k.sem("cols_ready"), 1)
        act.activation(k.silu_c[:, :, 0], k.col("c", 0, 8), ACT.Silu).then_inc(k.sem("silu_ready"), 1)
        act.activation(k.silu_c[:, :, 1], k.col("c_ctx", 0, 8), ACT.Silu).then_inc(k.sem("silu_ready"), 1)
        self.mod_rows(act, 0, NADA // 2)
        act.wait_ge(k.sem("x_in"), 32)
        for t in range(NCH):
            if t:
                act.wait_ge(k.sem("squared"), t)
            act.activation(self.sq, self.X[:, t, :], ACT.Square, accum_out=self.ss[:, t:t + 1]).then_inc(k.sem("squared"), 1)
        act.wait_ge(k.sem("variance"), 1)
        act.activation(self.rs, self.ss, ACT.Sqrt).then_inc(k.sem("root"), 1)
        self.mod_rows(act, NADA // 2, NADA)

    def mod_rows(self, act, lo, hi):
        k = self.k
        for n in range(lo, hi):
            act.wait_ge(k.sem("tile_done"), n + 1)
            act.activation(self.mod[0:2, n * GW:(n + 1) * GW], k.bank[2 * (n % 2)][0:2, 0:GW], ACT.Copy).then_inc(k.sem("tile_free"), 1)

    def vector(self, dve, link):
        k = self.k
        dve.wait_ge(k.sem("turned"), 1)
        dve.tensor_copy(k.cols, k.bank[7][:, 0:NROWT * P].rearrange("p (a b) -> p a b", a=NROWT)).then_inc(k.sem("cols_ready"), 1)
        dve.wait_ge(k.sem("squared"), NCH)
        dve.tensor_scalar(self.ss, self.ss, 1.0 / D, 1e-6, ALU.mult, ALU.add).then_inc(k.sem("variance"), 1)
        dve.wait_ge(k.sem("root"), 1)
        link(dve.reciprocal(self.rs, self.rs))
        for t in range(NCH):
            dve.tensor_scalar(self.X[:, t, :], self.X[:, t, :], self.rs[:, t:t + 1], None, ALU.mult).then_inc(k.sem("x_scaled"), 1)
        dve.wait_ge(k.sem("cols_ready"), 1)
        dve.wait_ge(k.sem("modc_done"), 1)
        dve.tensor_copy(k.modc, k.bank[7][:, 0:32].rearrange("p (a b) -> p a b", a=16)).then_inc(k.sem("modc_ready"), 1)
        dve.wait_ge(k.sem("modc_ready"), 1)
        link(dve.tensor_scalar(k.modA, k.modc[:, 8:16, :], 1.0, None, ALU.add))
        link(dve.tensor_tensor(k.modA, k.modA, bc(k.col("norm1_g", 0, 8).unsqueeze(2), [P, 8, 2]), ALU.mult))
        for d in range(KT):
            dve.wait_ge(k.sem("turned"), TURNED["x"] + d + 1)
            dve.tensor_scalar(k.hT[:, d, 0:CTX], k.bank[6 + d % 2][:, 0:CTX], k.modA[:, d, 1:2], k.modc[:, d, 1:2],
                              ALU.mult, ALU.add).then_inc(k.sem("h_ready"), 1)
            dve.tensor_scalar(k.hT[:, d, CTX:TOK], k.bank[4 + d % 2], k.modA[:, d, 0:1], k.modc[:, d, 0:1],
                              ALU.mult, ALU.add).then_inc(k.sem("h_ready"), 1)

    def gpsimd(self, pool):
        k = self.k
        pool.memset(self.rows, 0.0).then_inc(k.sem("cleared"), 1)
        pool.memset(k.zeros, 0.0).then_inc(k.sem("cleared"), 1)


def project(k, pe, name, j, ctx, w=P):
    T = TILE0[name] + j
    if j == 0:
        k.await_weights(pe, name)
    pe.wait_ge(k.sem("tile_free"), T - 1)
    wt = k.slot(name)
    lat, cb = k.bank[2 * (T % 2)], k.bank[2 * (T % 2) + 1]
    for kt in range(KT):
        lhs = wt[:, kt, j * P:(j + 1) * P]
        if ctx:
            pe.matmul(cb[:, 0:CTX], lhs, k.hT[:, kt, 0:CTX], start=(kt == 0), stop=(kt == KT - 1))
        last = pe.matmul(lat[:, 0:LAT], lhs, k.hT[:, kt, CTX:TOK], start=(kt == 0), stop=(kt == KT - 1))
    last.then_inc(k.sem("tile_done"), 1)


def tile_banks(k, name, j):
    T = TILE0[name] + j
    return T, k.bank[2 * (T % 2)], k.bank[2 * (T % 2) + 1]


def mix_count(name, j):
    return TILE0[name] + j - TILE0["lora0"] - (NADA if name[-1] == "1" and name[0] in "rkv" else 0)


RAWW = 1 + CTX + 1 + LAT + 1
RAW_C, RAW_L = 1, 2 + CTX


def span(at, n):
    return slice(at, at + n) if isinstance(at, int) else bass.ds(at, n)


class Stage2:
    def __init__(self, k):
        self.k = k
        a = k.region()
        self.R = a.take(HT, LAT)
        self.KK = a.take(HT, TOK)
        self.B = [a.take(HT, TOK) for d in range(2)]
        self.KD = [a.take(HT, TOK) for d in range(2)]
        self.C = [a.take(HT, NCH * (P + 1)) for d in range(2)]
        self.V = a.take(NCH, BW)
        self.bonus = a.take(LCH, 8)
        self.row = a.take(GW)
        self.wlo, self.alo, self.glo = a.take(TOK), a.take(TOK), a.take(LAT)
        self.w2, self.a2, self.g2 = a.take(2, HALF), a.take(2, HALF), a.take(BW)
        self.mu0 = a.take(15)
        self.kac = a.take(4)
        self.Y = k.Ar.rearrange("p a b -> p (a b)").rearrange("p (a b) -> p a b", a=LCH)
        at = a.at
        self.st = []
        for d in range(2):
            s = {}
            if d == 0:
                at = a.at
            s["S0"] = a.take(HT, HS)
            s["ee"], s["fm"], s["ef"] = a.take(HT, 1), a.take(HT, 1), a.take(HT, 1)
            s["E"], s["F"] = a.take(HT, P + 1), a.take(HT, P + 1)
            s["ARall"] = a.take(HT * 2, 2, P)
            s["AR"] = s["ARall"].rearrange("p (j q) a t -> p j q a t", q=2)
            s["beta"], s["kappa"] = a.take(HT, P), a.take(HT, P)
            s["Vc"] = a.take(HALF)
            s["tok"] = a.take(2, HALF)
            s["LR"], s["MK"] = a.take(GH, 2, P), a.take(GH, 2, P)
            s["X"], s["XT"], s["T1"] = a.take(GH, P), a.take(GH, P), a.take(GH, P)
            s["rhs"], s["U"] = a.take(HALF), a.take(HALF)
            self.st.append(s)
        b = Arena(k.sb, at, a.at)
        self.K, self.VT, self.SQ = b.take(HT, TOK), b.take(HT, TOK), b.take(HT, TOK)
        self.lw, self.at = b.take(2, TOK), b.take(2, TOK)
        self.cs = b.take(2, TOK)
        self.raw = b.take(2, RAWW)
        b = Arena(k.sb, at, a.at)
        self.Z, self.Z2 = b.take(LCH, BW), b.take(LCH, BW)
        self.gng, self.gnb = b.take(BW), b.take(BW)
        self.mean, self.rstd = b.take(LCH, 8), b.take(LCH, 8)

    def loops_done(self, eng, g):
        for d in range(2):
            eng.wait_ge(self.k.sem("state_new%d" % d), (NCH + 1) * g)

    def chunk_loops(self, eng, body):
        body(0, False, 1, False)
        body(1, False, 2, True)
        with eng.Fori(CCH, NCH - 1) as i:
            body(i, True, i + 1, True)
        body(NCH - 1, True, None, True)

    def await_state(self, eng, d, g, i):
        eng.wait_ge(self.k.sem("state_new%d" % d), (NCH + 1) * g + 1 + i)

    def gpsimd(self, pool):
        k = self.k
        pool.wait_ge(k.sem("h_ready"), 2 * KT)
        pool.dma_start(self.g2, k.ins["rwkv_g2"][0]).then_inc(k.sem("lora_w_in"), 16)
        pool.memset(self.w2, 0.0).then_inc(k.sem("cleared"), 1)
        pool.memset(self.a2, 0.0).then_inc(k.sem("cleared"), 1)
        pool.wait_ge(k.sem("cleared"), CLEARED["lora"] + 2)
        for g in range(2):
            if g:
                self.loops_done(pool, g)
            for w, name in ((self.w2, "rwkv_w2"), (self.a2, "rwkv_a2")):
                for d in range(2):
                    pool.dma_start(w[HS * d:HS * d + HS, d, :], k.ins[name][0, d, :, g * HALF:(g + 1) * HALF])\
                        .then_inc(k.sem("lora_w_in"), 16)
            for s in range(2):
                pool.memset(self.raw[:, s, 0:1], 0.0)
                pool.memset(self.raw[:, s, RAW_L - 1:RAW_L], 0.0)
                ins = pool.memset(self.raw[:, s, RAWW - 1:RAWW], 0.0)
            ins.then_inc(k.sem("cleared"), 1)
            pool.wait_ge(k.sem("unit_used"), 4 * (g + 1))
            for lat in (False, True):
                with pool.Fori(CCH * lat, CCH + LCH * lat) as i:
                    for d in range(2):
                        self.await_state(pool, d, g, i)
                        ch = self.chunk(d, i, lat)
                        pool.tensor_copy(self.st[d]["Vc"].unsqueeze(1),
                                         self.V[:, bass.ds(ch, 1), g * HALF:(g + 1) * HALF]).then_inc(k.sem("v_chunk%d" % d), 1)
        self.loops_done(pool, 2)
        pool.dma_start(self.gng, k.ins["rwkv_gn_g"].to_broadcast([P, BW])).then_inc(k.sem("gn_in"), 16)
        pool.dma_start(self.gnb, k.ins["rwkv_gn_b"].to_broadcast([P, BW])).then_inc(k.sem("gn_in"), 16)

    def chunk(self, d, i, lat):
        return i if d == 0 else i * -1 + (NCH + CCH - 1 if lat else CCH - 1)

    def tensor(self, pe):
        k = self.k
        for g in range(2):
            if g:
                self.loops_done(pe, g)
            else:
                pe.wait_ge(k.sem("h_ready"), 2 * KT)
                project(k, pe, "lora0", 0, True)
                project(k, pe, "lora0", 1, True)
                project(k, pe, "lora1", 0, False)
            for j in range(HT):
                project(k, pe, "r%d" % g, j, False)
            for n in "kv":
                for j in range(HT):
                    project(k, pe, n + str(g), j, True)
            pe.wait_ge(k.sem("tile_free"), TILE0["v%d" % g] + HT)
            for m in range(3):
                self.ada(pe, g, m, 3)
            for j in range(HT):
                pe.wait_ge(k.sem("kk_squared"), HT * g + j + 1)
                pe.matmul(k.bank[4 + 2 * j][:, 0:CTX], k.c("bones"), self.SQ[:, j, 0:CTX], start=True, stop=True)
                pe.matmul(k.bank[5 + 2 * j], k.c("bones"), self.SQ[:, j, CTX:TOK], start=True,
                          stop=True).then_inc(k.sem("kk_summed"), 1)
            pe.wait_ge(k.sem("mixed"), mix_count("v%d" % g, HT))
            for t in range(NCH):
                for j in range(HT):
                    ins = pe.transpose(k.bank[t // 2][:, (t % 2) * HALF + j * P:(t % 2) * HALF + (j + 1) * P],
                                       self.VT[:, j, t * P:(t + 1) * P], k.c("ident"))
                if t % 2:
                    ins.then_inc(k.sem("turned"), 1)
            pe.wait_ge(k.sem("rk_ready"), HT * (g + 1))
            pe.wait_ge(k.sem("tile_free"), TILE0["ada%d" % (NADA * (g + 1))] + 3)
            for c in range(LCH):
                for j in range(HT):
                    o = (c * HT + j) * 2
                    ins = pe.matmul(k.bank[3][:, o:o + 2], self.SQ[:, j, CTX + c * P:CTX + (c + 1) * P], k.c("head2"),
                                    start=True, stop=True)
            ins.then_inc(k.sem("bonus_done"), 1)
            pe.wait_ge(k.sem("lora_w_in"), 16 + 64 * (g + 1))
            pe.wait_ge(k.sem("lora_ready"), 1)
            for q in range(8):
                d, j, isa = q // 4, q // 2 % 2, q % 2
                if q < 2:
                    pe.wait_ge(k.sem("variance"), NORM["kk"] + HT * g + q + 1)
                else:
                    pe.wait_ge(k.sem("unit_half"), 8 * g + q - 1)
                w, src = (self.a2, self.alo) if isa else (self.w2, self.wlo)
                wd = w[:, d, j * P:(j + 1) * P]
                pe.matmul(k.bank[4 + 2 * (q % 2)][:, 0:CTX], wd, src[:, 0:CTX], start=True, stop=True)
                pe.matmul(k.bank[5 + 2 * (q % 2)], wd, src[:, CTX:TOK], start=True, stop=True).then_inc(k.sem("unit_mm"), 1)
                if 1 <= q < NADA - 2:
                    if q == 1:
                        pe.wait_ge(k.sem("v_copied"), 3 * g + 1)
                    self.ada(pe, g, q + 2, 0)
            pe.wait_ge(k.sem("v_copied"), 3 * (g + 1))
            pe.wait_ge(k.sem("tile_free"), TILE0["ada%d" % (NADA * (g + 1))] + NADA)
            pe.wait_ge(k.sem("bonus_copied"), g + 1)
            pe.wait_ge(k.sem("unit_half"), 8 * (g + 1))
            self.chunk_loops(pe, lambda i, lat, nxt, nlat: self.chunk_tensor(pe, g, i, lat))
        pe.wait_ge(k.sem("lora_ready"), 2)
        self.loops_done(pe, 2)
        for c in range(LCH):
            pe.matmul(k.bank[4 + c], self.glo[:, c * P:(c + 1) * P], self.g2, start=True, stop=True).then_inc(k.sem("gates_done"), 1)
        for j in range(2):
            project(k, pe, "cval0", j, False)
        for j in range(BT):
            pe.wait_ge(k.sem("z_ready"), LCH)
            for c in range(LCH):
                ins = pe.transpose(k.bank[4 + j][:, c * P:(c + 1) * P], self.Z[:, c, j * P:(j + 1) * P], k.c("ident"))
            ins.then_inc(k.sem("turned"), 1)

    def ada(self, pe, g, m, bank):
        k = self.k
        name = "ada%d" % (NADA * (g + 1) + m)
        T = TILE0[name]
        k.await_weights(pe, name)
        pe.wait_ge(k.sem("tile_free"), T)
        for kt in range(KT):
            ins = pe.matmul(k.bank[bank][0:1, 0:GW], k.silu_c[:, kt, 0:1], k.slot(name)[:, kt, :], start=(kt == 0),
                            stop=(kt == KT - 1))
        ins.then_inc(k.sem("tile_done"), 1)

    def ada_out(self, act, g, m, bank):
        k = self.k
        n = NADA * (g + 1) + m
        act.wait_ge(k.sem("tile_done"), TILE0["ada%d" % n] + 1)
        if n > NADA:
            act.wait_ge(k.sem("mod_out"), 16 * (n - NADA))
        act.activation(self.row[0:1, :], k.bank[bank][0:1, 0:GW], ACT.Copy).then_inc(k.sem("tile_free"), 1)
        act.wait_ge(k.sem("tile_free"), TILE0["ada%d" % n] + 1)
        act.dma_start(k.mod_dram[:, n * GW:(n + 1) * GW], self.row[0:1, :]).then_inc(k.sem("mod_out"), 16)

    def score_count(self, g, i, lat):
        return 4 * (NCH * g + i)

    def chunk_tensor(self, pe, g, i, lat):
        k = self.k
        it = NCH * g + i
        n = 2 if lat else 1
        sc = self.score_count(g, i, lat)
        banks = [k.bank[4 * d:4 * d + 4] for d in range(2)]
        for d in range(2):
            s = self.st[d]
            pe.wait_ge(k.sem("chunk_ops"), 2 * it + d + 1)
            if lat:
                pe.wait_ge(k.sem("rho_made"), 2 * (LCH * g + i - CCH) + d + 1)
            self.await_state(pe, d, g, i)
            pe.wait_ge(k.sem("y_added%d" % d), LCH * g + 1 + (i - CCH if lat else 0))
            for lhs, b0 in ((s["beta"], 0), (s["kappa"], 2)):
                for j in range(HT):
                    pe.matmul(banks[d][b0 + j][:, 0:2 * n * P].rearrange("p (q a t) -> p q a t", q=2, a=n),
                              lhs[:, j, :], s["AR"][:, j, :, 0:n, :], start=True, stop=True)\
                        .then_inc(k.sem("scores%d" % d), 1)
        for d in range(2):
            s = self.st[d]
            pe.wait_ge(k.sem("scores_kept%d" % d), sc + 1)
            for a, x in enumerate((s["beta"], s["kappa"])):
                for j in range(HT):
                    ins = pe.transpose(banks[d][0][:, a * HALF + j * P:a * HALF + (j + 1) * P], x[:, j, :], k.c("ident"))
            ins.then_inc(k.sem("tok_done"), 1)
        for d in range(2):
            s = self.st[d]
            pe.wait_ge(k.sem("tok_copied"), 2 * it + d + 1)
            pe.wait_ge(k.sem("scores_kept%d" % d), sc + 4)
            pe.wait_ge(k.sem("v_chunk%d" % d), it + 1)
            for h in range(GH):
                o = banks[d][0][:, h * HS:(h + 1) * HS]
                pe.matmul(o, s["ARall"][:, h, 0, :], s["S0"][:, h // 2, :], start=True, stop=False)
                ins = pe.matmul(o, s["MK"][:, h, 0, :], s["Vc"][:, h * HS:(h + 1) * HS], start=False, stop=True)
            ins.then_inc(k.sem("rhs_done"), 1)
        for d in range(2):
            s = self.st[d]
            pe.wait_ge(k.sem("lx_kept%d" % d), 7 * it + 1)
            for h in range(GH):
                pe.matmul(banks[d][2][:, h * P:(h + 1) * P], s["XT"][:, h, :], k.c("ident"), start=(h == 0),
                          stop=False, skip_group_check=True)
            pe.matmul(banks[d][3].rearrange("p (a b) -> p a b", a=GH), k.c("ident"), s["XT"], start=True,
                      stop=False, skip_group_check=True).then_inc(k.sem("x_done%d" % d), 1)
        for l in range(1, 7):
            for d in range(2):
                s = self.st[d]
                pe.wait_ge(k.sem("x_copied%d" % d), 7 * it + l)
                if l == 1:
                    pe.wait_ge(k.sem("rhs_copied"), 2 * it + d + 1)
                for h in range(GH):
                    ins = pe.matmul(banks[d][1][:, h * P:(h + 1) * P], s["LR"][:, h, 0, :],
                                    s["X"][:, h, :], start=True, stop=True)
                ins.then_inc(k.sem("lx_done%d" % d), 1)
            for d in range(2):
                s = self.st[d]
                pe.wait_ge(k.sem("lx_kept%d" % d), 7 * it + l + 1)
                for h in range(GH):
                    xt = s["XT"][:, h, :]
                    if l < 6:
                        pe.matmul(banks[d][2][:, h * P:(h + 1) * P], xt, s["T1"][:, h, :], start=False, stop=False,
                                  skip_group_check=True)
                    ins = pe.matmul(banks[d][3][:, h * P:(h + 1) * P], s["T1"][:, h, :], xt, start=False,
                                    stop=(l == 6), skip_group_check=True)
                ins.then_inc(k.sem("x_done%d" % d), 1)
        for d in range(2):
            s = self.st[d]
            pe.wait_ge(k.sem("x_copied%d" % d), 7 * it + 7)
            for h in range(GH):
                ins = pe.matmul(banks[d][0][:, h * HS:(h + 1) * HS], s["XT"][:, h, :], s["rhs"][:, h * HS:(h + 1) * HS],
                                start=True, stop=True)
            ins.then_inc(k.sem("u_done"), 1)
        for d in range(2):
            s = self.st[d]
            pe.wait_ge(k.sem("u_copied"), 2 * it + d + 1)
            if lat:
                for h in range(GH):
                    o, hv = banks[d][1][:, h * HS:(h + 1) * HS], slice(h * HS, (h + 1) * HS)
                    pe.matmul(o, s["ARall"][:, h, 1, :], s["S0"][:, h // 2, :], start=True, stop=False)
                    pe.matmul(o, s["LR"][:, h, 1, :], s["U"][:, hv], start=False, stop=False)
                    ins = pe.matmul(o, s["MK"][:, h, 1, :], s["Vc"][:, hv], start=False, stop=True)
                ins.then_inc(k.sem("y_done"), 1)
            for j in range(HT):
                for x, (a, v) in enumerate(((0, s["U"]), (1, s["Vc"]))):
                    for par in range(2):
                        hv = slice((2 * j + par) * HS, (2 * j + par + 1) * HS)
                        ins = pe.matmul(banks[d][0][HS * par:HS * par + HS, j * HS:(j + 1) * HS], s["tok"][:, a, hv], v[:, hv],
                                        start=(x == 0), stop=(x == 1))
            ins.then_inc(k.sem("state_grown"), 1)

    def scalar(self, act):
        k = self.k
        act.wait_ge(k.sem("h_ready"), 2 * KT)
        for g in range(2):
            if g:
                self.loops_done(act, g)
            act.wait_ge(k.sem("cleared"), CLEARED["raw"] + g + 1)
            tiles = ([("lora0", 0, 1), ("lora0", 1, 1), ("lora1", 0, 0)] if g == 0 else [])
            tiles += [("r%d" % g, j, 0) for j in range(HT)] + [(n + str(g), j, 1) for n in "kv" for j in range(HT)]
            for name, j, ctx in tiles:
                T, lat, cb = tile_banks(k, name, j)
                n = mix_count(name, j)
                act.wait_ge(k.sem("tile_done"), T + 1)
                if n >= 2:
                    act.wait_ge(k.sem("mixed"), n - 1)
                raw = self.raw[:, n % 2, :]
                if ctx:
                    act.activation(raw[:, RAW_C:RAW_C + CTX], cb[:, 0:CTX], ACT.Copy)
                act.activation(raw[:, RAW_L:RAW_L + LAT], lat, ACT.Copy).then_inc(k.sem("tile_free"), 1)
            for m in range(3):
                self.ada_out(act, g, m, 3)
            if g == 0:
                act.wait_ge(k.sem("mixed"), 3)
                act.activation(self.wlo, self.wlo, ACT.Tanh).then_inc(k.sem("lora_ready"), 1)
                act.activation(self.glo, self.glo, ACT.Sigmoid).then_inc(k.sem("lora_ready"), 1)
            for j in range(HT):
                act.wait_ge(k.sem("variance"), NORM["kk"] + HT * g + j + 1)
                act.activation(self.cs[:, j, :], self.cs[:, j, :], ACT.Sqrt).then_inc(k.sem("root"), 1)
            for t in range(3):
                act.wait_ge(k.sem("turned"), TURNED["v"] + 3 * g + t + 1)
                act.activation(self.V[:, 2 * t:2 * t + 2, g * HALF:(g + 1) * HALF],
                               k.bank[t].rearrange("p (a b) -> p a b", a=2), ACT.Copy).then_inc(k.sem("v_copied"), 1)
            for q in range(8):
                d, j, isa = q // 4, q // 2 % 2, q % 2
                act.wait_ge(k.sem("unit_mm"), 8 * g + q + 1)
                if q >= 4:
                    act.wait_ge(k.sem("unit_used"), 4 * g + q // 2 - 1)
                dst = (self.at if isa else self.lw)[:, q // 2 % 2, :]
                bias = k.col("rwkv_a0" if isa else "rwkv_w0", 4 * d + HT * g + j)
                act.activation(dst[:, 0:CTX], k.bank[4 + 2 * (q % 2)][:, 0:CTX], ACT.Sigmoid, bias=bias)
                act.activation(dst[:, CTX:TOK], k.bank[5 + 2 * (q % 2)], ACT.Sigmoid, bias=bias).then_inc(k.sem("unit_half"), 1)
                if 1 <= q < NADA - 2:
                    self.ada_out(act, g, q + 2, 0)
            act.wait_ge(k.sem("unit_used"), 4 * (g + 1))
            for d in range(2):
                self.exps(act, d, g, 0, False)
            self.chunk_loops(act, lambda i, lat, nxt, nlat: self.chunk_scalar(act, g, i, lat, nxt, nlat))
        act.wait_ge(k.sem("variance"), NORM["gn"] + 1)
        rstd = self.rstd.rearrange("p a b -> p (a b)")
        act.activation(rstd, rstd, ACT.Sqrt).then_inc(k.sem("root"), 1)
        for j in range(BT):
            act.wait_ge(k.sem("turned"), TURNED["z"] + j + 1)
            act.activation(k.Ar[:, j, :], k.bank[4 + j], ACT.Copy).then_inc(k.sem("rwkv_out"), 1)

    def exps(self, act, d, g, i, lat):
        s = self.st[d]
        src = self.C[d][:, :, span((P + 1) * self.chunk(d, i, lat), P + 1)]
        act.activation(s["E"], src, ACT.Exp).then_inc(self.k.sem("exps"), 1)
        act.activation(s["F"], src, ACT.Exp, scale=-1.0).then_inc(self.k.sem("exps"), 1)

    def chunk_scalar(self, act, g, i, lat, nxt, nlat):
        k = self.k
        it = NCH * g + i
        for d in range(2):
            s = self.st[d]
            act.wait_ge(k.sem("tok_done"), 2 * it + d + 1)
            act.activation(s["tok"].rearrange("p a b -> p (a b)"), k.bank[4 * d], ACT.Copy).then_inc(k.sem("tok_copied"), 1)
        for d in range(2):
            s = self.st[d]
            act.wait_ge(k.sem("rhs_done"), 2 * it + d + 1)
            act.activation(s["rhs"], k.bank[4 * d][:, 0:HALF], ACT.Copy).then_inc(k.sem("rhs_copied"), 1)
        for l in range(7):
            for d in range(2):
                s = self.st[d]
                act.wait_ge(k.sem("x_done%d" % d), 7 * it + l + 1)
                if l < 6:
                    ins = act.activation(s["X"], k.bank[4 * d + 2].rearrange("p (a b) -> p a b", a=GH), ACT.Copy)
                if l:
                    ins = act.activation(s["XT"], k.bank[4 * d + 3].rearrange("p (a b) -> p a b", a=GH), ACT.Copy)
                ins.then_inc(k.sem("x_copied%d" % d), 1)
            if l == 0 and nxt is not None:
                for d in range(2):
                    act.wait_ge(k.sem("chunk_ops"), 2 * it + d + 1)
                    if lat:
                        act.wait_ge(k.sem("rho_made"), 2 * (LCH * g + i - CCH) + d + 1)
                    self.exps(act, d, g, nxt, nlat)
            if l == 1:
                for d in range(2):
                    s = self.st[d]
                    self.await_state(act, d, g, i)
                    end = (P + 1) * self.chunk(d, i, lat) + (P if d == 0 else 0)
                    mid = (P + 1) * (self.chunk(d, i, lat) if nxt is None else self.chunk(d, nxt, nlat)) + P * d
                    act.activation(s["ee"], self.C[d][:, :, span(end, 1)], ACT.Exp).then_inc(k.sem("ends"), 1)
                    act.activation(s["fm"], self.C[d][:, :, span(mid, 1)], ACT.Exp, scale=-1.0).then_inc(k.sem("ends"), 1)
        for d in range(2):
            s = self.st[d]
            act.wait_ge(k.sem("u_done"), 2 * it + d + 1)
            act.activation(s["U"], k.bank[4 * d][:, 0:HALF], ACT.Copy, scale=-1.0).then_inc(k.sem("u_copied"), 1)

    def mix(self, dve, link, name, j, mu, dst_ctx, dst_lat):
        k = self.k
        T = TILE0[name] + j
        n = mix_count(name, j)
        raw = self.raw[:, n % 2, :]
        dve.wait_ge(k.sem("tile_free"), T + 1)
        parts = ([(dst_ctx, RAW_C, CTX)] if dst_ctx is not None else []) + [(dst_lat, RAW_L, LAT)]
        for dst, o, w in parts:
            link.step(dve.tensor_scalar(dst, raw[:, o:o + w], self.mu0[:, mu:mu + 1], None, ALU.mult))
        link.wait()
        for dst, o, w in parts:
            link.step(dve.scalar_tensor_tensor(dst, raw[:, o - 1:o - 1 + w], k.col("rwkv_mu_prev", mu), dst, ALU.mult, ALU.add))
        link.wait()
        for dst, o, w in parts:
            ins = dve.scalar_tensor_tensor(dst, raw[:, o + 1:o + 1 + w], k.col("rwkv_mu_next", mu), dst, ALU.mult, ALU.add)
            if o == RAW_C:
                link.step(ins)
        ins.then_inc(k.sem("mixed"), 1)
        link.wait()
        dve.wait_ge(k.sem("mixed"), n + 1)

    def vector(self, dve, link):
        k = self.k
        dve.wait_ge(k.sem("h_ready"), 2 * KT)
        link(dve.tensor_tensor(self.mu0, k.col("rwkv_mu_prev", 0, 15), k.col("rwkv_mu_next", 0, 15), ALU.add))
        link(dve.tensor_scalar(self.mu0, self.mu0, -1.0, 1.0, ALU.mult, ALU.add))
        link(dve.tensor_scalar(self.kac, k.col("rwkv_k_a", 0, 4), -1.0, 1.0, ALU.mult, ALU.add))
        for d in range(2):
            dve.memset(self.Y[:, d * HT:(d + 1) * HT, :], 0.0).then_inc(k.sem("y_added%d" % d), 1)
        for g in range(2):
            if g == 0:
                self.mix(dve, link, "lora0", 0, 12, self.wlo[:, 0:CTX], self.wlo[:, CTX:TOK])
                self.mix(dve, link, "lora0", 1, 13, self.alo[:, 0:CTX], self.alo[:, CTX:TOK])
                self.mix(dve, link, "lora1", 0, 14, None, self.glo)
            for j in range(HT):
                self.mix(dve, link, "r%d" % g, j, HT * g + j, None, self.R[:, j, :])
            for j in range(HT):
                self.mix(dve, link, "k%d" % g, j, 4 + HT * g + j, self.K[:, j, 0:CTX], self.K[:, j, CTX:TOK])
            for j in range(HT):
                self.mix(dve, link, "v%d" % g, j, 8 + HT * g + j, self.VT[:, j, 0:CTX], self.VT[:, j, CTX:TOK])
            for j in range(HT):
                link(dve.tensor_scalar(self.KK[:, j, :], self.K[:, j, :], k.col("rwkv_k_k", HT * g + j), None, ALU.mult))
                dve.tensor_tensor(self.SQ[:, j, :], self.KK[:, j, :], self.KK[:, j, :], ALU.mult).then_inc(k.sem("kk_squared"), 1)
            for j in range(HT):
                dve.wait_ge(k.sem("kk_summed"), HT * g + j + 1)
                link.step(dve.tensor_scalar(self.cs[:, j, 0:CTX], k.bank[4 + 2 * j][:, 0:CTX], 1e-12, None, ALU.add))
                dve.tensor_scalar(self.cs[:, j, CTX:TOK], k.bank[5 + 2 * j], 1e-12, None, ALU.add).then_inc(k.sem("variance"), 1)
                dve.scalar_tensor_tensor(self.SQ[:, j, CTX:TOK], self.R[:, j, :], k.col("rwkv_r_k", HT * g + j),
                                         self.K[:, j, CTX:TOK], ALU.mult, ALU.mult).then_inc(k.sem("rk_ready"), 1)
            for j in range(HT):
                dve.wait_ge(k.sem("root"), NORM["kk"] + HT * g + j + 1)
                link(dve.reciprocal(self.cs[:, j, :], self.cs[:, j, :]))
                link(dve.tensor_tensor(self.KK[:, j, :], self.KK[:, j, :], self.cs[:, j, :], ALU.mult))
            dve.wait_ge(k.sem("bonus_done"), g + 1)
            dve.tensor_copy(self.bonus[:, :, GH * g:GH * g + GH],
                            k.bank[3][:, 0:LCH * GH].rearrange("p (a b) -> p a b", a=LCH)).then_inc(k.sem("bonus_copied"), 1)
            for u in range(4):
                d, j = u // 2, u % 2
                lw, a, cs = self.lw[:, u % 2, :], self.at[:, u % 2, :], self.cs[:, u % 2, :]
                dve.wait_ge(k.sem("unit_half"), 8 * g + 2 * u + 1)
                link(dve.tensor_scalar(lw, lw, LOGW, None, ALU.mult))
                back = slice(None, None, -1 if d else 1)
                link(dve.tensor_tensor_scan(cs[:, back], k.c("reset"), lw[:, back], 0.0, ALU.mult, ALU.add))
                cs3 = cs.rearrange("p (c t) -> p c t", t=P)
                mid = cs3[:, :, HS - 1 + d:HS + d]
                C = self.C[d][:, j, :].rearrange("p (c t) -> p c t", t=P + 1)
                dve.tensor_tensor(C[:, :, 1 - d:1 - d + P], cs3, bc(mid, [P, NCH, P]), ALU.subtract)
                dve.tensor_scalar(C[:, :, P * d:P * d + 1], mid, -1.0, None, ALU.mult)
                dve.wait_ge(k.sem("unit_half"), 8 * g + 2 * u + 2)
                dve.tensor_tensor(self.B[d][:, j, :], self.KK[:, j, :], a, ALU.mult)
                link(dve.tensor_scalar(self.KD[d][:, j, :], a, k.col("rwkv_k_a", HT * g + j), self.kac[:, HT * g + j:HT * g + j + 1],
                                       ALU.mult, ALU.add))
                dve.tensor_tensor(self.KD[d][:, j, :], self.KD[d][:, j, :], self.K[:, j, :], ALU.mult).then_inc(k.sem("unit_used"), 1)
            dve.wait_ge(k.sem("unit_used"), 4 * (g + 1))
            for d in range(2):
                link.step(dve.memset(self.st[d]["ARall"], 0.0))
                dve.memset(self.st[d]["S0"], 0.0).then_inc(k.sem("state_new%d" % d), 1)
            link.wait()
            for d in range(2):
                self.operands(dve, d, g, 0, False)
            self.chunk_loops(dve, lambda i, lat, nxt, nlat: self.chunk_vector(dve, g, i, lat, nxt, nlat))
        self.finish(dve, link)

    def operands(self, dve, d, g, i, lat):
        k, s = self.k, self.st[d]
        E, F = s["E"], s["F"]
        dve.wait_ge(k.sem("exps"), 4 * (NCH * g + i) + 2 * d + 2)
        cols = span(P * self.chunk(d, i, lat), P)
        for par in range(2):
            rows = slice(HS * par, HS * par + HS)
            dve.tensor_tensor(s["AR"][rows, :, par, 0, :], self.KK[rows, :, cols], E[rows, :, d:d + P], ALU.mult)
        dve.tensor_tensor(s["beta"], self.B[d][:, :, cols], F[:, :, 1 - d:1 - d + P], ALU.mult)
        dve.tensor_tensor(s["kappa"], self.KD[d][:, :, cols], F[:, :, 1 - d:1 - d + P], ALU.mult).then_inc(k.sem("chunk_ops"), 1)

    def chunk_vector(self, dve, g, i, lat, nxt, nlat):
        k = self.k
        it = NCH * g + i
        sc = self.score_count(g, i, lat)
        n = 2 if lat else 1
        for d in range(2):
            s = self.st[d]
            keep = k.c("keep%d" % d)
            for q in range(4):
                dve.wait_ge(k.sem("scores%d" % d), sc + q + 1)
                dst = s["LR"] if q < 2 else s["MK"]
                dst = dst[:, 2 * (q % 2):2 * (q % 2) + 2, :, :].rearrange("p q a t -> p q (a t)")[:, :, 0:n * P]
                dve.tensor_tensor(dst, k.bank[4 * d + q][:, 0:2 * n * P].rearrange("p (q x) -> p q x", q=2),
                                  bc(keep[:, 0:n * P].unsqueeze(1), [P, 2, n * P]), ALU.mult).then_inc(k.sem("scores_kept%d" % d), 1)
        for d in range(2):
            s = self.st[d]
            dve.wait_ge(k.sem("scores_kept%d" % d), sc + 2)
            dve.tensor_tensor(s["XT"], s["LR"][:, :, 0, :], bc(k.c("lev0").unsqueeze(1), [P, GH, P]),
                              ALU.mult).then_inc(k.sem("xt_part"), 1)
            dve.wait_ge(k.sem("xt_part"), 2 * it + d + 1)
            dve.tensor_tensor(s["XT"], s["XT"], bc(k.c("ident").unsqueeze(1), [P, GH, P]), ALU.add)\
                .then_inc(k.sem("lx_kept%d" % d), 1)
        for l in range(1, 7):
            for d in range(2):
                s = self.st[d]
                dve.wait_ge(k.sem("lx_done%d" % d), 6 * it + l)
                dve.tensor_tensor(s["T1"], k.bank[4 * d + 1].rearrange("p (a b) -> p a b", a=GH),
                                  bc(k.c("lev%d" % l).unsqueeze(1), [P, GH, P]), ALU.mult).then_inc(k.sem("lx_kept%d" % d), 1)
            if l == 1 and nxt is not None:
                dve.wait_ge(k.sem("tok_done"), 2 * it + 2)
                dve.wait_ge(k.sem("rhs_done"), 2 * it + 2)
                for d in range(2):
                    self.operands(dve, d, g, nxt, nlat)
        for d in range(2):
            s = self.st[d]
            if lat:
                dve.wait_ge(k.sem("y_done"), 2 * (LCH * g + i - CCH) + d + 1)
                dve.wait_ge(k.sem("y_added%d" % (1 - d)), LCH * g + 1 + i - CCH)
                dve.wait_ge(k.sem("y_added%d" % d), LCH * g + 1 + i - CCH)
                y = self.Y[:, span(self.chunk(d, i, lat) - CCH, 1), g * HALF:(g + 1) * HALF]
                dve.tensor_tensor(y, y, k.bank[4 * d + 1][:, 0:HALF].unsqueeze(1), ALU.add).then_inc(k.sem("y_added%d" % d), 1)
            if nlat and nxt is not None:
                cols = span(P * (self.chunk(d, nxt, True) - CCH), P)
                for par in range(2):
                    rows = slice(HS * par, HS * par + HS)
                    ins = dve.tensor_tensor(s["AR"][rows, :, par, 1, :], self.R[rows, :, cols],
                                            s["E"][rows, :, 1 - d:1 - d + P], ALU.mult)
                ins.then_inc(k.sem("rho_made"), 1)
            dve.wait_ge(k.sem("ends"), 4 * it + 2 * d + 2)
            dve.tensor_tensor(s["ef"], s["ee"], s["fm"], ALU.mult).then_inc(k.sem("state_sum"), 1)
            dve.wait_ge(k.sem("state_grown"), 2 * it + d + 1)
            dve.tensor_tensor(s["S0"], s["S0"], k.bank[4 * d][:, 0:HT * HS].rearrange("p (a b) -> p a b", a=HT),
                              ALU.add).then_inc(k.sem("state_sum"), 1)
            dve.wait_ge(k.sem("state_sum"), 4 * it + 2 * d + 2)
            dve.tensor_tensor(s["S0"], s["S0"], bc(s["ef"], [P, HT, HS]), ALU.mult).then_inc(k.sem("state_new%d" % d), 1)

    def finish(self, dve, link):
        k = self.k
        y4 = self.Y.rearrange("p c (h v) -> p (c h) v", v=HS)
        z4 = self.Z.rearrange("p c (h v) -> p (c h) v", v=HS)
        q4 = self.Z2.rearrange("p c (h v) -> p (c h) v", v=HS)
        v4 = self.V[:, CCH:NCH, :].rearrange("p c (h v) -> p (c h) v", v=HS)
        NH = LCH * 8
        flat = lambda x: x.rearrange("p a b -> p (a b)")
        wide = lambda x: bc(flat(x).unsqueeze(2), [P, NH, HS])
        for d in range(2):
            dve.wait_ge(k.sem("y_added%d" % d), 2 * LCH + 1)
        self.loops_done(dve, 2)
        link(dve.tensor_reduce(flat(self.mean), y4, AX, ALU.add))
        link(dve.tensor_scalar(flat(self.mean), flat(self.mean), 1.0 / HS, None, ALU.mult))
        link(dve.tensor_tensor(z4, y4, wide(self.mean), ALU.subtract))
        link(dve.tensor_tensor(q4, z4, z4, ALU.mult))
        link(dve.tensor_reduce(flat(self.rstd), q4, AX, ALU.add))
        dve.tensor_scalar(flat(self.rstd), flat(self.rstd), 1.0 / HS, 64e-5, ALU.mult, ALU.add).then_inc(k.sem("variance"), 1)
        dve.wait_ge(k.sem("root"), NORM["gn"] + 1)
        link(dve.reciprocal(flat(self.rstd), flat(self.rstd)))
        link(dve.tensor_tensor(z4, z4, wide(self.rstd), ALU.mult))
        dve.wait_ge(k.sem("gn_in"), 32)
        link(dve.tensor_tensor(self.Z, self.Z, bc(self.gng.unsqueeze(1), [P, LCH, BW]), ALU.mult))
        link(dve.tensor_tensor(q4, v4, wide(self.bonus), ALU.mult))
        link(dve.tensor_tensor(self.Z, self.Z, bc(self.gnb.unsqueeze(1), [P, LCH, BW]), ALU.add))
        link(dve.tensor_tensor(self.Z, self.Z, self.Z2, ALU.add))
        for c in range(LCH):
            dve.wait_ge(k.sem("gates_done"), c + 1)
            dve.tensor_tensor(self.Z[:, c, :], self.Z[:, c, :], k.bank[4 + c], ALU.mult).then_inc(k.sem("z_ready"), 1)


UW = LAT + CONV_K - 1
LP = 3
LXW = LP + CTX + LP + LAT + LP
XW = CTX + LP + LAT
XL = CTX + LP
EARLY = 3


class Stage3:
    def __init__(self, k):
        self.k = k
        a = k.region()
        k.Ac, k.Al, k.At = a.take(BT, LAT), a.take(BT, LAT), a.take(BT, LAT)
        k.free3 = a.at
        conv_at = a.at
        self.U, self.acc, self.sq = a.take(BT, UW), a.take(BT, LAT), a.take(BT, LAT)
        self.crs = a.take(LAT)
        lru_at = a.at
        self.LX = a.take(BT, LXW)
        self.xc, self.gr, self.gi, self.a = [a.take(2, XW) for n in range(4)]
        self.tmp = a.take(XW)
        self.WB = a.take(16, P)
        self.lam = a.take(6, 8)
        lru_end = a.at
        self.rt = a.take(LAT)
        self.q, self.kk, self.V = a.take(2, LAT), a.take(2, TOK), a.take(NCH, BW)
        self.att = a.take(2, LAT)
        self.part = a.take(1, LAT)
        self.tab = Arena(k.sb, lru_at, lru_end).take(RCONST.shape[1])
        b = Arena(k.sb, conv_at, lru_at)
        self.qz = b.take(4, LAT)
        b.take(BT * UW - 4 * LAT)
        self.O, self.Osq, self.ors = b.take(2, LAT), b.take(2, LAT), b.take(2, LAT)

    def table(self, name):
        o, n = RAT[name]
        return self.tab[:, o:o + n]

    def gpsimd(self, pool):
        k = self.k
        pool.wait_ge(k.sem("rwkv_out"), BT)
        for j in range(BT):
            for lo, hi in ((0, LP), (LP + CTX, 2 * LP + CTX), (LXW - LP, LXW)):
                ins = pool.memset(self.LX[:, j, lo:hi], 0.0)
        ins.then_inc(k.sem("cleared"), 1)
        for j in range(BT):
            pool.memset(self.U[:, j, 0:CONV_K // 2], 0.0)
            ins = pool.memset(self.U[:, j, UW - CONV_K // 2:UW], 0.0)
        ins.then_inc(k.sem("cleared"), 1)
        pool.memset(self.WB, 0.0).then_inc(k.sem("cleared"), 1)
        pool.wait_ge(k.sem("cleared"), CLEARED["wb"] + 1)
        for w, name in enumerate(("lru_wr", "lru_wi")):
            for half in range(2):
                src = k.ins[name][0].rearrange("d (j q) a b -> q a (d j) b", q=2)[half]
                dst = self.WB[HS * half:HS * half + HS, 8 * w:8 * w + 8, HS * half:HS * half + HS]
                pool.dma_start(dst, src).then_inc(k.sem("wb_in"), 16)
        plink = Chain(pool, k.sem("pool_step"))
        pool.wait_ge(k.sem("cleared"), CLEARED["u"] + 1)
        for j in range(EARLY, BT):
            pool.wait_ge(k.sem("gated"), j + 1)
            for t in range(CONV_K):
                x, w, acc = self.U[:, j, t:t + LAT], k.col("conv_w", t * BT + j), self.acc[:, j, :]
                if t == 0:
                    plink(pool.tensor_scalar(acc, x, w, k.col("conv_b", j), ALU.mult, ALU.add))
                    continue
                plink(pool.tensor_scalar(self.part[:, 0, :], x, w, None, ALU.mult))
                ins = pool.tensor_tensor(acc, acc, self.part[:, 0, :], ALU.add)
                if t < CONV_K - 1:
                    plink(ins)
                else:
                    ins.then_inc(k.sem("conv_share"), 1)
        pool.wait_ge(k.sem("conv_done"), EARLY)
        pool.wait_ge(k.sem("conv_share"), BT - EARLY)
        for h in range(4):
            ins = pool.memset(self.qz[HS * (1 - h % 2):HS * (1 - h % 2) + HS, h, :], 0.0)
        ins.then_inc(k.sem("cleared"), 1)
        pool.wait_ge(k.sem("lru_out"), BT)
        pool.dma_start(self.tab, k.ins["ret_tables"]).then_inc(k.sem("tab_in"), 16)

    TAIL = ([("qk%d" % (n // 2), n % 2) for n in range(4)] + [("rv%d" % (n // NCH), n % NCH) for n in range(2 * NCH)]
            + [("rg%d" % (n // 2), n % 2) for n in range(4)])

    def tensor(self, pe):
        k = self.k
        for h in range(2):
            for name in ("cval", "cgate"):
                for j in range(2):
                    if name + str(h) != "cval0":
                        project(k, pe, name + str(h), j, False)
        for n in range(4):
            project(k, pe, "lx%d" % (n // 2), n % 2, True)
        for n in range(4):
            project(k, pe, "lg%d" % (n // 2), n % 2, False)
        pe.wait_ge(k.sem("rwkv_out"), BT)
        pe.wait_ge(k.sem("wb_in"), 64)
        for n, (name, j) in enumerate(self.TAIL):
            if n % 2 == 0 and n < 16:
                self.gates(pe, n // 2)
            if name[:2] == "rv":
                self.values(pe, name, j)
            else:
                project(k, pe, name, j, name == "qk1")
        pe.wait_ge(k.sem("gate_read"), 16)
        pe.wait_ge(k.sem("conv_done"), EARLY)
        pe.wait_ge(k.sem("conv_share"), BT - EARLY)
        for j in range(BT):
            ins = pe.matmul(k.bank[4], k.c("ones"), self.acc[:, j, :], start=(j == 0), stop=(j == BT - 1))
        ins.then_inc(k.sem("mean_summed"), 1)
        for j in range(BT):
            pe.wait_ge(k.sem("squared"), SQUARED["conv"] + j + 1)
            ins = pe.matmul(k.bank[5], k.c("ones"), self.sq[:, j, :], start=(j == 0), stop=(j == BT - 1))
        ins.then_inc(k.sem("var_summed"), 1)
        pe.wait_ge(k.sem("tab_in"), 16)
        pe.wait_ge(k.sem("tile_free"), TILE0["merge0"])
        for n, x in enumerate((self.q[:, 0, :], self.q[:, 1, :], self.kk[:, 0, CTX:TOK], self.kk[:, 1, CTX:TOK])):
            pe.matmul(k.bank[n], self.table("rot"), x, start=True, stop=True).then_inc(k.sem("rotated"), 1)
        for h in range(4):
            for jt in range(NCH):
                n = h * NCH + jt
                if n == 0:
                    pe.wait_ge(k.sem("rope_done"), 4)
                    pe.wait_ge(k.sem("centred"), BT)
                    pe.wait_ge(k.sem("variance"), NORM["conv"] + 1)
                if n >= 2:
                    pe.wait_ge(k.sem("att_kept"), n - 1)
                pe.matmul(k.bank[4 + n % 2], self.kk[:, h // 2, jt * P:(jt + 1) * P], self.qz[:, h, :],
                          start=True, stop=True).then_inc(k.sem("att_done"), 1)
                if n >= 1:
                    self.att_v(pe, n - 1)
                if h and jt == 2:
                    self.ret_mean(pe, h - 1)
                if h and jt == NCH - 1:
                    self.ret_var(pe, h - 1)
        self.att_v(pe, 4 * NCH - 1)
        self.ret_mean(pe, 3)
        self.ret_var(pe, 3)

    def att_v(self, pe, n):
        k = self.k
        h, jt = n // NCH, n % NCH
        pe.wait_ge(k.sem("att_kept"), n + 1)
        if jt == 0 and h >= 2:
            pe.wait_ge(k.sem("o_copied"), h - 1)
        ins = pe.matmul(k.bank[6 + h % 2], self.V[:, jt, h * P:(h + 1) * P], self.att[:, n % 2, :],
                        start=(jt == 0), stop=(jt == NCH - 1))
        ins.then_inc(k.sem("att_used"), 1)

    def ret_mean(self, pe, h):
        k = self.k
        pe.wait_ge(k.sem("o_copied"), h + 1)
        if h:
            pe.wait_ge(k.sem("variance"), NORM["ret"] + h)
        pe.matmul(k.bank[0], k.c("ones"), self.O[:, h % 2, :], start=True, stop=True).then_inc(k.sem("mean_summed"), 1)

    def ret_var(self, pe, h):
        k = self.k
        pe.wait_ge(k.sem("squared"), SQUARED["ret"] + h + 1)
        pe.matmul(k.bank[1], k.c("ones"), self.Osq[:, h % 2, :], start=True, stop=True).then_inc(k.sem("var_summed"), 1)

    def values(self, pe, name, t):
        k = self.k
        T, lat, _ = tile_banks(k, name, t)
        if t == 0:
            k.await_weights(pe, name)
        pe.wait_ge(k.sem("tile_free"), T - 1)
        for kt in range(KT):
            ins = pe.matmul(lat[:, 0:GW], k.hT[:, kt, t * P:(t + 1) * P], k.slot(name)[:, kt, :], start=(kt == 0),
                            stop=(kt == KT - 1))
        ins.then_inc(k.sem("tile_done"), 1)

    def gates(self, pe, u):
        k = self.k
        j, d = u // 2, u % 2
        pe.wait_ge(k.sem("xc_ready"), u + 1)
        for w in range(2):
            if u:
                pe.wait_ge(k.sem("gate_read"), 2 * u - 1 + w)
            lhs = self.WB[:, 8 * w + 4 * d + j, :]
            pe.matmul(k.bank[5 + 2 * w][:, 0:CTX], lhs, self.xc[:, d, 0:CTX], start=True, stop=True)
            pe.matmul(k.bank[4 + 2 * w], lhs, self.xc[:, d, XL:XW], start=True, stop=True).then_inc(k.sem("gate_mm"), 1)

    def scalar(self, act):
        k = self.k
        act.wait_ge(k.sem("mod_out"), 16 * 2 * NADA)
        act.activation(self.lam[:, 0, :], k.col("lru_lambda", 0, 8), ACT.Abs).then_inc(k.sem("lam_abs"), 1)
        act.wait_ge(k.sem("lam_abs"), 1)
        act.activation(self.lam[:, 1, :], self.lam[:, 0, :], ACT.Exp, scale=-1.0).then_inc(k.sem("lam_exp"), 1)
        act.wait_ge(k.sem("cleared"), CLEARED["u"] + 1)
        act.wait_ge(k.sem("cleared"), CLEARED["lx"] + 1)
        for h in range(2):
            for j in range(2):
                T, lat, _ = tile_banks(k, "cval%d" % h, j)
                act.wait_ge(k.sem("tile_done"), T + 1)
                act.activation(self.U[:, 2 * h + j, CONV_K // 2:CONV_K // 2 + LAT], lat, ACT.Copy).then_inc(k.sem("tile_free"), 1)
            for j in range(2):
                T, lat, _ = tile_banks(k, "cgate%d" % h, j)
                act.wait_ge(k.sem("tile_done"), T + 1)
                act.activation(k.Ac[:, 2 * h + j, :], lat, ACT.Sigmoid).then_inc(k.sem("tile_free"), 1)
        for n in range(4):
            T, lat, cb = tile_banks(k, "lx%d" % (n // 2), n % 2)
            act.wait_ge(k.sem("tile_done"), T + 1)
            act.activation(self.LX[:, n, LP:LP + CTX], cb[:, 0:CTX], ACT.Copy)
            act.activation(self.LX[:, n, 2 * LP + CTX:2 * LP + CTX + LAT], lat, ACT.Copy).then_inc(k.sem("tile_free"), 1)
        for n in range(4):
            T, lat, _ = tile_banks(k, "lg%d" % (n // 2), n % 2)
            act.wait_ge(k.sem("tile_done"), T + 1)
            act.activation(k.Al[:, n, :], lat, ACT.Gelu_apprx_tanh).then_inc(k.sem("tile_free"), 1)
        for n, (name, j) in enumerate(self.TAIL):
            T, lat, cb = tile_banks(k, name, j)
            if n % 2 == 0 and n < 16:
                self.gate_scalar(act, n // 2)
            act.wait_ge(k.sem("tile_done"), T + 1)
            if name[:2] == "rv":
                ins = act.activation(self.V[:, j, int(name[2]) * GW:int(name[2]) * GW + GW], lat[:, 0:GW], ACT.Copy)
            elif name[:2] == "rg":
                ins = act.activation(k.At[:, 2 * int(name[2]) + j, :], lat, ACT.Silu)
            elif name == "qk0":
                ins = act.activation(self.q[:, j, :], lat, ACT.Copy)
            else:
                act.activation(self.kk[:, j, 0:CTX], cb[:, 0:CTX], ACT.Copy, scale=0.125)
                ins = act.activation(self.kk[:, j, CTX:TOK], lat, ACT.Copy, scale=0.125)
            ins.then_inc(k.sem("tile_free"), 1)
        for j in range(BT):
            act.wait_ge(k.sem("centred"), j + 1)
            act.activation(self.sq[:, j, :], self.acc[:, j, :], ACT.Square).then_inc(k.sem("squared"), 1)
        act.wait_ge(k.sem("variance"), NORM["conv"] + 1)
        act.activation(self.crs, self.crs, ACT.Sqrt).then_inc(k.sem("root"), 1)
        for j in range(BT):
            act.wait_ge(k.sem("conv_normed"), j + 1)
            act.activation(k.Ac[:, j, :], self.acc[:, j, :], ACT.Silu, bias=k.col("conv_ln_b", j),
                           scale=k.col("conv_ln_g", j)).then_inc(k.sem("conv_out"), 1)
        act.wait_ge(k.sem("conv_out"), BT)
        for h in range(4):
            act.wait_ge(k.sem("att_used"), NCH * (h + 1))
            if h >= 2:
                act.wait_ge(k.sem("ret_out"), h - 1)
            act.activation(self.O[:, h % 2, :], k.bank[6 + h % 2], ACT.Copy).then_inc(k.sem("o_copied"), 1)
            act.wait_ge(k.sem("centred"), BT + h + 1)
            act.activation(self.Osq[:, h % 2, :], self.O[:, h % 2, :], ACT.Square).then_inc(k.sem("squared"), 1)
            act.wait_ge(k.sem("variance"), NORM["ret"] + h + 1)
            act.activation(self.ors[:, h % 2, :], self.ors[:, h % 2, :], ACT.Sqrt).then_inc(k.sem("root"), 1)

    def gate_scalar(self, act, u):
        k = self.k
        j, d = u // 2, u % 2
        gr, gi, a = self.gr[:, d, :], self.gi[:, d, :], self.a[:, d, :]
        for w, (g, name) in enumerate(((gr, "lru_br"), (gi, "lru_bi"))):
            act.wait_ge(k.sem("gate_mm"), 2 * u + w + 1)
            if u >= 2:
                act.wait_ge(k.sem("lru_out"), j)
            bias = k.col(name, 4 * d + j)
            act.activation(g[:, 0:CTX], k.bank[5 + 2 * w][:, 0:CTX], ACT.Sigmoid, bias=bias)
            act.activation(g[:, XL:XW], k.bank[4 + 2 * w], ACT.Sigmoid, bias=bias).then_inc(k.sem("gate_read"), 1)
        act.wait_ge(k.sem("gate_read"), 2 * u + 2)
        act.wait_ge(k.sem("lam_ready"), 1)
        c = self.lam[:, 4, 4 * d + j:4 * d + j + 1]
        nc_ = self.lam[:, 5, 4 * d + j:4 * d + j + 1]
        act.activation(a[:, 0:CTX], gr[:, 0:CTX], ACT.Exp, scale=c)
        act.activation(a[:, XL:XW], gr[:, XL:XW], ACT.Exp, scale=c).then_inc(k.sem("lru_a"), 1)
        act.activation(gr[:, 0:CTX], gr[:, 0:CTX], ACT.Tanh, scale=nc_)
        act.activation(gr[:, XL:XW], gr[:, XL:XW], ACT.Tanh, scale=nc_).then_inc(k.sem("lru_a"), 1)
        act.wait_ge(k.sem("lru_power"), u + 1)
        act.activation(gr[:, 0:CTX], gr[:, 0:CTX], ACT.Sqrt)
        act.activation(gr[:, XL:XW], gr[:, XL:XW], ACT.Sqrt).then_inc(k.sem("lru_norm"), 1)

    def vector(self, dve, link):
        k = self.k
        lam = self.lam
        dve.wait_ge(k.sem("rwkv_out"), BT)
        dve.wait_ge(k.sem("lam_exp"), 1)
        link(dve.tensor_scalar(lam[:, 2, :], lam[:, 1, :], 2.0, None, ALU.add))
        link(dve.reciprocal(lam[:, 2, :], lam[:, 2, :]))
        link(dve.tensor_tensor(lam[:, 1, :], lam[:, 1, :], lam[:, 2, :], ALU.mult))
        link(dve.tensor_tensor(lam[:, 2, :], lam[:, 1, :], lam[:, 1, :], ALU.mult))
        link(dve.tensor_scalar(lam[:, 3, :], lam[:, 2, :], 1.0 / 19, 1.0 / 17, ALU.mult, ALU.add))
        for n in range(15, 0, -2):
            link(dve.tensor_tensor(lam[:, 3, :], lam[:, 3, :], lam[:, 2, :], ALU.mult))
            link(dve.tensor_scalar(lam[:, 3, :], lam[:, 3, :], 1.0 / n, None, ALU.add))
        link(dve.tensor_tensor(lam[:, 3, :], lam[:, 3, :], lam[:, 1, :], ALU.mult))
        link(dve.tensor_scalar(lam[:, 0, :], k.col("lru_lambda", 0, 8), -1.0, 0.0, ALU.mult, ALU.max))
        link(dve.scalar_tensor_tensor(lam[:, 3, :], lam[:, 3, :], 2.0, lam[:, 0, :], ALU.mult, ALU.add))
        link(dve.tensor_scalar(lam[:, 4, :], lam[:, 3, :], -8.0, None, ALU.mult))
        dve.tensor_scalar(lam[:, 5, :], lam[:, 3, :], 8.0, None, ALU.mult).then_inc(k.sem("lam_ready"), 1)
        dve.wait_ge(k.sem("cleared"), CLEARED["u"] + 1)
        for j in range(BT):
            dve.wait_ge(k.sem("tile_free"), TILE0["cgate%d" % (j // 2)] + j % 2 + 1)
            u = self.U[:, j, CONV_K // 2:CONV_K // 2 + LAT]
            dve.tensor_tensor(u, u, k.Ac[:, j, :], ALU.mult).then_inc(k.sem("gated"), 1)
        for j in range(EARLY):
            dve.wait_ge(k.sem("gated"), j + 1)
            self.conv_taps(dve, link, j)
        dve.wait_ge(k.sem("cleared"), CLEARED["lx"] + 1)
        for u in range(8):
            if u % 2 == 0:
                self.lru_conv(dve, link, u)
                self.lru_conv(dve, link, u + 1)
            self.lru_unit(dve, link, u)
        dve.wait_ge(k.sem("mean_summed"), 1)
        for j in range(BT):
            dve.scalar_tensor_tensor(self.acc[:, j, :], k.bank[4], -1.0 / BW, self.acc[:, j, :], ALU.mult,
                                     ALU.add).then_inc(k.sem("centred"), 1)
        dve.wait_ge(k.sem("var_summed"), 1)
        dve.tensor_scalar(self.crs, k.bank[5], 1.0 / BW, 1e-5, ALU.mult, ALU.add).then_inc(k.sem("variance"), 1)
        dve.wait_ge(k.sem("root"), NORM["conv"] + 1)
        link(dve.reciprocal(self.crs, self.crs))
        for j in range(BT):
            dve.wait_ge(k.sem("squared"), SQUARED["conv"] + j + 1)
            dve.tensor_tensor(self.acc[:, j, :], self.acc[:, j, :], self.crs, ALU.mult).then_inc(k.sem("conv_normed"), 1)
        dve.wait_ge(k.sem("tab_in"), 16)
        for n, x in enumerate((self.q[:, 0, :], self.q[:, 1, :], self.kk[:, 0, CTX:TOK], self.kk[:, 1, CTX:TOK])):
            dve.wait_ge(k.sem("rotated"), n + 1)
            link.step(dve.tensor_tensor(self.rt, k.bank[n], self.table("sin"), ALU.mult))
            link(dve.tensor_tensor(x, x, self.table("cos"), ALU.mult))
            if n < 2:
                dve.wait_ge(k.sem("cleared"), CLEARED["q"] + 1)
                dve.tensor_tensor(self.qz[0:HS, 2 * n, :], x[0:HS], self.rt[0:HS], ALU.add)
                dve.tensor_tensor(self.qz[HS:P, 2 * n + 1, :], x[HS:P], self.rt[HS:P], ALU.add).then_inc(k.sem("rope_done"), 1)
            else:
                dve.tensor_tensor(x, x, self.rt, ALU.add).then_inc(k.sem("rope_done"), 1)
            dve.wait_ge(k.sem("rope_done"), n + 1)
        for h in range(4):
            for jt in range(NCH):
                n = h * NCH + jt
                dve.wait_ge(k.sem("att_done"), n + 1)
                if n >= 2:
                    dve.wait_ge(k.sem("att_used"), n - 1)
                if jt < CCH:
                    decay = self.table("far%d" % h)[:, P - P * jt:P - P * jt + LAT]
                else:
                    decay = self.table("near%d" % h)[:, 3 * P - P * (jt - CCH):3 * P - P * (jt - CCH) + LAT]
                dve.tensor_tensor(self.att[:, n % 2, :], k.bank[4 + n % 2], decay, ALU.mult).then_inc(k.sem("att_kept"), 1)
                if h and jt == 3:
                    self.ret_centre(dve, h - 1)
            if h:
                self.ret_vector(dve, link, h - 1)
        self.ret_centre(dve, 3)
        self.ret_vector(dve, link, 3)

    def ret_centre(self, dve, h):
        k = self.k
        O = self.O[:, h % 2, :]
        dve.wait_ge(k.sem("mean_summed"), 1 + h + 1)
        dve.wait_ge(k.sem("o_copied"), h + 1)
        dve.scalar_tensor_tensor(O, k.bank[0], -1.0 / P, O, ALU.mult, ALU.add).then_inc(k.sem("centred"), 1)

    def ret_vector(self, dve, link, h):
        k = self.k
        O, rs = self.O[:, h % 2, :], self.ors[:, h % 2, :]
        dve.wait_ge(k.sem("centred"), BT + h + 1)
        dve.wait_ge(k.sem("var_summed"), 1 + h + 1)
        dve.tensor_scalar(rs, k.bank[1], 1.0 / P, 1e-5, ALU.mult, ALU.add).then_inc(k.sem("variance"), 1)
        dve.wait_ge(k.sem("root"), NORM["ret"] + h + 1)
        link(dve.reciprocal(rs, rs))
        link(dve.tensor_tensor(O, O, rs, ALU.mult))
        link(dve.tensor_scalar(O, O, k.col("ret_gn_g", h), k.col("ret_gn_b", h), ALU.mult, ALU.add))
        dve.tensor_tensor(k.At[:, h, :], k.At[:, h, :], O, ALU.mult).then_inc(k.sem("ret_out"), 1)

    def conv_taps(self, eng, link, j):
        k = self.k
        for t in range(CONV_K):
            x, w = self.U[:, j, t:t + LAT], k.col("conv_w", t * BT + j)
            if t == 0:
                link(eng.tensor_scalar(self.acc[:, j, :], x, w, k.col("conv_b", j), ALU.mult, ALU.add))
                continue
            ins = eng.scalar_tensor_tensor(self.acc[:, j, :], x, w, self.acc[:, j, :], ALU.mult, ALU.add)
            if t < CONV_K - 1:
                link(ins)
            else:
                ins.then_inc(k.sem("conv_done"), 1)

    def lru_conv(self, dve, link, u):
        k = self.k
        j, d = u // 2, u % 2
        xc = self.xc[:, d, :]
        dve.wait_ge(k.sem("tile_free"), TILE0["lx0"] + j + 1)
        if j:
            dve.wait_ge(k.sem("gate_mm"), 2 * u - 2)
            dve.wait_ge(k.sem("lru_out"), j)
        for t in range(4):
            x = self.LX[:, j, LP * d + t:LP * d + t + XW]
            w = k.col("lru_conv_w", (4 * d + t) * BT + j)
            if t == 0:
                link(dve.tensor_scalar(xc, x, w, k.col("lru_conv_b", 4 * d + j), ALU.mult, ALU.add))
            elif t < 3:
                link(dve.scalar_tensor_tensor(xc, x, w, xc, ALU.mult, ALU.add))
            else:
                dve.scalar_tensor_tensor(xc, x, w, xc, ALU.mult, ALU.add).then_inc(k.sem("xc_ready"), 1)

    def lru_unit(self, dve, link, u):
        k = self.k
        j, d = u // 2, u % 2
        xc, gr, gi, a = self.xc[:, d, :], self.gr[:, d, :], self.gi[:, d, :], self.a[:, d, :]
        parts = (slice(0, CTX), slice(XL, XW))
        dve.wait_ge(k.sem("lru_a"), 2 * u + 2)
        for s in parts:
            link.step(dve.tensor_tensor(self.tmp[:, s], a[:, s], a[:, s], ALU.mult))
        link.wait()
        for s in parts:
            ins = dve.scalar_tensor_tensor(gr[:, s], self.tmp[:, s], 1.0, gr[:, s], ALU.add, ALU.mult)
        ins.then_inc(k.sem("lru_power"), 1)
        dve.wait_ge(k.sem("xc_ready"), u + 1)
        dve.wait_ge(k.sem("gate_read"), 2 * u + 2)
        for s in parts:
            link.step(dve.tensor_tensor(gi[:, s], gi[:, s], xc[:, s], ALU.mult))
        link.wait()
        dve.wait_ge(k.sem("lru_norm"), u + 1)
        for s in parts:
            link.step(dve.tensor_tensor(gi[:, s], gi[:, s], gr[:, s], ALU.mult))
        link.wait()
        dve.wait_ge(k.sem("gate_mm"), 2 * u + 2)
        if d == 0:
            c, l, last = slice(0, CTX), slice(XL, XW), slice(CTX - 1, CTX)
        else:
            c, l, last = slice(CTX - 1, None, -1), slice(XW - 1, XL - 1, -1), slice(0, 1)
        link(dve.tensor_tensor_scan(xc[:, c], a[:, c], gi[:, c], 0.0, ALU.mult, ALU.add))
        link(dve.tensor_tensor_scan(xc[:, l], a[:, l], gi[:, l], xc[:, last], ALU.mult, ALU.add))
        if d:
            link(dve.tensor_tensor(self.tmp[:, 0:LAT], self.xc[:, 0, XL:XW], self.xc[:, 1, XL:XW], ALU.add))
            dve.wait_ge(k.sem("tile_free"), TILE0["lg0"] + j + 1)
            dve.tensor_tensor(k.Al[:, j, :], k.Al[:, j, :], self.tmp[:, 0:LAT], ALU.mult).then_inc(k.sem("lru_out"), 1)


T_MERGE, T_OUT = TILE0["merge0"], TILE0["out0"]


def load_experts(k, sp, name, experts):
    for u, e in enumerate(experts):
        sp.dma_start(k.we[name][u].unsqueeze(1),
                     k.ins["e_" + name][0].rearrange("e (k p) n -> p e k n", p=P)[:, span(e, 1)])\
            .then_inc(k.sem(name + "_in"), 16)


PROJ = ("rwkv_proj", "conv_proj", "lru_proj", "ret_proj")


class Stage4:
    def __init__(self, k):
        self.k = k
        a = Arena(k.sb, k.words - 10600, k.words)
        self.X1 = k.X1 = a.take(LCH, D)
        self.mod = k.mod = a.take(4, D)
        self.fg = k.fg = a.take(D)
        k.slot_f, k.slot_i, k.wt = a.take(2, LCH), a.take(2, LCH), a.take(2, LCH)
        self.wr = a.take(KT, NE)
        self.br = a.take(NE)
        self.r = [a.take(LCH, NE) for n in range(5)]
        top = k.words - 10600
        b = Arena(k.sb, k.free3, top)
        self.mixed = b.take(KT, LAT)
        self.PRflat = b.take(2 * 4 * BT * P)
        self.gs = b.take(4, LAT)
        self.tmp = b.take(LAT)
        self.n2 = b.take(D)
        self.bada = Arena(k.sb, b.at, top).take(4, D)
        self.sqbuf = b.take(D)
        k.we = {"w3": Arena(k.sb, k.ring_at, k.free), "w1": Arena(k.sb, k.ring_at + RSLOT * SLOTW, k.free),
                "w2": Arena(k.sb, k.free3 + 2 * LCH * D, top)}
        k.we = {name: [r.take(*((DE // P, D) if name == "w2" else (KT, DE))) for u in range(2)] for name, r in k.we.items()}
        c = Arena(k.sb, k.free3, top)
        self.H2 = c.take(LCH, D)
        self.H2T = c.take(KT, LAT)
        c = Arena(k.sb, k.free, top)
        self.ss = k.small[:, 16:20]
        self.rs = k.small[:, 20:24]
        self.oh = [c.take(LCH, NE) for n in range(2)]
        self.g8 = c.take(LCH * NG, 8)
        self.gscore, self.gid = c.take(LCH, NG), c.take(LCH, NG)
        self.v1, self.v2 = c.take(LCH), c.take(LCH)
        self.be = c.take(NBLK - NE, NE)
        self.gscore2 = c.take(LCH, NG)
        self.cntb = c.take(NBLK)
        self.tok_i = c.take(LCH).bitcast(I32)
        self.row = c.take(4, NE)
        self.place_f, self.place_i = c.take(2, LCH), c.take(2, LCH)
        k.block_e = k.small[:, 32:32 + NBLK]
        k.npair = k.small[:, 88:89]

    def sync(self, sp):
        k = self.k
        for m in range(2):
            old = GROUPS[GIDX["merge%d" % (2 * m + 1)] - RSLOT]
            sp.wait_ge(k.sem("tile_done"), TILE0[old[0]] + old[2])
            self.load_gates(sp, m, 0)
        sp.wait_ge(k.sem("ret_out"), 4)
        sp.wait_ge(k.sem("tab_in"), 16)
        for m in range(2):
            self.load_proj(sp, m, 0)
        with sp.Fori(0, 3) as i:
            for u in range(2):
                m = i * 2 + (2 + u)
                sp.wait_ge(k.sem("proj_done"), i * 8 + (4 * u + 4))
                self.load_merge(sp, m, u)
        for n in range(D // GW):
            name, loads, _ = GROUPS[GIDX["out%d" % n]]
            old = GROUPS[GIDX[name] - RSLOT]
            sp.wait_ge(k.sem("tile_done"), TILE0[old[0]] + old[2])
            src, col, w, at = loads[0]
            sp.dma_start(k.slot(name), k.ins[src][0].rearrange("(k p) n -> p k n", p=P)[:, :, col:col + w])\
                .then_inc(k.sem("weights%d" % (GIDX[name] % RSLOT)), 16)
        sp.wait_ge(k.sem("proj_done"), 32)
        load_experts(k, sp, "w1", (0, 1))
        sp.wait_ge(k.sem("tile_done"), NTILES)
        load_experts(k, sp, "w3", (0, 1))
        sp.wait_ge(k.sem("h2_ready"), LCH)
        sp.dma_start(k.h2_dram.rearrange("(t p) d -> p t d", p=P), self.H2).then_inc(k.sem("h2_out"), 16)
        load_experts(k, sp, "w2", (0, 1))

    def load_merge(self, sp, m, par):
        self.load_gates(sp, m, par)
        self.load_proj(sp, m, par)

    def load_gates(self, sp, m, par):
        k = self.k
        static = isinstance(m, int)
        for h in range(2):
            slot = (GIDX["merge0"] + 2 * (par if not static else m) + h) % RSLOT
            for b in range(2):
                base = C_MERGE + (2 * h + b) * D
                cols = slice(base + m * P, base + m * P + P) if static else bass.ds(m * P + base, P)
                sp.dma_start(k.ring[:, slot, :].rearrange("p (k n) -> p k n", k=KT)[:, :, b * P:(b + 1) * P],
                             k.ins["w_in"][0].rearrange("(k p) n -> p k n", p=P)[:, :, cols])\
                    .then_inc(k.sem("weights%d" % slot), 16)

    def load_proj(self, sp, m, par):
        k = self.k
        static = isinstance(m, int)
        cols = slice(m * P, m * P + P) if static else bass.ds(m * P, P)
        par = m if static else par
        for b in range(4):
            sp.dma_start(self.PR4(par, b),
                         k.ins[PROJ[b]][0].rearrange("(k p) n -> p k n", p=P)[:, :, cols])\
                .then_inc(k.sem("proj_in%d" % par), 16)

    def PR4(self, par, b):
        o = (par * 4 + b) * BT * P
        return self.PRflat[:, o:o + BT * P].rearrange("p (k n) -> p k n", k=BT)

    def gpsimd(self, pool):
        k = self.k
        pool.wait_ge(k.sem("ret_out"), 4)
        pool.wait_ge(k.sem("proj_done"), 1)
        pool.dma_start(self.X1, k.ins["x"][0].rearrange("(t p) d -> p t d", p=P)).then_inc(k.sem("x1_in"), 16)
        pool.wait_ge(k.sem("mod_out"), 16 * 2 * NADA)
        pool.dma_start(self.mod, k.mod_dram[:, 2 * D:6 * D].rearrange("a (r n) -> a r n", r=4).to_broadcast([P, 4, D])).then_inc(k.sem("x1_in"), 16)
        pool.dma_start(self.fg, k.ins["final_g"].rearrange("(a n) -> a n", a=1).to_broadcast([P, D])).then_inc(k.sem("x1_in"), 16)
        pool.dma_start(self.n2, k.ins["norm2_g"].to_broadcast([P, D])).then_inc(k.sem("x1_in"), 16)
        pool.dma_start(self.br, k.ins["b_router"].rearrange("(a n) -> a n", a=1).to_broadcast([P, NE])).then_inc(k.sem("x1_in"), 16)
        pool.dma_start(self.wr, k.ins["w_router"].rearrange("(k p) n -> p k n", p=P)).then_inc(k.sem("x1_in"), 16)
        pool.dma_start(self.bada, k.ins["b_ada"][:, 2 * D:6 * D].rearrange("a (r n) -> a r n", r=4).to_broadcast([P, 4, D])).then_inc(k.sem("x1_in"), 16)
        pool.wait_ge(k.sem("x1_in"), 112)
        pool.tensor_tensor(self.mod, self.mod, self.bada, ALU.add).then_inc(k.sem("mod_ready"), 1)
        pool.wait_ge(k.sem("rows_zeroed"), 32)
        for t in range(LCH):
            for q in range(2):
                pool.wait_ge(k.sem("slots_ready"), 2)
                pool.indirect_dma_start(out=k.list_dram,
                                        out_offset=bass.IndirectOffsetOnAxis(ap=self.place_i[:, q, t:t + 1].bitcast(U32), axis=0),
                                        in_=self.tok_i[:, t:t + 1], in_offset=None).then_inc(k.sem("list_out"), 16)

    def tensor(self, pe):
        k = self.k
        A = (k.Ar, k.Ac, k.Al, k.At)
        pe.wait_ge(k.sem("tile_free"), T_MERGE)
        pe.wait_ge(k.sem("variance"), NORM["ret"] + 4)
        pe.wait_ge(k.sem("conv_out"), BT)
        g0 = GIDX["merge0"]
        with pe.Fori(0, 4) as i:
            for u in range(2):
                for b in range(4):
                    g = g0 + 2 * u + b // 2
                    if b % 2 == 0:
                        before = sum(16 * len(GROUPS[x][1]) for x in range(g % RSLOT, g + 1, RSLOT))
                        pe.wait_ge(k.sem("weights%d" % (g % RSLOT)), i * 32 + before)
                    q = 4 * u + b
                    pe.wait_ge(k.sem("tile_free"), i * 8 + (T_MERGE + q - 3))
                    w = k.ring[:, g % RSLOT, :].rearrange("p (k n) -> p k n", k=KT)
                    for kt in range(KT):
                        ins = pe.matmul(k.bank[q % 4], w[:, kt, (b % 2) * P:(b % 2 + 1) * P], k.hT[:, kt, CTX:TOK],
                                        start=(kt == 0), stop=(kt == KT - 1))
                    ins.then_inc(k.sem("tile_done"), 1)
                    if b == 0:
                        pe.wait_ge(k.sem("proj_in%d" % u), i * 64 + 64)
                    pe.wait_ge(k.sem("mix_step"), i * 8 + (q + 1))
                    for kt in range(BT):
                        ins = pe.matmul(k.bank[4 + q % 4], self.PR4(u, b)[:, kt, :], A[b][:, kt, :], start=(kt == 0),
                                        stop=(kt == BT - 1))
                    ins.then_inc(k.sem("proj_done"), 1)
        pe.wait_ge(k.sem("mix_step"), 4 + 32)
        pe.wait_ge(k.sem("tile_free"), T_OUT)
        for n in range(D // GW):
            name = "out%d" % n
            k.await_weights(pe, name)
            for t in range(LCH):
                q = n * LCH + t
                if q >= 4:
                    pe.wait_ge(k.sem("out_read"), q - 3)
                for kt in range(KT):
                    ins = pe.matmul(k.bank[q % 4][:, 0:GW], self.mixed[:, kt, t * P:(t + 1) * P], k.slot(name)[:, kt, :],
                                    start=(kt == 0), stop=(kt == KT - 1))
                ins.then_inc(k.sem("tile_done"), 1)
        for d in range(KT):
            pe.wait_ge(k.sem("h2_ready"), LCH)
            if d >= 2:
                pe.wait_ge(k.sem("h2t_copied"), d - 1)
            for t in range(LCH):
                ins = pe.transpose(k.bank[4 + d % 2][:, t * P:(t + 1) * P], self.H2[:, t, d * P:(d + 1) * P], k.c("ident"))
            ins.then_inc(k.sem("turned"), 1)
        pe.wait_ge(k.sem("h2t_copied"), KT)
        for t in range(LCH):
            for kt in range(KT):
                ins = pe.matmul(k.bank[6][:, t * NE:(t + 1) * NE], self.H2T[:, kt, t * P:(t + 1) * P], self.wr[:, kt, :],
                                start=(kt == 0), stop=(kt == KT - 1))
        ins.then_inc(k.sem("logits"), 1)
        pe.wait_ge(k.sem("chosen"), 1)
        M = self.r[2]
        for t in range(LCH):
            o = k.bank[7][:, t * NE:(t + 1) * NE]
            for s in range(t):
                pe.matmul(o, k.c("ones"), M[:, s, :], start=(s == 0), stop=False)
            pe.matmul(o, k.c("keep0")[:, 0:P], M[:, t, :], start=(t == 0), stop=True)
        for t in range(LCH):
            ins = pe.matmul(k.bank[7][:, LCH * NE:(LCH + 1) * NE], k.c("ones"), M[:, t, :], start=(t == 0), stop=(t == LCH - 1))
        ins.then_inc(k.sem("ranked"), 1)

    def scalar(self, act):
        k = self.k
        act.wait_ge(k.sem("ret_out"), 4)
        with act.Fori(0, 4) as i:
            for u in range(2):
                for b in range(4):
                    q = 4 * u + b
                    act.wait_ge(k.sem("tile_done"), i * 8 + (T_MERGE + q + 1))
                    act.wait_ge(k.sem("mix_step"), i * 8 + (q + 1))
                    act.activation(self.gs[:, q % 4, :], k.bank[q % 4], ACT.Sigmoid,
                                   bias=self.bmerge(i, u, b)).then_inc(k.sem("tile_free"), 1)
        act.wait_ge(k.sem("x1_ready"), 16)
        for t in range(LCH):
            if t:
                act.wait_ge(k.sem("squared"), SQUARED["norm2"] + t)
            act.activation(self.sqbuf, self.X1[:, t, :], ACT.Square, accum_out=self.ss[:, t:t + 1]).then_inc(k.sem("squared"), 1)
        act.wait_ge(k.sem("variance"), NORM["norm2"] + 1)
        act.activation(self.rs, self.ss, ACT.Sqrt).then_inc(k.sem("root"), 1)
        for d in range(KT):
            act.wait_ge(k.sem("turned"), TURNED["h2"] + d + 1)
            act.activation(self.H2T[:, d, :], k.bank[4 + d % 2], ACT.Copy).then_inc(k.sem("h2t_copied"), 1)
        act.wait_ge(k.sem("logits"), 1)
        act.activation(self.r[0], k.bank[6][:, 0:LCH * NE].rearrange("p (a b) -> p a b", a=LCH), ACT.Sigmoid).then_inc(k.sem("affinity"), 1)

    def bmerge(self, i, u, b):
        r = ROWAT["b_merge"] + b * KT + u
        return self.k.cols[:, r // P, bass.ds(i * 2 + r % P, 1)]

    def vector(self, dve, link):
        k = self.k
        dve.memset(k.small[:, 90:91], 0.0).then_inc(k.sem("mix_step"), 4)
        with dve.Fori(0, 4) as i:
            for u in range(2):
                for b in range(4):
                    q = 4 * u + b
                    dve.wait_ge(k.sem("tile_free"), i * 8 + (T_MERGE + q + 1))
                    dve.wait_ge(k.sem("proj_done"), i * 8 + (q + 1))
                    gs, pr = self.gs[:, q % 4, :], k.bank[4 + q % 4]
                    m = self.mixed[:, bass.ds(i * 2 + u, 1), :].rearrange("p a b -> p (a b)")
                    if b == 0:
                        dve.tensor_tensor(m, gs, pr, ALU.mult).then_inc(k.sem("mix_step"), 1)
                    else:
                        dve.wait_ge(k.sem("mix_step"), i * 8 + (q + 4))
                        dve.tensor_tensor(self.tmp, gs, pr, ALU.mult).then_inc(k.sem("mix_part"), 1)
                        dve.wait_ge(k.sem("mix_part"), i * 6 + (3 * u + b))
                        dve.tensor_tensor(m, m, self.tmp, ALU.add).then_inc(k.sem("mix_step"), 1)
        dve.wait_ge(k.sem("mix_step"), 36)
        dve.wait_ge(k.sem("x1_in"), 112)
        dve.wait_ge(k.sem("mod_ready"), 1)
        for n in range(D // GW):
            for t in range(LCH):
                q = n * LCH + t
                dve.wait_ge(k.sem("tile_done"), T_OUT + q + 1)
                cols = slice(n * GW, (n + 1) * GW)
                dve.tensor_tensor(self.tmp[:, (q % 2) * GW:(q % 2 + 1) * GW], k.bank[q % 4][:, 0:GW], self.mod[:, 0, cols],
                                  ALU.mult).then_inc(k.sem("out_read"), 1)
                dve.wait_ge(k.sem("out_read"), q + 1)
                dve.tensor_tensor(self.X1[:, t, cols], self.X1[:, t, cols], self.tmp[:, (q % 2) * GW:(q % 2 + 1) * GW],
                                  ALU.add).then_inc(k.sem("x1_ready"), 1)
        link(dve.scalar_tensor_tensor(self.mod[:, 2, :], self.mod[:, 2, :], 1.0, self.n2, ALU.add, ALU.mult))
        dve.wait_ge(k.sem("squared"), SQUARED["norm2"] + LCH)
        dve.tensor_scalar(self.ss, self.ss, 1.0 / D, 1e-6, ALU.mult, ALU.add).then_inc(k.sem("variance"), 1)
        dve.wait_ge(k.sem("root"), NORM["norm2"] + 1)
        link(dve.reciprocal(self.rs, self.rs))
        for t in range(LCH):
            link(dve.scalar_tensor_tensor(self.H2[:, t, :], self.X1[:, t, :], self.rs[:, t:t + 1], self.mod[:, 2, :], ALU.mult, ALU.mult))
            dve.tensor_tensor(self.H2[:, t, :], self.H2[:, t, :], self.mod[:, 1, :], ALU.add).then_inc(k.sem("h2_ready"), 1)
        self.route(dve, link)

    def first_of(self, link, dve, vals, best, ids, dst, scratch, n):
        sh = [P, LCH, n]
        big = 1000.0
        link(dve.tensor_tensor(scratch, vals, bc(best.unsqueeze(2), sh), ALU.is_equal))
        link(dve.tensor_scalar(scratch, scratch, -big, big, ALU.mult, ALU.add))
        link(dve.tensor_tensor(scratch, scratch, bc(ids.unsqueeze(1), sh), ALU.add))
        link(dve.tensor_reduce(self.v2, scratch, AX, ALU.min))
        link(dve.tensor_tensor(dst, bc(ids.unsqueeze(1), sh), bc(self.v2.unsqueeze(2), sh), ALU.is_equal))

    def route(self, dve, link):
        k = self.k
        aff, sel, M, s1, s2 = self.r
        ids = k.c("iota32")
        dve.wait_ge(k.sem("affinity"), 1)
        link(dve.tensor_tensor(sel, aff, bc(self.br.unsqueeze(1), [P, LCH, NE]), ALU.add))
        flat = lambda x: x.rearrange("p a b -> p (a b)")
        for n in range(LCH * NG):
            link.step(dve.max(self.g8[:, n, :], flat(sel)[:, n * EPG:(n + 1) * EPG]))
        link.wait()
        link(dve.tensor_tensor(flat(self.gscore), self.g8[:, :, 0], self.g8[:, :, 1], ALU.add))
        link(dve.tensor_reduce(self.v1, self.gscore, AX, ALU.max))
        self.first_of(link, dve, self.gscore, self.v1, ids[:, 0:NG], self.gid, self.gscore2, NG)
        s14 = s1.rearrange("p a (g e) -> p (a g) e", g=NG)
        link(dve.tensor_copy(s14, bc(flat(self.gid).unsqueeze(2), [P, LCH * NG, EPG])))
        link(dve.tensor_tensor(sel, sel, s1, ALU.mult))
        link(dve.tensor_scalar(s1, s1, 1e30, -1e30, ALU.mult, ALU.add))
        link(dve.tensor_tensor(sel, sel, s1, ALU.add))
        for q in range(2):
            link(dve.tensor_reduce(self.v1, sel, AX, ALU.max))
            self.first_of(link, dve, sel, self.v1, ids, self.oh[q], s1, NE)
            link(dve.tensor_tensor(s1, aff, self.oh[q], ALU.mult))
            link(dve.tensor_reduce(k.wt[:, q, :], s1, AX, ALU.add))
            if q == 0:
                link(dve.scalar_tensor_tensor(sel, self.oh[0], -3e30, sel, ALU.mult, ALU.add))
        dve.tensor_tensor(M, self.oh[0], self.oh[1], ALU.add).then_inc(k.sem("chosen"), 1)
        link(dve.tensor_tensor(self.v1, k.wt[:, 0, :], k.wt[:, 1, :], ALU.add))
        link(dve.reciprocal(self.v1, self.v1))
        link(dve.tensor_tensor(k.wt, k.wt, bc(self.v1.unsqueeze(1), [P, 2, LCH]), ALU.mult))
        dve.wait_ge(k.sem("ranked"), 1)
        cnt, over, end, jump = [self.row[:, n, :] for n in range(4)]
        link(dve.tensor_copy(cnt, k.bank[7][:, LCH * NE:(LCH + 1) * NE]))
        link(dve.tensor_scalar(over, cnt, SL + 0.5, None, ALU.is_gt))
        for n in range(2, LAT // SL):
            link(dve.scalar_tensor_tensor(over, cnt, n * SL + 0.5, over, ALU.is_gt, ALU.add))
        link(dve.tensor_tensor_scan(end, k.c("ones")[:, 0:NE], over, 0.0, ALU.mult, ALU.add))
        link(dve.tensor_tensor(jump, end, over, ALU.subtract))
        link(dve.tensor_tensor(jump, jump, ids, ALU.subtract))
        link(dve.tensor_scalar(jump, jump, NE - 1.0, float(SL), ALU.add, ALU.mult))
        rank = k.bank[7][:, 0:LCH * NE].rearrange("p (a b) -> p a b", a=LCH)
        wide = lambda x: bc(x.unsqueeze(1), [P, LCH, NE])
        link(dve.tensor_scalar(s1, rank, SL - 0.5, None, ALU.is_gt))
        link(dve.tensor_tensor(s1, s1, wide(jump), ALU.mult))
        link(dve.tensor_tensor(s1, s1, rank, ALU.add))
        link(dve.tensor_scalar(self.row[:, 0, :], ids, float(SL), None, ALU.mult))
        link(dve.tensor_tensor(s2, s1, wide(self.row[:, 0, :]), ALU.add))
        for q in range(2):
            link(dve.tensor_tensor(s1, s2, self.oh[q], ALU.mult))
            link(dve.tensor_reduce(k.slot_f[:, q, :], s1, AX, ALU.add))
        link(dve.tensor_copy(k.slot_i.bitcast(I32), k.slot_f))
        link(dve.tensor_scalar(self.place_i.bitcast(I32), k.slot_i.bitcast(I32), 7, None, ALU.logical_shift_right))
        link(dve.tensor_copy(self.place_f, self.place_i.bitcast(I32)))
        link(dve.tensor_scalar(self.place_f, self.place_f, 1.0 - P * NPAIR, None, ALU.mult))
        link(dve.scalar_tensor_tensor(self.place_f, k.slot_f, float(NPAIR), self.place_f, ALU.mult, ALU.add))
        link(dve.tensor_copy(self.tok_i, k.c("tokid")))
        dve.tensor_copy(self.place_i.bitcast(I32), self.place_f).then_inc(k.sem("slots_ready"), 1)
        no = NBLK - NE
        sh = [P, no, NE]
        link(dve.tensor_copy(self.cntb[:, 0:NE], ids))
        link(dve.tensor_tensor(self.be, bc(end.unsqueeze(1), sh), bc(k.c("iotab")[:, 0:no].unsqueeze(2), sh), ALU.is_le))
        link(dve.tensor_reduce(self.cntb[:, NE:NBLK], self.be, AX, ALU.add))
        link(dve.tensor_scalar(self.cntb, self.cntb, float(NE - 1), None, ALU.min))
        link(dve.tensor_copy(k.block_e.bitcast(I32), self.cntb))
        link(dve.tensor_scalar(self.cntb[:, 0:no // 2], k.c("iotab")[:, 0:no:2], end[:, NE - 1:NE], None, ALU.is_lt))
        link(dve.tensor_reduce(self.v1[:, 0:1], self.cntb[:, 0:no // 2], AX, ALU.add))
        link(dve.tensor_scalar(self.v1[:, 0:1], self.v1[:, 0:1], float(NE // 2), None, ALU.add))
        dve.tensor_copy(k.npair.bitcast(I32), self.v1[:, 0:1]).then_inc(k.sem("slots_ready"), 1)


class Stage5:
    def __init__(self, k):
        self.k = k
        c = Arena(k.sb, k.free3, k.free3 + 8192)
        self.xg, self.xT = c.take(D), c.take(KT, P)
        self.sil, self.g, self.gT = c.take(DE), c.take(DE), c.take(DE // P, P)
        self.y = c.take(D)
        self.idx = c.take(NPAIR).bitcast(I32)
        self.idu, self.spare_i = c.take(1).bitcast(I32), c.take(1).bitcast(I32)
        a = Arena(k.sb, k.ring_at, k.free)
        self.yg = a.take(LCH * 2, D)
        self.sq = a.take(D)
        self.ss, self.rs = k.small[:, 96:100], k.small[:, 100:104]

    def steps(self, eng):
        k = self.k
        eng.wait_ge(k.sem("slots_ready"), 2)
        eng.wait_ge(k.sem("primed"), 1)
        return eng.value_load(k.npair[0:1, :].bitcast(I32), min_val=NE // 2, max_val=NPAIR)

    def sync(self, sp):
        k = self.k
        n = self.steps(sp)
        with sp.Fori(1, n) as i:
            e = [sp.value_load(k.block_e[0:1, bass.ds(i * 2 + u, 1)].bitcast(I32), min_val=0, max_val=NE - 1)
                 for u in range(2)]
            sp.wait_ge(k.sem("h1_done"), i)
            load_experts(k, sp, "w1", e)
            sp.wait_ge(k.sem("h3_done"), i)
            load_experts(k, sp, "w3", e)
            sp.wait_ge(k.sem("ye_done"), i)
            load_experts(k, sp, "w2", e)
        for t in range(LCH):
            sp.wait_ge(k.sem("out_ready"), t + 1)
            sp.dma_start(k.out[0, t * P:(t + 1) * P, :], k.X1[:, t, :]).then_inc(k.sem("stored"), 16)
        sp.wait_ge(k.sem("stored"), 16 * LCH)

    def gpsimd(self, pool):
        k = self.k
        pool.wait_ge(k.sem("list_out"), 16 * 2 * LCH)
        pool.wait_ge(k.sem("h2_out"), 16)
        pool.wait_ge(k.sem("logits"), 1)
        pool.dma_start(self.idx, k.list_dram.rearrange("(p b) a -> p (b a)", p=P)).then_inc(k.sem("idx_in"), 16)
        pool.wait_ge(k.sem("idx_in"), 16)
        n = self.steps(pool)
        with pool.Fori(0, n) as i:
            pool.wait_ge(k.sem("x_lifted"), i + 1)
            pool.tensor_copy(self.idu, self.idx[:, bass.ds(i, 1)]).then_inc(k.sem("idx_picked"), 1)
            pool.wait_ge(k.sem("idx_picked"), i + 1)
            pool.tensor_copy(self.spare_i, self.idx[:, bass.ds(i * -1 + (NPAIR - 1), 1)])
            pool.indirect_dma_start(out=self.xg, out_offset=None, in_=k.h2_dram,
                                    in_offset=bass.IndirectOffsetOnAxis(ap=self.idu.bitcast(U32), axis=0))\
                .then_inc(k.sem("xg_in"), 16)
        pool.wait_ge(k.sem("rows_stored"), 1)
        for t in range(LCH):
            for q in range(2):
                pool.indirect_dma_start(out=self.yg[:, 2 * t + q, :], out_offset=None, in_=k.y_dram,
                                        in_offset=bass.IndirectOffsetOnAxis(ap=k.slot_i[:, q, t:t + 1].bitcast(U32), axis=0))\
                    .then_inc(k.sem("yg_in%d" % t), 16)

    def tensor(self, pe):
        k = self.k
        bank, ident = k.bank, k.c("ident")
        half = lambda u: slice(SL * u, SL * u + SL)
        n = self.steps(pe)
        with pe.Fori(0, n) as i:
            pe.wait_ge(k.sem("xg_in"), i * 16 + 16)
            for kt in range(KT):
                ins = pe.transpose(bank[kt // 4][:, (kt % 4) * P:(kt % 4 + 1) * P], self.xg[:, kt * P:(kt + 1) * P], ident)
            ins.then_inc(k.sem("x_lifted"), 1)
            pe.wait_ge(k.sem("xt_copied"), i + 1)
            for w, name in enumerate(("w1", "w3")):
                pe.wait_ge(k.sem(name + "_in"), i * 32 + 32)
                for kt in range(KT):
                    for u in range(2):
                        ins = pe.matmul(bank[2 + w][half(u), :], self.xT[:, kt, half(u)], k.we[name][u][:, kt, :],
                                        start=(kt == 0), stop=(kt == KT - 1))
                ins.then_inc(k.sem("h1_done") if w == 0 else k.sem("h3_done"), 1)
            pe.wait_ge(k.sem("g_ready"), i + 1)
            for kt in range(DE // P):
                ins = pe.transpose(bank[4][:, kt * P:(kt + 1) * P], self.g[:, kt * P:(kt + 1) * P], ident)
            ins.then_inc(k.sem("gt_done"), 1)
            pe.wait_ge(k.sem("gt_copied"), i + 1)
            pe.wait_ge(k.sem("w2_in"), i * 32 + 32)
            pe.wait_ge(k.sem("ye_act"), i + 1)
            pe.wait_ge(k.sem("ye_dve"), i + 1)
            for h in range(2):
                for kt in range(DE // P):
                    for u in range(2):
                        ins = pe.matmul(bank[5 + h][half(u), :], self.gT[:, kt, half(u)],
                                        k.we["w2"][u][:, kt, h * 512:(h + 1) * 512], start=(kt == 0),
                                        stop=(kt == DE // P - 1))
            ins.then_inc(k.sem("ye_done"), 1)

    def scalar(self, act):
        k = self.k
        act.wait_ge(k.sem("rows_zeroed"), 32)
        n = self.steps(act)
        with act.Fori(0, n) as i:
            act.wait_ge(k.sem("h1_done"), i + 1)
            act.activation(self.sil, k.bank[2], ACT.Silu).then_inc(k.sem("silu_made"), 1)
            act.wait_ge(k.sem("ye_done"), i + 1)
            act.wait_ge(k.sem("y_out"), i * 16 + 16)
            act.activation(self.y[:, 0:512], k.bank[5], ACT.Copy).then_inc(k.sem("ye_act"), 1)
            act.wait_ge(k.sem("ye_act"), i + 2)
            act.wait_ge(k.sem("ye_dve"), i + 2)
            act.dma_start(k.y_dram[bass.ds(i * P, P), :], self.y).then_inc(k.sem("y_out"), 16)
        act.wait_ge(k.sem("y_out"), n * 16 + 16)
        act.activation(self.sil[:, 0:1], k.c("ones")[:, 0:1], ACT.Copy).then_inc(k.sem("rows_stored"), 1)
        for t in range(LCH):
            act.wait_ge(k.sem("x2_ready"), t + 1)
            if t:
                act.wait_ge(k.sem("squared"), SQUARED["final"] + t)
            act.activation(self.sq, k.X1[:, t, :], ACT.Square, accum_out=self.ss[:, t:t + 1]).then_inc(k.sem("squared"), 1)
        act.wait_ge(k.sem("variance"), NORM["final"] + 1)
        act.activation(self.rs, self.ss, ACT.Sqrt).then_inc(k.sem("root"), 1)

    def vector(self, dve, link):
        k = self.k
        for n, (name, count) in enumerate((("x_lifted", 1), ("ye_act", 1), ("ye_dve", 1), ("y_out", 16))):
            dve.memset(k.small[:, 110 + n:111 + n], 0.0).then_inc(k.sem(name), count)
        dve.wait_ge(k.sem("y_out"), 16)
        dve.memset(k.small[:, 92:93], 0.0).then_inc(k.sem("primed"), 1)
        n = self.steps(dve)
        with dve.Fori(0, n) as i:
            dve.wait_ge(k.sem("x_lifted"), i + 2)
            for half in range(2):
                ins = dve.tensor_copy(self.xT[:, 4 * half:4 * half + 4, :], k.bank[half].rearrange("p (a b) -> p a b", a=4))
            ins.then_inc(k.sem("xt_copied"), 1)
            dve.wait_ge(k.sem("silu_made"), i + 1)
            dve.wait_ge(k.sem("h3_done"), i + 1)
            dve.tensor_tensor(self.g, self.sil, k.bank[3], ALU.mult).then_inc(k.sem("g_ready"), 1)
            dve.wait_ge(k.sem("gt_done"), i + 1)
            dve.tensor_copy(self.gT, k.bank[4].rearrange("p (a b) -> p a b", a=4)).then_inc(k.sem("gt_copied"), 1)
            dve.wait_ge(k.sem("ye_done"), i + 1)
            dve.wait_ge(k.sem("y_out"), i * 16 + 16)
            dve.tensor_copy(self.y[:, 512:1024], k.bank[6]).then_inc(k.sem("ye_dve"), 1)
        for t in range(LCH):
            dve.wait_ge(k.sem("yg_in%d" % t), 32)
            y0, y1 = self.yg[:, 2 * t, :], self.yg[:, 2 * t + 1, :]
            link(dve.tensor_scalar(y0, y0, k.wt[:, 0, t:t + 1], None, ALU.mult))
            link(dve.scalar_tensor_tensor(y0, y1, k.wt[:, 1, t:t + 1], y0, ALU.mult, ALU.add))
            link(dve.tensor_tensor(y0, y0, k.mod[:, 3, :], ALU.mult))
            dve.tensor_tensor(k.X1[:, t, :], k.X1[:, t, :], y0, ALU.add).then_inc(k.sem("x2_ready"), 1)
        dve.wait_ge(k.sem("squared"), SQUARED["final"] + LCH)
        dve.tensor_scalar(self.ss, self.ss, 1.0 / D, 1e-6, ALU.mult, ALU.add).then_inc(k.sem("variance"), 1)
        dve.wait_ge(k.sem("root"), NORM["final"] + 1)
        link(dve.reciprocal(self.rs, self.rs))
        for t in range(LCH):
            dve.scalar_tensor_tensor(k.X1[:, t, :], k.X1[:, t, :], self.rs[:, t:t + 1], k.fg, ALU.mult, ALU.mult)\
                .then_inc(k.sem("out_ready"), 1)


WLAST = GIDX["merge0"]


def STAGES(k):
    return [Stage1(k), Stage2(k), Stage3(k), Stage4(k), Stage5(k)]


SEMS = [
    "tile_done",
    "weights0",
    "weights1",
    "weights2",
    "weights3",
    "cleared",
    "const_in",
    "rows_in",
    "x_in",
    "exps",
    "rows_zeroed",
    "turned",
    "silu_ready",
    "tile_free",
    "modc_done",
    "x_scaled",
    "h_ready",
    "modc_ready",
    "cols_ready",
    "squared",
    "variance",
    "root",
    "state_new0",
    "state_new1",
    "lora_w_in",
    "unit_used",
    "v_chunk0",
    "v_chunk1",
    "gn_in",
    "kk_squared",
    "kk_summed",
    "mixed",
    "rk_ready",
    "bonus_done",
    "lora_ready",
    "unit_half",
    "unit_mm",
    "v_copied",
    "bonus_copied",
    "gates_done",
    "z_ready",
    "mod_out",
    "chunk_ops",
    "rho_made",
    "y_added0",
    "y_added1",
    "scores0",
    "scores1",
    "scores_kept0",
    "scores_kept1",
    "tok_done",
    "tok_copied",
    "rhs_done",
    "lx_kept0",
    "lx_kept1",
    "x_done0",
    "x_done1",
    "x_copied0",
    "x_copied1",
    "rhs_copied",
    "lx_done0",
    "lx_done1",
    "u_done",
    "u_copied",
    "y_done",
    "state_grown",
    "rwkv_out",
    "ends",
    "xt_part",
    "state_sum",
    "wb_in",
    "pool_step",
    "gated",
    "conv_share",
    "conv_done",
    "lru_out",
    "tab_in",
    "gate_read",
    "mean_summed",
    "var_summed",
    "rotated",
    "rope_done",
    "centred",
    "att_kept",
    "att_done",
    "o_copied",
    "att_used",
    "xc_ready",
    "gate_mm",
    "lam_abs",
    "lam_exp",
    "conv_normed",
    "conv_out",
    "ret_out",
    "lam_ready",
    "lru_a",
    "lru_power",
    "lru_norm",
    "proj_done",
    "h2_ready",
    "h2_out",
    "proj_in0",
    "proj_in1",
    "x1_in",
    "mod_ready",
    "slots_ready",
    "list_out",
    "mix_step",
    "out_read",
    "h2t_copied",
    "logits",
    "chosen",
    "ranked",
    "x1_ready",
    "affinity",
    "mix_part",
    "primed",
    "h1_done",
    "h3_done",
    "ye_done",
    "out_ready",
    "stored",
    "idx_in",
    "x_lifted",
    "idx_picked",
    "xg_in",
    "rows_stored",
    "yg_in0",
    "yg_in1",
    "xt_copied",
    "g_ready",
    "gt_done",
    "gt_copied",
    "w2_in",
    "ye_act",
    "ye_dve",
    "silu_made",
    "y_out",
    "x2_ready",
    "vector_step",
    "yg_in2",
    "yg_in3",
    "w1_in",
    "w3_in",
]

NAMES = ["x", "c", "ctx", "c_ctx", "w_ada", "b_ada", "norm1_g", "norm2_g", "w_in", "b_merge", "rwkv_mu_prev",
         "rwkv_mu_next", "rwkv_w0", "rwkv_w2", "rwkv_a0", "rwkv_a2", "rwkv_g2", "rwkv_k_k", "rwkv_k_a", "rwkv_r_k",
         "rwkv_gn_g", "rwkv_gn_b", "rwkv_proj", "conv_w", "conv_b", "conv_ln_g", "conv_ln_b", "conv_proj",
         "lru_conv_w", "lru_conv_b", "lru_wr", "lru_br", "lru_wi", "lru_bi", "lru_lambda", "lru_proj", "ret_gn_g",
         "ret_gn_b", "ret_proj", "w_out", "w_router", "b_router", "e_w1", "e_w3", "e_w2", "final_g"]


def backbone_block(nc, ins, out):
    with ExitStack() as ctx:
        k = Kernel(nc, ctx, ins, out)
        stages = STAGES(k)
        for s in SEMS:
            k.sem(s)
        block = ctx.enter_context(nc.Block())

        @block.sync
        def _(sp):
            for s in stages:
                if hasattr(s, "sync"):
                    s.sync(sp)

        @block.gpsimd
        def _(pool):
            for s in stages:
                if hasattr(s, "gpsimd"):
                    s.gpsimd(pool)

        @block.tensor
        def _(pe):
            for s in stages:
                if hasattr(s, "tensor"):
                    s.tensor(pe)

        @block.scalar
        def _(act):
            for s in stages:
                if hasattr(s, "scalar"):
                    s.scalar(act)

        @block.vector
        def _(dve):
            link = Chain(dve, k.sem("vector_step"))
            for s in stages:
                if hasattr(s, "vector"):
                    s.vector(dve, link)


def kernel(**inputs):
    import concourse.bacc as bacc
    from concourse.bass_utils import run_bass_kernel_spmd

    nc = bacc.Bacc("TRN2", target_bir_lowering=False, num_devices=1)
    arrays, ins = {}, {}
    for name in NAMES:
        arrays["in_" + name] = np.ascontiguousarray(inputs[name])
    arrays["in_const_tables"] = CONST
    arrays["in_ret_tables"] = RCONST
    for name, a in arrays.items():
        ins[name[3:]] = nc.dram_tensor(name, a.shape, mybir.dt.from_np(a.dtype), kind="ExternalInput").ap()
    out = nc.dram_tensor("out", (1, LAT, D), F32, kind="ExternalOutput").ap()
    backbone_block(nc, ins, out)
    result = run_bass_kernel_spmd(nc, [arrays], core_ids=[0])
    return result.results[0]["out"]
```
